# Optimizing a Trainium2 kernel written in Bass

```python
import math
import jax, jax.numpy as jnp
from jax import lax
import numpy as np

D_MODEL = 1024
BATCH = 1
SEQ = 512
DEPTH = 1

MIX_WIDTH = D_MODEL
MOBA_WIDTH = MIX_WIDTH // 2
MOBA_HEAD_DIM = 64
MOBA_HEADS = MOBA_WIDTH // MOBA_HEAD_DIM
MOBA_BLOCK = 256
MOBA_TOPK = 3
QUERY_CHUNK = 128
GDN_WIDTH = MIX_WIDTH - MOBA_WIDTH
GDN_HEAD_DIM = 128
GDN_HEADS = GDN_WIDTH // GDN_HEAD_DIM
GDN_CONV = 4
GDN_CHUNK = 64
IN_SPLITS = (MOBA_WIDTH,) * 4 + (GDN_WIDTH,) * 4 + (GDN_HEADS, GDN_HEADS)
IN_WIDTH = sum(IN_SPLITS)
RMS_EPS = 1e-6
NEG_INF = -1e30


def rms_norm(x, w):
    xf = x.astype(jnp.float32)
    y = xf * lax.rsqrt(jnp.mean(xf * xf, axis=-1, keepdims=True) + RMS_EPS)
    return (y * w.astype(jnp.float32)).astype(x.dtype)

def alibi_slopes(n_heads):
    start = 2.0 ** (-8.0 / n_heads)
    return jnp.asarray(start ** np.arange(1, n_heads + 1), dtype=jnp.float32)

def moba_attention(q, k, v):
    B, T, H, dh = q.shape
    nb = -(-T // MOBA_BLOCK)
    pad = nb * MOBA_BLOCK - T
    n_qc = T // QUERY_CHUNK
    k_sel = min(MOBA_TOPK, nb - 1)
    scale = dh ** -0.5
    slopes = alibi_slopes(H)
    qh = q.transpose(0, 2, 1, 3)
    pad_cfg = ((0, 0), (0, pad), (0, 0), (0, 0))
    kb = jnp.pad(k, pad_cfg).reshape(B, nb, MOBA_BLOCK, H, dh).transpose(0, 3, 1, 2, 4)
    vb = jnp.pad(v, pad_cfg).reshape(B, nb, MOBA_BLOCK, H, dh).transpose(0, 3, 1, 2, 4)
    kbar = jnp.mean(kb.astype(jnp.float32), axis=3)
    blk_off = jnp.arange(MOBA_BLOCK)
    head_idx = jnp.arange(H)[:, None, None]

    def chunk_attend(step):
        bi = step // n_qc
        q0 = (step % n_qc) * QUERY_CHUNK
        own = q0 // MOBA_BLOCK
        qc = lax.dynamic_slice_in_dim(qh[bi], q0, QUERY_CHUNK, axis=1)
        kb_b, vb_b = kb[bi], vb[bi]
        t_pos = q0 + jnp.arange(QUERY_CHUNK)
        k_own = lax.dynamic_index_in_dim(kb_b, own, axis=1, keepdims=False)
        v_own = lax.dynamic_index_in_dim(vb_b, own, axis=1, keepdims=False)
        dist_own = (t_pos[:, None] - (own * MOBA_BLOCK + blk_off)[None, :]).astype(jnp.float32)
        logit_own = (jnp.einsum('hqd,hkd->hqk', qc, k_own).astype(jnp.float32) * scale
                     - slopes[:, None, None] * dist_own)
        logit_own = jnp.where(dist_own >= 0, logit_own, NEG_INF)
        if k_sel == 0:
            p = jax.nn.softmax(logit_own, axis=-1).astype(v.dtype)
            return jnp.einsum('hqk,hkd->hqd', p, v_own)
        gate = jnp.einsum('hqd,hnd->hqn', qc.astype(jnp.float32), kbar[bi])
        gate = jnp.where(jnp.arange(nb) < own, gate, NEG_INF)
        _, sel = lax.top_k(gate, k_sel)
        k_g = kb_b[head_idx, sel]
        v_g = vb_b[head_idx, sel]
        s_sel = sel[..., None] * MOBA_BLOCK + blk_off
        dist_sel = (t_pos[None, :, None, None] - s_sel).astype(jnp.float32)
        logit_sel = (jnp.einsum('hqd,hqnkd->hqnk', qc, k_g).astype(jnp.float32) * scale
                     - slopes[:, None, None, None] * dist_sel)
        valid = (jnp.arange(k_sel) < own)[None, None, :, None]
        logit_sel = jnp.where(valid, logit_sel, NEG_INF).reshape(H, QUERY_CHUNK, k_sel * MOBA_BLOCK)
        p = jax.nn.softmax(jnp.concatenate([logit_sel, logit_own], axis=-1), axis=-1).astype(v.dtype)
        p_sel = p[..., :k_sel * MOBA_BLOCK].reshape(H, QUERY_CHUNK, k_sel, MOBA_BLOCK)
        p_own = p[..., k_sel * MOBA_BLOCK:]
        return (jnp.einsum('hqnk,hqnkd->hqd', p_sel, v_g)
                + jnp.einsum('hqk,hkd->hqd', p_own, v_own))

    out = lax.map(chunk_attend, jnp.arange(B * n_qc))
    out = out.reshape(B, n_qc, H, QUERY_CHUNK, dh).transpose(0, 1, 3, 2, 4)
    return out.reshape(B, T, H * dh)

def causal_depthwise_conv(x, w):
    K, C = w.shape
    return lax.conv_general_dilated(
        x, w[:, None, :].astype(x.dtype), window_strides=(1,), padding=((K - 1, 0),),
        dimension_numbers=('NWC', 'WIO', 'NWC'), feature_group_count=C)

def l2_normalize(x):
    return x * lax.rsqrt(jnp.sum(x * x, axis=-1, keepdims=True) + RMS_EPS)

def gated_delta_rule(q, k, v, g, beta):
    B, T, H, dk = q.shape
    dv = v.shape[-1]
    C = GDN_CHUNK
    nc = T // C
    q = l2_normalize(q) * (dk ** -0.5)
    k = l2_normalize(k)

    def chunks(t):
        return t.reshape(B, nc, C, H, -1).transpose(1, 0, 3, 2, 4)

    q, k, v = chunks(q), chunks(k), chunks(v)
    beta = beta.reshape(B, nc, C, H).transpose(1, 0, 3, 2)
    gc = jnp.cumsum(g.reshape(B, nc, C, H).transpose(1, 0, 3, 2), axis=-1)
    causal = jnp.tril(jnp.ones((C, C), dtype=bool))
    strict = jnp.tril(jnp.ones((C, C), dtype=bool), -1)
    decay = jnp.exp(jnp.where(causal, gc[..., :, None] - gc[..., None, :], -jnp.inf))
    k_beta = k * beta[..., None]
    a = jnp.where(strict, jnp.einsum('nbhid,nbhjd->nbhij', k_beta, k) * decay, 0.0)
    eye = jnp.eye(C, dtype=jnp.float32)
    t_inv = lax.linalg.triangular_solve(a + eye, jnp.broadcast_to(eye, a.shape),
                                        left_side=True, lower=True, unit_diagonal=True)
    u = t_inv @ (v * beta[..., None])
    w = t_inv @ (k_beta * jnp.exp(gc)[..., None])
    intra = jnp.where(causal, jnp.einsum('nbhid,nbhjd->nbhij', q, k) * decay, 0.0)
    q_dec = q * jnp.exp(gc)[..., None]
    k_dec = k * jnp.exp(gc[..., -1:] - gc)[..., None]
    g_last = jnp.exp(gc[..., -1])

    def step(S, xs):
        q_i, k_i, u_i, w_i, intra_i, gl = xs
        v_new = u_i - w_i @ S
        o = q_i @ S + intra_i @ v_new
        S = S * gl[..., None, None] + jnp.einsum('bhcd,bhce->bhde', k_i, v_new)
        return S, o

    S0 = jnp.zeros((B, H, dk, dv), dtype=jnp.float32)
    _, o = lax.scan(step, S0, (q_dec, k_dec, u, w, intra, g_last))
    return o.transpose(1, 0, 3, 2, 4).reshape(B, T, H, dv)

def hybrid_layer(x, norm_pre_w, w_in, conv_w, a_log, dt_bias, gdn_norm_w, w_out, norm_post_w):
    B, T, _ = x.shape
    h = rms_norm(x, norm_pre_w)
    proj = h @ w_in.astype(x.dtype)
    split_at = list(np.cumsum(IN_SPLITS)[:-1])
    a_q, a_k, a_v, a_z, d_q, d_k, d_v, d_z, d_b, d_a = jnp.split(proj, split_at, axis=-1)

    heads_a = lambda t: t.reshape(B, T, MOBA_HEADS, MOBA_HEAD_DIM)
    moba_out = moba_attention(heads_a(a_q), heads_a(a_k), heads_a(a_v)) * jax.nn.silu(a_z)

    qkv = jax.nn.silu(causal_depthwise_conv(jnp.concatenate([d_q, d_k, d_v], axis=-1), conv_w))
    g_q, g_k, g_v = jnp.split(qkv, 3, axis=-1)
    heads_b = lambda t: t.reshape(B, T, GDN_HEADS, GDN_HEAD_DIM).astype(jnp.float32)
    beta = jax.nn.sigmoid(d_b.astype(jnp.float32))
    g = -jnp.exp(a_log.astype(jnp.float32)) * jax.nn.softplus(
        d_a.astype(jnp.float32) + dt_bias.astype(jnp.float32))
    o = gated_delta_rule(heads_b(g_q), heads_b(g_k), heads_b(g_v), g, beta)
    gdn_out = rms_norm(o, gdn_norm_w).reshape(B, T, GDN_WIDTH).astype(x.dtype) * jax.nn.silu(d_z)

    mixed = jnp.concatenate([moba_out, gdn_out], axis=-1) @ w_out.astype(x.dtype)
    return x + rms_norm(mixed, norm_post_w)

def first_inputs(seed: int = 0) -> dict:
    key = jax.random.key(seed)
    ks = jax.random.split(key, 9)
    f32 = jnp.float32
    x = jax.random.normal(ks[0], (BATCH, SEQ, D_MODEL), f32)
    norm_pre_w = 1.0 + 0.05 * jax.random.normal(ks[1], (DEPTH, D_MODEL), f32)
    w_in = jax.random.normal(ks[2], (DEPTH, D_MODEL, IN_WIDTH), f32) * D_MODEL ** -0.5
    conv_w = jax.random.normal(ks[3], (DEPTH, GDN_CONV, 3 * GDN_WIDTH), f32) * GDN_CONV ** -0.5
    a_log = jnp.log(jax.random.uniform(ks[4], (DEPTH, GDN_HEADS), f32, minval=1.0, maxval=16.0))
    dt = jnp.exp(jax.random.uniform(ks[5], (DEPTH, GDN_HEADS), f32,
                                    minval=math.log(1e-3), maxval=math.log(1e-1)))
    dt_bias = dt + jnp.log(-jnp.expm1(-dt))
    gdn_norm_w = 1.0 + 0.05 * jax.random.normal(ks[6], (DEPTH, GDN_HEAD_DIM), f32)
    w_out = jax.random.normal(ks[7], (DEPTH, MIX_WIDTH, D_MODEL), f32) * MIX_WIDTH ** -0.5
    norm_post_w = 1.0 + 0.05 * jax.random.normal(ks[8], (DEPTH, D_MODEL), f32)
    return {"x": x, "norm_pre_w": norm_pre_w, "w_in": w_in, "conv_w": conv_w,
            "a_log": a_log, "dt_bias": dt_bias, "gdn_norm_w": gdn_norm_w,
            "w_out": w_out, "norm_post_w": norm_post_w}

def first_block(x, norm_pre_w, w_in, conv_w, a_log, dt_bias, gdn_norm_w, w_out, norm_post_w):
    for layer in range(DEPTH):
        x = hybrid_layer(x, norm_pre_w[layer], w_in[layer], conv_w[layer], a_log[layer],
                         dt_bias[layer], gdn_norm_w[layer], w_out[layer], norm_post_w[layer])
    return x


A_HEADS = 4
A_DK = 128
A_DV = 128
A_CHUNK = 64
A_QK_W = A_HEADS * A_DK
A_V_W = A_HEADS * A_DV
B_HEADS = 8
B_KV_GROUPS = 2
B_HPG = B_HEADS // B_KV_GROUPS
B_HEAD_DIM = 64
B_Q_W = B_HEADS * B_HEAD_DIM
B_KV_W = B_KV_GROUPS * B_HEAD_DIM
CMP_LEN = 32
CMP_STRIDE = 16
CMP_HIDDEN = 256
SEL_LEN = 64
SEL_TOPK = 16
WINDOW = 512
Q_BLOCK = 128
FORCE_SCORE = 1e4
NEG = -1e30
ROPE_THETA = 500000.0
ROT_DIM = B_HEAD_DIM // 4
D_FF = 4 * D_MODEL
EPS = 1e-6

IN_SIZES = [A_QK_W, A_QK_W, A_V_W, A_V_W,
            B_Q_W, 6 * B_KV_W, 3 * B_HEADS,
            2 * D_MODEL]
N_IN = int(sum(IN_SIZES))
SPLIT_POINTS = [int(v) for v in np.cumsum(IN_SIZES)[:-1]]


def rmsnorm(x, g):
    xf = x.astype(jnp.float32)
    y = xf * lax.rsqrt(jnp.mean(xf * xf, axis=-1, keepdims=True) + EPS) * g.astype(jnp.float32)
    return y.astype(x.dtype)

def masked_softmax(s, mask):
    s = jnp.where(mask, s.astype(jnp.float32), NEG)
    m = jnp.max(s, axis=-1, keepdims=True)
    p = jnp.where(mask, jnp.exp(s - m), 0.0)
    return p / jnp.maximum(jnp.sum(p, axis=-1, keepdims=True), 1e-30)

def partial_rope(t, positions):
    half = ROT_DIM // 2
    inv_freq = ROPE_THETA ** (-jnp.arange(0, ROT_DIM, 2, dtype=jnp.float32) / ROT_DIM)
    ang = positions.astype(jnp.float32)[..., None] * inv_freq
    cos = jnp.cos(ang)[:, :, None, :].astype(t.dtype)
    sin = jnp.sin(ang)[:, :, None, :].astype(t.dtype)
    t1, t2, rest = t[..., :half], t[..., half:ROT_DIM], t[..., ROT_DIM:]
    return jnp.concatenate([t1 * cos - t2 * sin, t2 * cos + t1 * sin, rest], axis=-1)

def hgrn2_mixer(q, f_pre, v, g, lb, norm_g):
    bsz, s, _ = q.shape
    n = s // A_CHUNK
    f32 = jnp.float32
    f = lb + (1.0 - lb) * jax.nn.sigmoid(f_pre.astype(f32))
    k = 1.0 - f

    def heads(t, d):
        return t.astype(f32).reshape(bsz, n, A_CHUNK, A_HEADS, d).transpose(0, 3, 1, 2, 4)

    qh, kh, vh, lfh = heads(q, A_DK), heads(k, A_DK), heads(v, A_DV), heads(jnp.log(f), A_DK)
    b = jnp.cumsum(lfh, axis=3)
    b_last = b[..., -1:, :]
    q_dec = qh * jnp.exp(b)
    k_dec = kh * jnp.exp(-b)
    causal = jnp.tril(jnp.ones((A_CHUNK, A_CHUNK), dtype=bool))
    attn = jnp.where(causal, jnp.einsum('bhnsk,bhntk->bhnst', q_dec, k_dec), 0.0)
    o_intra = jnp.einsum('bhnst,bhntv->bhnsv', attn, vh)
    kv = jnp.einsum('bhntk,bhntv->nbhkv', kh * jnp.exp(b_last - b), vh)
    decay = jnp.exp(b_last[..., 0, :]).transpose(2, 0, 1, 3)

    def step(state, inp):
        dec, kv_n = inp
        return dec[..., None] * state + kv_n, state

    s0 = jnp.zeros((bsz, A_HEADS, A_DK, A_DV), f32)
    _, s_start = lax.scan(step, s0, (decay, kv))
    o_inter = jnp.einsum('bhnsk,nbhkv->bhnsv', q_dec, s_start)
    o = (o_intra + o_inter).transpose(0, 2, 3, 1, 4).reshape(bsz, s, A_HEADS, A_DV)
    o = rmsnorm(o, norm_g) * jax.nn.silu(g.astype(f32).reshape(bsz, s, A_HEADS, A_DV))
    return o.reshape(bsz, s, A_V_W).astype(q.dtype)

def nsa_mixer(q, kc_tok, vc_tok, ks, vs, kw, vw, gate_pre, positions,
              pe_k, pe_v, w1_k, w2_k, w1_v, w2_v):
    bsz, s, _ = q.shape
    G, HPG, HD = B_KV_GROUPS, B_HPG, B_HEAD_DIM

    def kvh(t):
        return t.reshape(bsz, s, G, HD)

    q = partial_rope(q.reshape(bsz, s, B_HEADS, HD), positions)
    kc_tok = partial_rope(kvh(kc_tok), positions)
    vc_tok = kvh(vc_tok)
    ks = partial_rope(kvh(ks), positions)
    kw = partial_rope(kvh(kw), positions)

    n_cmp = (s - CMP_LEN) // CMP_STRIDE + 1
    blk_idx = np.arange(n_cmp)[:, None] * CMP_STRIDE + np.arange(CMP_LEN)[None, :]

    def compress(tok, pe, w1, w2):
        blocks = tok[:, blk_idx] + pe[None, None, :, None, :]
        flat = blocks.transpose(0, 1, 3, 2, 4).reshape(bsz, n_cmp, G, CMP_LEN * HD)
        return (jax.nn.gelu(flat @ w1) @ w2).transpose(0, 2, 1, 3)

    kc = compress(kc_tok, pe_k, w1_k, w2_k)
    vc = compress(vc_tok, pe_v, w1_v, w2_v)
    cmp_end = jnp.asarray(blk_idx[:, -1], jnp.int32)

    n_slc = s // SEL_LEN
    cs = np.arange(n_cmp)[:, None] * CMP_STRIDE
    ss = np.arange(n_slc)[None, :] * SEL_LEN
    overlap = np.clip(np.minimum(cs + CMP_LEN, ss + SEL_LEN) - np.maximum(cs, ss), 0, None) / CMP_LEN
    overlap = jnp.asarray(overlap, jnp.float32)
    n_top = min(SEL_TOPK, n_slc)

    qg = q.reshape(bsz, s, G, HPG, HD).transpose(0, 2, 3, 1, 4) * (HD ** -0.5)
    ks_g = ks.transpose(0, 2, 1, 3)
    vs_g = kvh(vs).transpose(0, 2, 1, 3)
    pad = ((0, 0), (0, 0), (WINDOW, 0), (0, 0))
    kw_pad = jnp.pad(kw.transpose(0, 2, 1, 3), pad)
    vw_pad = jnp.pad(kvh(vw).transpose(0, 2, 1, 3), pad)
    gates = jax.nn.sigmoid(gate_pre.reshape(bsz, s, G, HPG, 3)).transpose(0, 2, 3, 1, 4)
    bi = jnp.arange(bsz)[:, None, None]
    gi = jnp.arange(G)[None, :, None]
    sel_off = jnp.arange(SEL_LEN)
    jblk = jnp.arange(n_slc)

    def block_fn(blk):
        q0 = blk * Q_BLOCK
        qb = lax.dynamic_slice_in_dim(qg, q0, Q_BLOCK, axis=3)
        gb = lax.dynamic_slice_in_dim(gates, q0, Q_BLOCK, axis=3)
        t = q0 + jnp.arange(Q_BLOCK)
        p_c = masked_softmax(jnp.einsum('bghqd,bgcd->bghqc', qb, kc),
                             cmp_end[None, :] <= t[:, None])
        o_c = jnp.einsum('bghqc,bgcd->bghqd', p_c.astype(vc.dtype), vc)
        imp = jnp.einsum('bghqc,cj->bgqj', p_c, overlap)
        cur = t // SEL_LEN
        causal_blk = jblk[None, :] <= cur[:, None]
        forced = (jblk[None, :] == 0) | (jblk[None, :] == cur[:, None]) | (jblk[None, :] == cur[:, None] - 1)
        imp = jnp.where(forced & causal_blk, FORCE_SCORE, imp)
        imp = jnp.where(causal_blk, imp, NEG)
        top_val, top_idx = lax.top_k(imp, n_top)
        tok_idx = top_idx[..., None] * SEL_LEN + sel_off
        tok_ok = (top_val > 0.5 * NEG)[..., None] & (tok_idx <= t[None, None, :, None, None])
        flat_idx = tok_idx.reshape(bsz, G, Q_BLOCK * n_top * SEL_LEN)
        k_sel = ks_g[bi, gi, flat_idx].reshape(bsz, G, Q_BLOCK, n_top * SEL_LEN, HD)
        v_sel = vs_g[bi, gi, flat_idx].reshape(bsz, G, Q_BLOCK, n_top * SEL_LEN, HD)
        p_s = masked_softmax(jnp.einsum('bghqd,bgqkd->bghqk', qb, k_sel),
                             tok_ok.reshape(bsz, G, 1, Q_BLOCK, n_top * SEL_LEN))
        o_s = jnp.einsum('bghqk,bgqkd->bghqd', p_s.astype(v_sel.dtype), v_sel)
        k_w = lax.dynamic_slice_in_dim(kw_pad, q0, WINDOW + Q_BLOCK, axis=2)
        v_w = lax.dynamic_slice_in_dim(vw_pad, q0, WINDOW + Q_BLOCK, axis=2)
        s_pos = q0 - WINDOW + jnp.arange(WINDOW + Q_BLOCK)
        m_w = (s_pos[None, :] <= t[:, None]) & (s_pos[None, :] > t[:, None] - WINDOW) & (s_pos[None, :] >= 0)
        p_w = masked_softmax(jnp.einsum('bghqd,bgkd->bghqk', qb, k_w), m_w)
        o_w = jnp.einsum('bghqk,bgkd->bghqd', p_w.astype(v_w.dtype), v_w)
        return gb[..., 0:1] * o_c + gb[..., 1:2] * o_s + gb[..., 2:3] * o_w

    out = lax.map(block_fn, jnp.arange(s // Q_BLOCK))
    return out.transpose(1, 0, 4, 2, 3, 5).reshape(bsz, s, B_Q_W)

def second_inputs(seed: int = 0) -> dict:
    key = jax.random.key(seed)
    ks = jax.random.split(key, 20)
    f32 = jnp.float32

    def nrm(k, shape, scale):
        return jax.random.normal(k, shape, f32) * scale

    L = DEPTH
    x = jax.random.normal(ks[0], (BATCH, SEQ, D_MODEL), f32)
    offsets = jax.random.randint(ks[1], (BATCH, 1), 0, 2048, dtype=jnp.int32)
    positions = (offsets + jnp.arange(SEQ, dtype=jnp.int32)[None, :]).astype(jnp.int32)
    return {
        "x": x,
        "positions": positions,
        "norm1_g": 1.0 + nrm(ks[2], (L, D_MODEL), 0.02),
        "w_in": nrm(ks[3], (L, D_MODEL, N_IN), D_MODEL ** -0.5),
        "lb_param": nrm(ks[4], (L + 1, A_QK_W), 0.1),
        "hgrn_norm_g": 1.0 + nrm(ks[5], (L, A_DV), 0.02),
        "cmp_pe_k": nrm(ks[6], (L, CMP_LEN, B_HEAD_DIM), 0.1),
        "cmp_pe_v": nrm(ks[7], (L, CMP_LEN, B_HEAD_DIM), 0.1),
        "cmp_w1_k": nrm(ks[8], (L, CMP_LEN * B_HEAD_DIM, CMP_HIDDEN), (CMP_LEN * B_HEAD_DIM) ** -0.5),
        "cmp_w2_k": nrm(ks[9], (L, CMP_HIDDEN, B_HEAD_DIM), CMP_HIDDEN ** -0.5),
        "cmp_w1_v": nrm(ks[10], (L, CMP_LEN * B_HEAD_DIM, CMP_HIDDEN), (CMP_LEN * B_HEAD_DIM) ** -0.5),
        "cmp_w2_v": nrm(ks[11], (L, CMP_HIDDEN, B_HEAD_DIM), CMP_HIDDEN ** -0.5),
        "w_br_a": nrm(ks[12], (L, A_V_W, D_MODEL), A_V_W ** -0.5),
        "w_br_b": nrm(ks[13], (L, B_Q_W, D_MODEL), B_Q_W ** -0.5),
        "w_out": nrm(ks[14], (L, D_MODEL, D_MODEL), D_MODEL ** -0.5),
        "norm2_g": 1.0 + nrm(ks[15], (L, D_MODEL), 0.02),
        "w_ff1": nrm(ks[16], (L, D_MODEL, D_FF), D_MODEL ** -0.5),
        "w_ff2": nrm(ks[17], (L, D_FF, D_MODEL), D_FF ** -0.5),
        "final_g": 1.0 + nrm(ks[18], (D_MODEL,), 0.02),
    }

def second_block(x, positions, norm1_g, w_in, lb_param, hgrn_norm_g, cmp_pe_k, cmp_pe_v,
              cmp_w1_k, cmp_w2_k, cmp_w1_v, cmp_w2_v, w_br_a, w_br_b, w_out,
              norm2_g, w_ff1, w_ff2, final_g):
    lb_all = jnp.cumsum(jax.nn.softmax(lb_param.astype(jnp.float32), axis=0), axis=0)
    h = x
    for l in range(DEPTH):
        xn = rmsnorm(h, norm1_g[l])
        proj = xn @ w_in[l]
        a_q, a_f, a_i, a_g, b_q, b_kv, b_gate, m_gate = jnp.split(proj, SPLIT_POINTS, axis=-1)
        kc, vc, ks_, vs_, kw_, vw_ = jnp.split(b_kv, 6, axis=-1)
        y_a = hgrn2_mixer(a_q, a_f, a_i, a_g, lb_all[l], hgrn_norm_g[l])
        y_b = nsa_mixer(b_q, kc, vc, ks_, vs_, kw_, vw_, b_gate, positions,
                        cmp_pe_k[l], cmp_pe_v[l], cmp_w1_k[l], cmp_w2_k[l], cmp_w1_v[l], cmp_w2_v[l])
        g_a, g_b = jnp.split(jax.nn.sigmoid(m_gate), 2, axis=-1)
        merged = g_a * (y_a @ w_br_a[l]) + g_b * (y_b @ w_br_b[l])
        h = h + merged @ w_out[l]
        hn = rmsnorm(h, norm2_g[l])
        h = h + jnp.square(jax.nn.relu(hn @ w_ff1[l])) @ w_ff2[l]
    return rmsnorm(h, final_g)


def setup_inputs(seed=0):
    out = dict(first_inputs(seed))
    for name, value in second_inputs(seed + 1).items():
        if name != "x":
            out[name + "_2"] = value
    return out


def reference(
    x, norm_pre_w, w_in, conv_w, a_log, dt_bias, gdn_norm_w, w_out, norm_post_w, positions_2,
    norm1_g_2, w_in_2, lb_param_2, hgrn_norm_g_2, cmp_pe_k_2, cmp_pe_v_2, cmp_w1_k_2,
    cmp_w2_k_2, cmp_w1_v_2, cmp_w2_v_2, w_br_a_2, w_br_b_2, w_out_2, norm2_g_2, w_ff1_2,
    w_ff2_2, final_g_2,
):
    x = first_block(
        x, norm_pre_w, w_in, conv_w, a_log, dt_bias, gdn_norm_w, w_out, norm_post_w,
    )
    return second_block(
        x, positions_2, norm1_g_2, w_in_2, lb_param_2, hgrn_norm_g_2, cmp_pe_k_2, cmp_pe_v_2,
        cmp_w1_k_2, cmp_w2_k_2, cmp_w1_v_2, cmp_w2_v_2, w_br_a_2, w_br_b_2, w_out_2, norm2_g_2,
        w_ff1_2, w_ff2_2, final_g_2,
    )


_drawn_inputs = setup_inputs


def setup_inputs(seed=0):
    import zlib

    import numpy as np

    out = dict(_drawn_inputs(seed))
    spreads = {}
    factors = {'norm1_g_2': 5.4,
     'lb_param_2': 2.814,
     'hgrn_norm_g_2': 8.0,
     'cmp_pe_k_2': 8.0,
     'cmp_pe_v_2': 38.128,
     'cmp_w1_k_2': 2.87,
     'cmp_w2_k_2': 2.875,
     'norm2_g_2': 14.184,
     'final_g_2': 7.791}
    for name, (base, spread) in spreads.items():
        noise = np.random.default_rng([zlib.crc32(name.encode()), seed]).standard_normal(out[name].shape)
        drawn = base * np.exp(spread * noise) if base else spread * noise
        out[name] = __import__('jax').numpy.asarray(drawn.astype(out[name].dtype))
    for name, factor in factors.items():
        out[name] = (out[name] * factor).astype(out[name].dtype)
    return out
```

```python
from contextlib import ExitStack

import numpy as np
import concourse.bass as bass
from concourse import mybir

F32 = mybir.dt.float32
F32R = mybir.dt.float32r
I32 = mybir.dt.int32
ALU = mybir.AluOpType
ACT = mybir.ActivationFunctionType
AX = mybir.AxisListType.X

P = 128
T = 512
NT = T // P
D = 1024
KD = D // P
NC = 512
EPS = 1e-6
BIG = 1e30

H1, DH = 8, 64
HG, DG = 4, 128
N_CMP, CMP_C = 31, 32
N_GATE = 24
FF = 4096
LEVELS = (1, 2, 4, 8, 16, 32, 64)
HG_CHUNK = 64

UPS = 4
B1_SLABS, A1_SLABS, O1_SLABS = 5, 3, 2
B2_SLABS, A2_SLABS = 4, 3
M_UNITS = 24
O2_SLABS = 2
FF_HALVES, FF1_SLABS, FF2_UNITS = 2, 4, 8
U_B1 = 0
U_A1 = U_B1 + UPS * B1_SLABS
U_O1 = U_A1 + UPS * A1_SLABS
U_B2 = U_O1 + UPS * O1_SLABS
U_A2 = U_B2 + UPS * B2_SLABS
U_M = U_A2 + UPS * A2_SLABS
U_O2 = U_M + M_UNITS
U_FF = U_O2 + UPS * O2_SLABS
SLAB_B1 = 1
SLAB_A1 = SLAB_B1 + B1_SLABS
SLAB_O1 = SLAB_A1 + A1_SLABS
SLAB_B2 = SLAB_O1 + O1_SLABS
SLAB_A2 = SLAB_B2 + B2_SLABS
SLAB_M = SLAB_A2 + A2_SLABS
SLAB_O2 = SLAB_M + 8
SLAB_FF = SLAB_O2 + O2_SLABS
SLABS_HALF = FF1_SLABS + 2
U_HALF = UPS * FF1_SLABS + 2 * FF2_UNITS
N_UNITS = U_FF + FF_HALVES * U_HALF
RING = 4

def _columns(parts):
    at, out = 0, {}
    for name, n in parts:
        out[name] = (at, at + n)
        at += n
    return out, at

CONST_COLS, N_CONST = _columns(
    [("ident", P), ("tri", P), ("ones", P), ("future", P), ("rope_swap", P)]
    + [(f"level{s}", P) for s in LEVELS]
    + [("alibi", T), ("causal", T), ("restart", T), ("cmp_hide", NT * CMP_C), ("cmp_keep", NT * CMP_C),
       ("inv_freq", 1)])
PARAM_COLS, N_PARAM = _columns(
    [("norm_pre", KD), ("norm1", KD), ("norm2", KD), ("conv", 48), ("gdn_norm", 1), ("hgrn_norm", 1),
     ("lb", 8), ("a_log", HG), ("dt_bias", HG)])


def constant_table():
    c = np.zeros((P, N_CONST), np.float32)

    def put(name, value):
        a, b = CONST_COLS[name]
        c[:, a:b] = value

    row, col = np.arange(P)[:, None], np.arange(P)[None, :]
    put("ident", row == col)
    put("tri", row <= col)
    put("ones", 1.0)
    put("future", np.where(col >= row, 0.0, -BIG))
    swap = np.zeros((P, P), np.float32)
    for g in (0, DH):
        for d in range(8):
            swap[g + d + 8, g + d] = -1.0
            swap[g + d, g + d + 8] = 1.0
    put("rope_swap", swap)
    for s in LEVELS:
        put(f"level{s}", (col // (2 * s) == row // (2 * s)) & (col // s % 2 == 1) & (row // s % 2 == 0))
    dist = row + (T - P) - np.arange(T)[None, :]
    put("alibi", np.where(dist >= 0, 0.5 * dist, BIG))
    put("causal", np.where(dist >= 0, 0.0, BIG))
    put("restart", np.arange(T)[None, :] % HG_CHUNK != 0)
    t = np.arange(NT)[None, :, None] * P + np.arange(P)[:, None, None]
    cc = np.arange(CMP_C)[None, None, :]
    seen = (16 * cc + 31 <= t) & (cc < N_CMP)
    put("cmp_hide", np.where(seen, 0.0, BIG).reshape(P, -1))
    put("cmp_keep", seen.reshape(P, -1))
    inv = (500000.0 ** (-np.arange(0, 16, 2) / 16)).astype(np.float32)
    d = np.arange(P) % DH
    put("inv_freq", np.where(d < 16, inv[d % 8], 0.0)[:, None])
    return c


def slab_units(w):
    k, n = w.shape
    w = np.pad(w, ((0, 0), (0, NC - n))) if n < NC else w
    return w.reshape(k // (2 * P), 2, P, NC).transpose(0, 2, 1, 3).reshape(-1, P, 2 * NC)


def by_partition(v):
    return v.reshape(-1, P).T


def two_blocks(nc, units, consts, params, x, w_ba, norm_post, final_g, positions, pe_kv, w1_kv, w2_kv, out):
    ctx = ExitStack()
    base = (nc.sbuf_base + 31) // 32 * 32
    KB = 1024

    def sb(name, shape, dtype, at):
        return nc.alloc_sbuf_tensor_at(name, shape, dtype, offset=base + int(at * KB))

    with ctx:
        def sem(name):
            return ctx.enter_context(nc.semaphore(name))

        C = sb("consts_sb", [P, N_CONST], F32, 0)
        PAR = sb("params_sb", [P, N_PARAM], F32, 14)
        SMALL = sb("small", [P, 384], F32, 14.5)
        raw = sb("w_raw", [P, RING, 2, NC], F32, 16)
        w_hi = sb("w_hi", [P, RING, 2, NC], F32R, 32)
        w_lo = sb("w_lo", [P, RING, 2, NC], F32R, 48)
        X = sb("residual", [P, NT, D], F32, 64)
        ht_hi = sb("ht_hi", [P, KD, T], F32R, 80)
        ht_lo = sb("ht_lo", [P, KD, T], F32R, 96)

        def const(name):
            a, b = CONST_COLS[name]
            return C[:, a:b]

        def param(name, k=0, n=1):
            a = PARAM_COLS[name][0] + k
            return PAR[:, a:a + n]

        ident = const("ident")

        PB = sb("feature_major", [P, 4 * B1_SLABS, T], F32, 112)
        PA = sb("token_major", [P, A1_SLABS, NT, NC], F32, 152)
        V1, Z1, DZ = PA[:, 0], PA[:, 1], PA[:, 2]
        xn = sb("normalized", [P, NT, D], F32, 176)
        wba = sb("w_ba_sb", [P, KD, 8], F32, 192)
        wba_hi = sb("w_ba_hi", [P, KD, P], F32R, 192.5)
        wba_lo = sb("w_ba_lo", [P, KD, P], F32R, 196.5)
        ba_row = sb("ba_row", [P, T], F32, 200.5)
        conv4 = sb("conv_sum", [P, 4, T], F32, 176)
        kz = sb("k_padded", [P, 4, 2, T], F32, 176)
        q_st = sb("q_staged", [P, T], F32, 192)
        pr = sb("probs", [P, 2, T], F32, 194)
        pt = sb("probs_t", [P, 2, T], F32, 198)
        alibi = sb("alibi_bias", [P, 2, T], F32, 203)
        KM = sb("gdn_k_tok", [P, HG, NT, DG], F32, 80)
        VM = sb("gdn_v_tok", [P, HG, NT, DG], F32, 88)
        GO = sb("gdn_out", [P, NT, HG, DG], F32, 96)
        sq = sb("gdn_squares", [P, NT, DG], F32, 104)
        d_names = ["KT", "TG", "IB", "EG", "DEC", "AT", "INT", "QD", "KBG", "KDEC", "VB", "U", "TI", "XS",
                   "WN", "VN", "S", "MA", "OS"]
        G = {n: sb(f"gdn_{n}", [P, HG, DG], F32, (176 + 2 * i) if i < 15 else (106 + 2 * (i - 15)) if i < 18
                   else 104) for i, n in enumerate(d_names[:18])}
        G["OS"] = G["TG"]
        mixed = sb("mixed", [P, NT, D], F32, 112)
        post_w = sb("norm_post_sb", [P, D], F32, 128)

        acc = [nc.alloc_psum_tensor(f"acc{b}", [P, NC], F32) for b in range(4)]
        aux = [nc.alloc_psum_tensor(f"aux{b}", [P, NC], F32) for b in range(4)]

        consts_in = sem("consts_in")
        x_in = sem("x_in")
        wait_passed = sem("wait_passed")
        small_in = sem("small_in")
        raw_in = [sem(f"raw_in{j}") for j in range(RING)]
        hi_split = sem("hi_split")
        w_split = sem("w_split")
        unit_used = sem("unit_used")
        acc_ready = [sem(f"acc_ready{b}") for b in range(3)]
        acc_out = [sem(f"acc_out{b}") for b in range(4)]
        dve = sem("dve_step")
        flipped = sem("flipped")
        flip_hi = sem("flip_hi")
        flip_lo = sem("flip_lo")
        stored = sem("stored")

        class Steps:

            def __init__(self, eng, semaphore):
                self.eng, self.sem, self.at, self.made = eng, semaphore, 0, 0

            def __call__(self, instruction):
                self.at = self.at + 1
                self.made += 1
                instruction.then_inc(self.sem, 1)
                self.eng.wait_ge(self.sem, self.at)

            def loop(self, count, per):
                start = self.at
                with self.eng.Fori(0, count) as i:
                    self.at = i * per + start
                    before = self.made
                    yield i
                    assert self.made - before == per, (self.made - before, per)
                self.at = start + count * per

        def alone(eng):
            eng.sem_inc(wait_passed, 1)

        def split_product(pe, bank, first_operand, second_operand, start, stop):
            (ah, al), (bh, bl) = first_operand, second_operand
            nc.tensor.matmul(bank, ah, bh, start=start, stop=False)
            nc.tensor.matmul(bank, ah, bl, start=False, stop=False)
            return nc.tensor.matmul(bank, al, bh, start=False, stop=stop)

        def weight_unit(pe, unit, slot, k0, hi, lo, slab, first, last, tokens_out):
            pe.wait_ge(w_split, unit + 1)
            for b in range(4):
                if first:
                    pe.wait_ge(acc_out[b], slab)
                for kk in range(2):
                    k = k0 + kk
                    cols = slice(b * P, (b + 1) * P)
                    w = (w_hi[:, slot, kk, cols], w_lo[:, slot, kk, cols])
                    if tokens_out:
                        w = (w_hi[:, slot, kk], w_lo[:, slot, kk])
                        a = (hi[:, k, cols], lo[:, k, cols])
                        done = split_product(pe, acc[b][:], a, w, first and kk == 0, last and kk == 1)
                    else:
                        a = (hi[:, k], lo[:, k])
                        done = split_product(pe, acc[b][:], w, a, first and kk == 0, last and kk == 1)
                if last and b < 3:
                    done.then_inc(acc_ready[b], 1)
            done.then_inc(unit_used, 1)

        def wait_bank(eng, b, slab, last_unit):
            if b < 3:
                eng.wait_ge(acc_ready[b], slab + 1)
            else:
                eng.wait_ge(unit_used, last_unit + 1)

        def flip_on_tensor(pe, source, chunks, count):
            for k in range(chunks):
                n = count + k
                if n >= 4:
                    pe.wait_ge(flip_lo, n - 3)
                    pe.wait_ge(flip_hi, n - 3)
                for t in range(NT):
                    done = nc.tensor.transpose(acc[k % 4][:, t * P:(t + 1) * P], source(t, k), ident)
                done.then_inc(flipped, 1)

        def flip_hi_part(act, hi, chunks, count, weight):
            for k in range(chunks):
                act.wait_ge(flipped, count + k + 1)
                nc.scalar.activation(hi[:, k], acc[k % 4][:], ACT.Copy, scale=weight(k)).then_inc(flip_hi, 1)

        def flip_lo_part(eng, hi, lo, chunks, count, weight):
            for k in range(chunks):
                eng.wait_ge(flip_hi, count + k + 1)
                nc.vector.scalar_tensor_tensor(out=lo[:, k], in0=acc[k % 4][:], scalar=weight(k),
                                               in1=hi[:, k].bitcast(F32), op0=ALU.mult,
                                               op1=ALU.subtract).then_inc(flip_lo, 1)

        FLIP1, FLIP_MIXED = 0, KD
        FLIP2 = FLIP_MIXED + KD
        FLIP_A, FLIP_B = FLIP2 + KD, FLIP2 + KD + 4
        FLIP3 = FLIP_B + 4

        def rsqrt(step, v, y, t):
            step(nc.vector.tensor_scalar(y.bitcast(I32), v.bitcast(I32), -0.5, float(0x5f3759df),
                                         ALU.mult, ALU.add))
            for _ in range(4):
                step(nc.vector.scalar_tensor_tensor(out=t, in0=y, scalar=-0.5, in1=y,
                                                    op0=ALU.mult, op1=ALU.mult))
                step(nc.vector.tensor_tensor(t, t, v, ALU.mult))
                step(nc.vector.scalar_tensor_tensor(out=y, in0=t, scalar=1.5, in1=y,
                                                    op0=ALU.add, op1=ALU.mult))
        RSQRT_STEPS = 13

        def small(a, n):
            return SMALL[:, a:a + n]
        ss, rstd, tmp4 = small(0, 4), small(4, 4), small(8, 4)
        beta, gcol, ba, rkq, ssq = small(16, 16), small(32, 16), small(48, 32), small(80, 32), small(112, 32)
        eg, egl, dl, c_bk = small(144, 16), small(160, 16), small(176, 16), small(192, 16)
        c_kbg, c_kdec, c_rq, rk_c = small(208, 16), small(224, 16), small(240, 16), small(256, 16)
        go_ss, go_rs, t32, nega = small(272, 16), small(288, 16), small(304, 32), small(336, 4)
        nmin, psum_, rs8 = small(340, 8), small(348, 8), small(356, 8)

        q_staged = sem("q_staged")
        scored = sem("scored")
        biased = sem("biased")
        probs = sem("probs_ready")
        probs_flipped = sem("probs_flipped")
        probs_out = sem("probs_out")
        weighed = sem("weighed")
        values_used = sem("values_used")
        STEPS = H1 * NT
        MOBA, SELECTED, WINDOW = 0, STEPS, 2 * STEPS

        def attention_on_tensor(pe, first, q, keys, values):
            with pe.Fori(0, 4) as c:
                def scores(n):
                    h, t = divmod(n, NT)
                    if n >= 2:
                        pe.wait_ge(biased, c * 8 + (first + n - 1))
                    w = (t + 1) * P
                    nc.tensor.matmul(aux[n % 2][:, :w], q[:, t * P:(t + 1) * P], keys(c, h)[:, :w],
                                     start=True, stop=True).then_inc(scored, 1)

                def flip(n):
                    t = n % NT
                    pe.wait_ge(probs, c * 8 + (first + n + 1))
                    if n >= 1:
                        pe.wait_ge(probs_out, c * 8 + (first + n))
                    for j in range(t + 1):
                        done = nc.tensor.transpose(aux[2][:, j * P:(j + 1) * P],
                                                   pr[:, n % 2, j * P:(j + 1) * P], ident)
                    done.then_inc(probs_flipped, 1)

                def weigh(n):
                    h, t = divmod(n, NT)
                    pe.wait_ge(probs_out, c * 8 + (first + n + 1))
                    pe.wait_ge(values_used, c * 8 + (first + n + 1))
                    for j in range(t + 1):
                        done = nc.tensor.matmul(aux[3][:, :DH], pt[:, n % 2, j * P:(j + 1) * P],
                                                values(c, h, j), start=j == 0, stop=j == t)
                    done.then_inc(weighed, 1)

                pe.wait_ge(q_staged, c + (first // 8 + 1))
                scores(0)
                for n in range(8):
                    if n < 7:
                        scores(n + 1)
                    flip(n)
                    if n:
                        weigh(n - 1)
                weigh(7)

        def attention_on_scalar(act, first):
            with act.Fori(0, 4) as c:
                def move(n):
                    w = (n % NT + 1) * P
                    act.wait_ge(probs_flipped, c * 8 + (first + n + 1))
                    nc.scalar.activation(pt[:, n % 2, :w], aux[2][:, :w], ACT.Copy).then_inc(probs_out, 1)

                for n in range(8):
                    w = (n % NT + 1) * P
                    act.wait_ge(biased, c * 8 + (first + n + 1))
                    nc.scalar.activation(pr[:, n % 2, :w], pr[:, n % 2, :w], ACT.Exp, scale=-1.0,
                                         bias=nmin[:, n:n + 1],
                                         accum_out=psum_[:, n:n + 1]).then_inc(probs, 1)
                    if n:
                        move(n - 1)
                move(7)

        def attention_on_vector(eng, first, step, q, queries, bias, gate, result, after_pair, extra):
            for c in step.loop(4, (8 if gate is None else 16) + extra):
                eng.wait_ge(scored, c * 8 + (first + 1))
                nc.vector.tensor_scalar(q[:], queries(c), -DH ** -0.5, None, ALU.mult).then_inc(q_staged, 1)

                def negate(n):
                    h, t = divmod(n, NT)
                    w = (t + 1) * P
                    eng.wait_ge(scored, c * 8 + (first + n + 2))
                    if n >= 2:
                        eng.wait_ge(probs_flipped, c * 8 + (first + n - 1))
                    alone(eng)
                    nc.vector.tensor_tensor_reduce(
                        out=pr[:, n % 2, :w], in0=aux[n % 2][:, :w], in1=bias(h)[:, T - w:], scale=1.0,
                        scalar=3.0e38, op0=ALU.add, op1=ALU.min,
                        accum_out=nmin[:, n:n + 1]).then_inc(biased, 1)

                def finish(n):
                    h, t = divmod(n, NT)
                    eng.wait_ge(weighed, c * 8 + (first + n + 1))
                    step(nc.vector.reciprocal(rs8[:, n:n + 1], psum_[:, n:n + 1]))
                    op = ALU.mult
                    if gate is not None:
                        op = ALU.add
                        step(nc.vector.tensor_tensor(rs8[:, n:n + 1], rs8[:, n:n + 1], gate(c, h, t), ALU.mult))
                    nc.vector.scalar_tensor_tensor(out=result(c, h, t), in0=aux[3][:, :DH],
                                                   scalar=rs8[:, n:n + 1], in1=result(c, h, t),
                                                   op0=ALU.mult, op1=op).then_inc(values_used, 1)

                for n in range(8):
                    negate(n)
                    if n >= 2:
                        finish(n - 2)
                finish(6)
                finish(7)
                after_pair()

        names = ("x_squares normalized ba_split ba_product ba_row_out ba_flipped ba_tanh ba_in ba_exps "
                 "sp_log conv_done conv_silu k_padded g_flip g_copy g_square g_reduced gate_sums "
                 "gate_cols gate_exps gate_done tg_ready row_sums qk_ready e_ready dec_in dec_ready u0 "
                 "t0 t0_out masked x_ready x_out tx_ready solved wt_ready wn_out vn_ready vn_out "
                 "o_ready o_out o_square mixed_squares post_done go_done ").split()
        on = {n: sem(n) for n in names}
        post_in = sem("post_in")

        def as_heads(bank):
            return bank[:].rearrange("p (h t) -> p h t", h=HG)


        def tile_of(buf, first, n):
            return buf[:, first:first + HG, bass.ts(n, P)]

        def heads(column):
            return column.rearrange("p (t h) -> p t h", h=HG)

        def spread(column, n):
            return column.unsqueeze(2).to_broadcast([P, HG, n])

        def each_head(table):
            return table.unsqueeze(1).to_broadcast([P, HG, table.shape[1]])


        PB2 = sb("feature_major_2", [P, 4 * B2_SLABS, T], F32, 112)
        PA2 = sb("token_major_2", [P, A2_SLABS, NT, NC], F32, 144)
        VH, AG, VSW = PA2[:, 0], PA2[:, 1], PA2[:, 2]
        YB = sb("y_b", [P, NT, NC], F32, 168)
        OA = sb("hgrn_out", [P, NT, HG, DG], F32, 168)
        hn = ("F", "LF", "KK", "B", "E", "EI", "ET", "QD", "KD", "KL", "QL", "KTM", "AM", "SS", "SQ")
        HB = {n: sb(f"hgrn_{n}", [P, T], F32, 176 + 2 * i) for i, n in enumerate(hn)}
        HB["KT"] = HB["F"]
        kz2 = sb("k_padded_2", [P, 2, 2, T], F32, 176)
        kc2 = sb("cmp_tokens", [P, 2, 2, T], F32, 184)
        xc = sb("cmp_blocks", [P, 2, 2, 8, 2, CMP_C], F32, 194)
        rope = sb("rope_tables", [P, 2, T], F32, 202)
        rope_t = sb("rope_temp", [P, 4, T], F32, 184)
        w1 = sb("cmp_w1", [P, 2, 8, 256], F32, 112)
        w2 = sb("cmp_w2", [P, 2, 2, P], F32, 144)
        hid4 = sb("cmp_hidden_4", [P, 2, 2, 4, CMP_C], F32, 146)
        hid = sb("cmp_hidden", [P, 2, 2, 2, CMP_C], F32, 148)
        pe = sb("cmp_positions", [P, 2, 16], F32, 149)
        kcz = sb("cmp_keys", [P, 2, CMP_C], F32, 149.25)
        sg = sb("branch_gates", [P, NT, N_GATE], F32, 149.5)
        vcz = sb("cmp_values", [P, 2, 4, DH], F32, 150)
        lc = sb("cmp_logits", [P, 8, CMP_C], F32, 194)
        pc = sb("cmp_probs", [P, 8, CMP_C], F32, 195)
        pct = sb("cmp_probs_t", [P, 2, P], F32, 196)
        pos = sb("positions_sb", [P, T], I32, 198)
        ya_hi, ya_lo = sb("ya_hi", [P, 4, T], F32R, 112), sb("ya_lo", [P, 4, T], F32R, 120)
        yb_hi, yb_lo = sb("yb_hi", [P, 4, T], F32R, 128), sb("yb_lo", [P, 4, T], F32R, 136)
        GT = sb("gate_tanh", [P, 4, T], F32, 144)
        MM = sb("merged", [P, 4, T], F32, 152)
        mt_hi, mt_lo = sb("mt_hi", [P, KD, T], F32R, 160), sb("mt_lo", [P, KD, T], F32R, 176)
        TM = sb("merged_b", [P, 2, T], F32, 192)
        ff_hi, ff_lo = sb("ff_hi", [P, 16, T], F32R, 112), sb("ff_lo", [P, 16, T], F32R, 144)
        ff_r, ff_s = sb("ff_relu", [P, 4, T], F32, 176), sb("ff_square", [P, 4, T], F32, 184)
        fin_w = sb("final_sb", [P, D], F32, 192)

        c1, c2, dec, h_ss, h_rs = small(16, 4), small(20, 4), small(24, 4), small(32, 16), small(48, 16)
        mn8, sm8 = small(64, 8), small(72, 8)
        names2 = ("x2_squares normalized2 lb_in lb_tanh gate_th h_th h_f h_lf h_b h_exps h_tail h_et "
                 "h_kl h_ktflip h_ktm h_attn h_kv h_states h_o h_oa h_summed rot_ready rot_used roped "
                 "cmp_moved cmp_blocks hid_out hid4_ready cmp_kv cmp_z c_scores c_shift c_exp c_probs "
                 "c_flip c_flip_out c_values c_out gates_in sine m_merged mt_hi_s mt_lo_s x3_squares "
                 "normalized3 square_s ffhi_s fflo_s x4_squares final_s trig_in rope_done ").split()
        for n in names2:
            on[n] = sem(n)
        pos_in, fin_in, pe_in, w2_in = sem("pos_in"), sem("fin_in"), sem("pe_in"), sem("w2_in")
        w1_in = [sem(f"w1_in{j}") for j in range(2)]
        w1_used = sem("w1_used")
        CHUNKS = HG_CHUNK

        def chunked(buf):
            return buf[:].rearrange("p (t c s) -> p t c s", c=2, s=CHUNKS)

        ROPED = (8, 9, 10, 11, 12, 14, 15)

        def pe_second(pe):
            pe.wait_ge(on["normalized2"], NT)
            flip_on_tensor(pe, lambda t, k: xn[:, t, k * P:(k + 1) * P], KD, FLIP2)
            pe.wait_ge(flip_lo, FLIP2 + KD)
            with pe.Fori(0, B2_SLABS) as i:
                for j in range(UPS):
                    weight_unit(pe, i * UPS + (U_B2 + j), j, 2 * j, ht_hi, ht_lo, i + SLAB_B2,
                                j == 0, j == UPS - 1, False)
            with pe.Fori(0, A2_SLABS) as i:
                for j in range(UPS):
                    weight_unit(pe, i * UPS + (U_A2 + j), j, 2 * j, ht_hi, ht_lo, i + SLAB_A2,
                                j == 0, j == UPS - 1, True)
            for b in range(4):
                pe.wait_ge(acc_out[b], SLAB_M)
            with pe.Fori(0, HG) as h:
                pe.wait_ge(on["h_kl"], h + 1)
                for t in range(NT):
                    done = nc.tensor.transpose(aux[0][:, t * P:(t + 1) * P], HB["KL"][:, t * P:(t + 1) * P],
                                               ident)
                done.then_inc(on["h_ktflip"], 1)
                for t in range(NT):
                    a, m, z = t * P, t * P + CHUNKS, (t + 1) * P
                    nc.tensor.matmul(aux[1][0:CHUNKS, a:m], HB["KD"][:, a:m], HB["QD"][:, a:m],
                                     start=True, stop=True)
                    nc.tensor.matmul(aux[1][0:CHUNKS, m:z], HB["KT"][:, a:m], HB["QD"][:, m:z],
                                     start=True, stop=True)
                    done = nc.tensor.matmul(aux[1][CHUNKS:P, m:z], HB["KD"][:, m:z], HB["QD"][:, m:z],
                                            start=True, stop=True)
                done.then_inc(on["h_attn"], 1)
                pe.wait_ge(on["h_ktm"], h + 1)
                for t in range(NT - 1):
                    done = nc.tensor.matmul(aux[2][:, t * P:(t + 1) * P], HB["KTM"][:, t * P:(t + 1) * P],
                                            VH[:, t, bass.ts(h, P)], start=True, stop=True)
                done.then_inc(on["h_kv"], 1)
                pe.wait_ge(on["h_states"], h + 1)
                for t in range(NT):
                    o = aux[3][:, t * P:(t + 1) * P]
                    done = nc.tensor.matmul(o, HB["AM"][:, t * P:(t + 1) * P], VH[:, t, bass.ts(h, P)],
                                            start=True, stop=t == 0)
                    if t:
                        done = nc.tensor.matmul(o, HB["QL"][:, t * P:(t + 1) * P],
                                                HB["SS"][:, (t - 1) * P:t * P], start=False, stop=True)
                done.then_inc(on["h_o"], 1)
            pe.wait_ge(on["rope_done"], 1)
            for n, ch in enumerate(ROPED):
                if n >= 2:
                    pe.wait_ge(on["rot_used"], n - 1)
                nc.tensor.matmul(aux[n % 2][:], const("rope_swap"), PB2[:, ch], start=True,
                                 stop=True).then_inc(on["rot_ready"], 1)
            for kv in range(2):
                pe.wait_ge(on["cmp_blocks"], kv + 1)
                if kv:
                    pe.wait_ge(on["hid_out"], 1)
                for ab in range(2):
                    n = 2 * kv + ab
                    pe.wait_ge(w1_in[ab], 16 * (kv + 1))
                    for hh in range(2):
                        for lp in range(8):
                            o = aux[2 + hh][:, 0:2 * CMP_C].rearrange("p (g c) -> p g c", g=2)[:, :, 0:N_CMP]
                            done = nc.tensor.matmul(o, w1[:, ab, lp, hh * P:(hh + 1) * P],
                                                    xc[:, kv, ab, lp, :, ab:ab + N_CMP],
                                                    start=ab == 0 and lp == 0, stop=ab == 1 and lp == 7)
                    done.then_inc(w1_used, 1)
            pe.wait_ge(on["hid_out"], 2)
            pe.wait_ge(w2_in, 16)
            for hh in range(2):
                done = nc.tensor.matmul(aux[0][:, 0:2 * CMP_C], w2[:, 0, hh], hid[:, 0, hh], start=hh == 0,
                                        stop=hh == 1)
            pe.wait_ge(on["hid4_ready"], 1)
            for g in range(2):
                for hh in range(2):
                    done = nc.tensor.matmul(aux[1][:, g * DH:(g + 1) * DH], hid4[:, hh, g], w2[:, 1, hh, 0:DH],
                                            start=hh == 0, stop=hh == 1)
            done.then_inc(on["cmp_kv"], 1)
            pe.wait_ge(on["cmp_z"], 1)
            for t in range(NT):
                for c in range(4):
                    o = aux[0][:, 0:256].rearrange("p (g c k) -> p c g k", g=2, c=4)[:, c]
                    done = nc.tensor.matmul(o, PB2[:, 8 + c, t * P:(t + 1) * P], kcz[:], start=True, stop=True)
                done.then_inc(on["c_scores"], 1)
                pe.wait_ge(on["c_probs"], t + 1)
                for g in range(2):
                    done = nc.tensor.transpose(aux[1][:, g * P:(g + 1) * P], pc[:, 4 * g:4 * g + 4], ident)
                done.then_inc(on["c_flip"], 1)
                pe.wait_ge(on["c_flip_out"], t + 1)
                if t:
                    pe.wait_ge(on["c_out"], t)
                for g in range(2):
                    done = nc.tensor.matmul(aux[2][:, g * 256:(g + 1) * 256], pct[:, g], vcz[:, g],
                                            start=True, stop=True)
                done.then_inc(on["c_values"], 1)
            pe.wait_ge(on["c_out"], NT)
            for first, s in ((SELECTED, 0), (WINDOW, 1)):
                attention_on_tensor(pe, first, q_st, lambda c, h: kz2[:, s, h],
                                    lambda c, h, j: VSW[:, j, s * P + h * DH:s * P + (h + 1) * DH])
            pe.wait_ge(values_used, WINDOW + STEPS + 1)
            flip_on_tensor(pe, lambda t, k: AG[:, t, k * P:(k + 1) * P], 4, FLIP_A)
            flip_on_tensor(pe, lambda t, k: YB[:, t, k * P:(k + 1) * P], 4, FLIP_B)
            pe.wait_ge(flip_lo, FLIP_B + 4)
            with pe.Fori(0, 2) as s:
                slab, unit = s * 4 + SLAB_M, s * 12 + U_M
                for part, (n_units, at) in enumerate(((4, 0), (2, 4), (4, 6), (2, 10))):
                    hi, lo = (ht_hi, ht_lo) if n_units == 4 else (ya_hi, ya_lo) if part == 1 else (yb_hi, yb_lo)
                    for j in range(n_units):
                        weight_unit(pe, unit + (at + j), (at + j) % RING, 2 * j, hi, lo, slab + part,
                                    j == 0, j == n_units - 1, False)
            pe.wait_ge(on["mt_lo_s"], KD + 1)
            with pe.Fori(0, O2_SLABS) as i:
                for j in range(UPS):
                    weight_unit(pe, i * UPS + (U_O2 + j), j, 2 * j, mt_hi, mt_lo, i + SLAB_O2,
                                j == 0, j == UPS - 1, True)
            pe.wait_ge(on["normalized3"], NT)
            flip_on_tensor(pe, lambda t, k: xn[:, t, k * P:(k + 1) * P], KD, FLIP3)
            pe.wait_ge(flip_lo, FLIP3 + KD)
            with pe.Fori(0, FF_HALVES) as f:
                with pe.Fori(0, FF1_SLABS) as i:
                    for j in range(UPS):
                        weight_unit(pe, f * U_HALF + i * UPS + (U_FF + j), j, 2 * j, ht_hi, ht_lo,
                                    f * SLABS_HALF + i + SLAB_FF, j == 0, j == UPS - 1, False)
                pe.wait_ge(on["fflo_s"], f * 16 + 17)
                alone(pe)
                with pe.Fori(0, 2) as n:
                    for j in range(FF2_UNITS):
                        weight_unit(pe, f * U_HALF + n * FF2_UNITS + (U_FF + UPS * FF1_SLABS + j), j % RING,
                                    2 * j, ff_hi, ff_lo, f * SLABS_HALF + n + (SLAB_FF + FF1_SLABS),
                                    j == 0, j == FF2_UNITS - 1, True)

        def act_second(act):
            for t in range(NT):
                act.wait_ge(on["post_done"], t + 1)
                nc.scalar.activation(xn[:, t], X[:, t], ACT.Square,
                                     accum_out=ss[:, t:t + 1]).then_inc(on["x2_squares"], 1)
            flip_hi_part(act, ht_hi, KD, FLIP2, lambda k: param("norm1", k))
            with act.Fori(0, B2_SLABS) as i:
                for b in range(4):
                    wait_bank(act, b, i + SLAB_B2, i * UPS + (U_B2 + UPS - 1))
                    nc.scalar.activation(PB2[:, i * 4 + b], acc[b][:], ACT.Copy).then_inc(acc_out[b], 1)
            for s in range(A2_SLABS):
                for b in range(4):
                    wait_bank(act, b, SLAB_A2 + s, U_A2 + UPS * s + UPS - 1)
                    nc.scalar.activation(PA2[:, s, b], acc[b][:], ACT.Silu if s == 1 else ACT.Copy)\
                        .then_inc(acc_out[b], 1)
            act.wait_ge(on["lb_in"], 1)
            nc.scalar.activation(c1, c1, ACT.Tanh, scale=0.5).then_inc(on["lb_tanh"], 1)
            with act.Fori(0, HG) as h:
                act.wait_ge(on["h_summed"], h + 1)
                nc.scalar.activation(HB["F"][:], PB2[:, h + 4], ACT.Tanh, scale=0.5).then_inc(on["h_th"], 1)
                act.wait_ge(on["h_f"], h + 1)
                nc.scalar.activation(HB["LF"][:], HB["F"][:], ACT.Ln).then_inc(on["h_lf"], 1)
                act.wait_ge(on["h_b"], h + 1)
                nc.scalar.activation(HB["E"][:], HB["B"][:], ACT.Exp).then_inc(on["h_exps"], 1)
                nc.scalar.activation(HB["EI"][:], HB["B"][:], ACT.Exp, scale=-1.0).then_inc(on["h_exps"], 1)
                act.wait_ge(on["h_tail"], h + 1)
                nc.scalar.activation(HB["ET"][:], HB["ET"][:], ACT.Exp).then_inc(on["h_et"], 1)
                act.wait_ge(on["h_ktflip"], h + 1)
                nc.scalar.activation(HB["KTM"][:], aux[0][:], ACT.Copy).then_inc(on["h_ktm"], 1)
                act.wait_ge(on["h_o"], h + 1)
                nc.scalar.activation(OA[:, :, h], aux[3][:].rearrange("p (t d) -> p t d", t=NT),
                                     ACT.Copy).then_inc(on["h_oa"], 1)
                nc.scalar.activation(HB["SQ"][:], aux[3][:], ACT.Square).then_inc(on["h_oa"], 1)
            act.wait_ge(on["h_summed"], HG + 1)
            act.dma_start(pos[:], positions).then_inc(pos_in, 16)
            act.dma_start(pe[:].rearrange("p a b -> p (a b)"), pe_kv).then_inc(pe_in, 16)
            act.dma_start(w2[:].rearrange("p a b c -> p (a b c)"), w2_kv).then_inc(w2_in, 16)
            for ab in range(2):
                act.dma_start(w1[:, ab].rearrange("p a b -> p (a b)"), w1_kv[0, ab]).then_inc(w1_in[ab], 16)
            act.wait_ge(on["trig_in"], 1)
            nc.scalar.activation(rope[:], rope[:], ACT.Sin).then_inc(on["sine"], 1)
            nc.scalar.activation(sg[:], VSW[:, :, 2 * P:2 * P + N_GATE], ACT.Tanh, scale=0.5)\
                .then_inc(on["gate_th"], 1)
            act.wait_ge(on["rope_done"], 2)
            for kv in range(2):
                for g in range(2):
                    src = PB2[g * DH:(g + 1) * DH, 12 + kv]
                    act.dma_start(kc2[0:DH, kv, g], src).then_inc(on["cmp_moved"], 16)
                    act.dma_start(kc2[DH:P, kv, g, 0:T - 1], src[:, 1:T]).then_inc(on["cmp_moved"], 16)
            for kv in range(2):
                if kv == 0:
                    for ab in range(2):
                        act.wait_ge(w1_used, ab + 1)
                        act.dma_start(w1[:, ab].rearrange("p a b -> p (a b)"), w1_kv[1, ab])\
                            .then_inc(w1_in[ab], 16)
                else:
                    act.wait_ge(w1_used, 4)
                for hh in range(2):
                    done = nc.scalar.activation(
                        hid[:, kv, hh, :, 0:N_CMP],
                        aux[2 + hh][:, 0:2 * CMP_C].rearrange("p (g c) -> p g c", g=2)[:, :, 0:N_CMP],
                        ACT.Gelu_apprx_tanh)
                done.then_inc(on["hid_out"], 1)
            for t in range(NT):
                act.wait_ge(on["c_shift"], t + 1)
                nc.scalar.activation(pc[:], lc[:], ACT.Exp).then_inc(on["c_exp"], 1)
                act.wait_ge(on["c_flip"], t + 1)
                nc.scalar.activation(pct[:].rearrange("p g q -> p (g q)"), aux[1][:, 0:2 * P],
                                     ACT.Copy).then_inc(on["c_flip_out"], 1)
                act.wait_ge(on["c_values"], t + 1)
                nc.scalar.activation(YB[:, t], aux[2][:], ACT.Copy).then_inc(on["c_out"], 1)
            attention_on_scalar(act, SELECTED)
            attention_on_scalar(act, WINDOW)
            flip_hi_part(act, ya_hi, 4, FLIP_A, lambda k: param("hgrn_norm"))
            flip_hi_part(act, yb_hi, 4, FLIP_B, lambda k: 1.0)
            with act.Fori(0, 2) as s:
                slab, unit = s * 4 + SLAB_M, s * 12 + U_M
                for part, last in ((0, 3), (2, 9)):
                    for b in range(4):
                        wait_bank(act, b, slab + part, unit + last)
                        nc.scalar.activation(GT[:, b], acc[b][:], ACT.Tanh, scale=0.5).then_inc(acc_out[b], 1)
                for b in range(4):
                    act.wait_ge(on["m_merged"], s * 4 + (b + 1))
                    nc.scalar.activation(mt_hi[:, s * 4 + b], MM[:, b], ACT.Copy, scale=0.5)\
                        .then_inc(on["mt_hi_s"], 1)
            for t in range(NT):
                act.wait_ge(acc_out[t], SLAB_FF)
                nc.scalar.activation(xn[:, t], X[:, t], ACT.Square,
                                     accum_out=ss[:, t:t + 1]).then_inc(on["x3_squares"], 1)
            flip_hi_part(act, ht_hi, KD, FLIP3, lambda k: param("norm2", k))
            with act.Fori(0, FF_HALVES) as f:
                with act.Fori(0, FF1_SLABS) as i:
                    for b in range(4):
                        act.wait_ge(on["fflo_s"], f * 16 + i * 4 + 1)
                        wait_bank(act, b, f * SLABS_HALF + i + SLAB_FF, f * U_HALF + i * UPS + (U_FF + UPS - 1))
                        nc.scalar.activation(ff_r[:, b], acc[b][:], ACT.Relu).then_inc(acc_out[b], 1)
                    for b in range(4):
                        act.wait_ge(on["square_s"], f * 16 + i * 4 + (b + 1))
                        nc.scalar.activation(ff_hi[:, i * 4 + b], ff_s[:, b], ACT.Copy).then_inc(on["ffhi_s"], 1)
            act.dma_start(fin_w[:], final_g).then_inc(fin_in, 16)
            for t in range(NT):
                act.wait_ge(acc_out[t], SLAB_FF + FF_HALVES * SLABS_HALF)
                nc.scalar.activation(xn[:, t], X[:, t], ACT.Square,
                                     accum_out=ss[:, t:t + 1]).then_inc(on["x4_squares"], 1)

        TWO_PI_PARTS = (6.28125, 2029.0 / 2 ** 20, 2 * np.pi - 6.28125 - 2029.0 / 2 ** 20)
        ROUND = 1.5 * 2 ** 23

        def dve_second(eng, step):
            V = nc.vector

            def normalize(squares, target):
                eng.wait_ge(squares, NT)
                step(V.tensor_scalar(ss, ss, 1.0 / D, EPS, ALU.mult, ALU.add))
                rsqrt(step, ss, rstd, tmp4)
                for t in range(NT):
                    V.tensor_scalar(xn[:, t], X[:, t], rstd[:, t:t + 1], None, ALU.mult).then_inc(target, 1)

            normalize(on["x2_squares"], on["normalized2"])
            flip_lo_part(eng, ht_hi, ht_lo, KD, FLIP2, lambda k: param("norm1", k))
            V.tensor_tensor(c1, param("lb", 0, 4), param("lb", 4, 4), ALU.subtract).then_inc(on["lb_in"], 1)
            eng.wait_ge(on["lb_tanh"], 1)
            step(V.tensor_scalar(c1, c1, 0.5, 0.5, ALU.mult, ALU.add))
            step(V.tensor_scalar(c2, c1, 0.5, 0.5, ALU.mult, ALU.add))
            step(V.tensor_scalar(c1, c1, -0.5, 0.5, ALU.mult, ALU.add))
            for b in range(4):
                eng.wait_ge(acc_out[b], SLAB_A2)
            step(V.memset(HB["AM"][:], 0.0))
            for h in step.loop(HG, 12):
                one = bass.ds(h, 1)
                eng.wait_ge(on["h_th"], h + 1)
                V.tensor_scalar(HB["F"][:], HB["F"][:], c1[:, one], c2[:, one], ALU.mult,
                                ALU.add).then_inc(on["h_f"], 1)
                eng.wait_ge(on["h_lf"], h + 1)
                step(V.tensor_scalar(HB["KK"][:], HB["F"][:], -1.0, 1.0, ALU.mult, ALU.add))
                V.tensor_tensor_scan(HB["B"][:], const("restart"), HB["LF"][:], 0.0, ALU.mult,
                                     ALU.add).then_inc(on["h_b"], 1)
                eng.wait_ge(on["h_b"], h + 1)
                b8 = HB["B"][:].rearrange("p (n s) -> p n s", s=CHUNKS)
                V.tensor_tensor(HB["ET"][:].rearrange("p (n s) -> p n s", s=CHUNKS),
                                b8[:, :, CHUNKS - 1:CHUNKS].to_broadcast([P, T // CHUNKS, CHUNKS]), b8,
                                ALU.subtract).then_inc(on["h_tail"], 1)
                eng.wait_ge(on["h_exps"], h * 2 + 2)
                step(V.tensor_tensor(HB["QD"][:], PB2[:, h], HB["E"][:], ALU.mult))
                step(V.tensor_tensor(HB["KD"][:], HB["KK"][:], HB["EI"][:], ALU.mult))
                eng.wait_ge(on["h_et"], h + 1)
                step(V.tensor_tensor(HB["KT"][:], HB["KK"][:], HB["ET"][:], ALU.mult))
                e4, kt4, kl4 = chunked(HB["E"]), chunked(HB["KT"]), chunked(HB["KL"])
                qd4, ql4 = chunked(HB["QD"]), chunked(HB["QL"])
                last = slice(CHUNKS - 1, CHUNKS)
                shape = [P, NT, CHUNKS]
                step(V.tensor_tensor(ql4[:, :, 1], qd4[:, :, 1], e4[:, :, 0, last].to_broadcast(shape), ALU.mult))
                step(V.tensor_copy(ql4[:, :, 0], qd4[:, :, 0]))
                step(V.tensor_tensor(dec.unsqueeze(2), e4[:, :, 0, last], e4[:, :, 1, last], ALU.mult))
                step(V.tensor_copy(kl4[:, :, 1], kt4[:, :, 1]))
                V.tensor_tensor(kl4[:, :, 0], kt4[:, :, 0], e4[:, :, 1, last].to_broadcast(shape),
                                ALU.mult).then_inc(on["h_kl"], 1)
                eng.wait_ge(on["h_attn"], h + 1)
                alone(eng)
                attn = aux[1][:].rearrange("p (t s) -> p t s", t=NT)
                am = HB["AM"][:].rearrange("p (t s) -> p t s", t=NT)
                mask = const("tri").bitcast(I32)
                step(V.copy_predicated(am[0:CHUNKS],
                                       mask[0:CHUNKS].unsqueeze(1).to_broadcast([CHUNKS, NT, P]), attn[0:CHUNKS]))
                alone(eng)
                step(V.copy_predicated(am[CHUNKS:P, :, CHUNKS:P],
                                       mask[CHUNKS:P, CHUNKS:P].unsqueeze(1).to_broadcast([CHUNKS, NT, CHUNKS]),
                                       attn[CHUNKS:P, :, CHUNKS:P]))
                eng.wait_ge(on["h_kv"], h + 1)
                step(V.tensor_copy(HB["SS"][:, 0:P], aux[2][:, 0:P]))
                step(V.scalar_tensor_tensor(out=HB["SS"][:, P:2 * P], in0=HB["SS"][:, 0:P], scalar=dec[:, 1:2],
                                            in1=aux[2][:, P:2 * P], op0=ALU.mult, op1=ALU.add))
                V.scalar_tensor_tensor(out=HB["SS"][:, 2 * P:3 * P], in0=HB["SS"][:, P:2 * P],
                                       scalar=dec[:, 2:3], in1=aux[2][:, 2 * P:3 * P], op0=ALU.mult,
                                       op1=ALU.add).then_inc(on["h_states"], 1)
                eng.wait_ge(on["h_oa"], h * 2 + 2)
                V.tensor_reduce(heads(h_ss)[:, :, one], HB["SQ"][:].rearrange("p (t d) -> p t d", t=NT),
                                AX, ALU.add).then_inc(on["h_summed"], 1)
            eng.wait_ge(on["h_summed"], HG + 1)
            step(V.tensor_scalar(h_ss, h_ss, 1.0 / DG, EPS, ALU.mult, ALU.add))
            rsqrt(step, h_ss, h_rs, t32[:, 0:16])
            for t in range(NT):
                step(V.tensor_tensor(OA[:, t], OA[:, t], spread(h_rs[:, t * HG:(t + 1) * HG], DG), ALU.mult))
                step(V.tensor_tensor(AG[:, t], AG[:, t], OA[:, t].rearrange("p h d -> p (h d)"), ALU.mult))
            eng.wait_ge(pos_in, 16)
            ang, turns = rope_t[:, 0], rope_t[:, 1]
            step(V.tensor_copy(turns, pos[:]))
            step(V.tensor_scalar(ang, turns, const("inv_freq"), None, ALU.mult))
            for s, quarter in ((0, 0.25), (1, 0.0)):
                red = rope[:, s]
                step(V.tensor_scalar(turns, ang, float(1 / (2 * np.pi)), quarter, ALU.mult, ALU.add))
                step(V.tensor_scalar(turns, turns, ROUND, -ROUND, ALU.add, ALU.add))
                step(V.scalar_tensor_tensor(out=red, in0=turns, scalar=-TWO_PI_PARTS[0], in1=ang,
                                            op0=ALU.mult, op1=ALU.add))
                for part in TWO_PI_PARTS[1:]:
                    step(V.scalar_tensor_tensor(out=red, in0=turns, scalar=-float(part), in1=red,
                                                op0=ALU.mult, op1=ALU.add))
                if s == 0:
                    step(V.tensor_scalar(red, red, float(np.pi / 2), None, ALU.add))
                done = V.tensor_scalar(red, red, 3.1415925, -3.1415925, ALU.min, ALU.max)
                if s == 0:
                    step(done)
            done.then_inc(on["trig_in"], 1)
            step(V.memset(kz2[:], 0.0))
            eng.wait_ge(on["sine"], 1)
            V.memset(hid[:], 0.0).then_inc(on["rope_done"], 1)
            for n, ch in enumerate(ROPED):
                eng.wait_ge(on["rot_ready"], n + 1)
                turned = rope_t[:, n % 2]
                V.tensor_tensor(turned, aux[n % 2][:], rope[:, 1], ALU.mult).then_inc(on["rot_used"], 1)
                step(V.tensor_tensor(PB2[:, ch], PB2[:, ch], rope[:, 0], ALU.mult))
                eng.wait_ge(on["rot_used"], n + 1)
                if ch < 14:
                    V.tensor_tensor(PB2[:, ch], PB2[:, ch], turned, ALU.add).then_inc(on["roped"], 1)
                else:
                    for g in range(2):
                        rows = slice(g * DH, (g + 1) * DH)
                        step(V.tensor_tensor(kz2[rows, ch - 14, g], PB2[rows, ch], rope_t[rows, n % 2], ALU.add))
            eng.wait_ge(on["gate_th"], 1)
            V.tensor_scalar(sg[:], sg[:], 0.5, 0.5, ALU.mult, ALU.add).then_inc(on["gates_in"], 1)
            eng.wait_ge(on["roped"], 5)
            V.memset(kcz[:], 0.0).then_inc(on["rope_done"], 1)
            step(V.memset(vcz[:], 0.0))
            eng.wait_ge(pe_in, 16)
            eng.wait_ge(on["cmp_moved"], 16 * 8)
            for kv in range(2):
                tokens = kc2[:, kv].rearrange("p g (c l two) -> p l (g c) two", l=8, two=2)[:, :, :, 0]
                for ab in range(2):
                    done = V.tensor_tensor(
                        xc[:, kv, ab].rearrange("p l g c -> p l (g c)"), tokens,
                        pe[:, kv, 8 * ab:8 * ab + 8].unsqueeze(2).to_broadcast([P, 8, 2 * CMP_C]), ALU.add)
                    if ab == 0:
                        step(done)
                done.then_inc(on["cmp_blocks"], 1)
            eng.wait_ge(on["hid_out"], 2)
            for hh in range(2):
                done = V.tensor_copy(hid4[:, hh], hid[:, 1, hh].unsqueeze(2).to_broadcast([P, 2, 4, CMP_C]))
                if hh == 0:
                    step(done)
            done.then_inc(on["hid4_ready"], 1)
            eng.wait_ge(on["cmp_kv"], 1)
            for g in range(2):
                rows = slice(g * DH, (g + 1) * DH)
                step(V.tensor_copy(kcz[rows, g], aux[0][rows, g * CMP_C:(g + 1) * CMP_C]))
            for h in range(4):
                rows = slice(h * CMP_C, (h + 1) * CMP_C)
                done = V.tensor_copy(vcz[rows, :, h], aux[1][rows, 0:2 * DH].rearrange("p (g d) -> p g d", g=2))
                if h < 3:
                    step(done)
            done.then_inc(on["cmp_z"], 1)
            eng.wait_ge(on["gates_in"], 1)
            for t in range(NT):
                hide = each_of_8(const("cmp_hide")[:, t * CMP_C:(t + 1) * CMP_C])
                keep = each_of_8(const("cmp_keep")[:, t * CMP_C:(t + 1) * CMP_C])
                eng.wait_ge(on["c_scores"], t + 1)
                step(V.scalar_tensor_tensor(out=lc[:], in0=aux[0][:, 0:256].rearrange("p (h c) -> p h c", h=8),
                                            scalar=-DH ** -0.5, in1=hide, op0=ALU.mult, op1=ALU.add))
                step(V.tensor_reduce(mn8, lc[:], AX, ALU.min))
                V.tensor_tensor(lc[:], mn8.unsqueeze(2).to_broadcast([P, 8, CMP_C]), lc[:],
                                ALU.subtract).then_inc(on["c_shift"], 1)
                eng.wait_ge(on["c_exp"], t + 1)
                step(V.tensor_tensor(pc[:], pc[:], keep, ALU.mult))
                step(V.tensor_reduce(sm8, pc[:], AX, ALU.add))
                step(V.tensor_scalar(sm8, sm8, 1e-30, None, ALU.max))
                step(V.reciprocal(sm8, sm8))
                step(V.tensor_tensor(sm8, sm8, sg[:, t].rearrange("p (h b) -> p h b", b=3)[:, :, 0], ALU.mult))
                V.tensor_tensor(pc[:], pc[:], sm8.unsqueeze(2).to_broadcast([P, 8, CMP_C]),
                                ALU.mult).then_inc(on["c_probs"], 1)
            eng.wait_ge(on["c_out"], NT)
            for first, branch in ((SELECTED, 1), (WINDOW, 2)):
                eng.wait_ge(values_used, first + 1)
                attention_on_vector(eng, first, step, q_st, lambda c: PB2[:, c + 8], lambda h: const("causal"),
                                    lambda c, h, t: sg[:, t, bass.ds(c * 3 + (12 * h + branch), 1)],
                                    lambda c, h, t: YB[:, t, bass.ds(c * DH + 4 * DH * h, DH)], lambda: None, 0)
            flip_lo_part(eng, ya_hi, ya_lo, 4, FLIP_A, lambda k: param("hgrn_norm"))
            flip_lo_part(eng, yb_hi, yb_lo, 4, FLIP_B, lambda k: 1.0)
            with eng.Fori(0, 2) as s:
                slab, unit = s * 4 + SLAB_M, s * 12 + U_M
                eng.wait_ge(on["mt_lo_s"], s * 4 + 1)
                for b in range(4):
                    wait_bank(eng, b, slab + 1, unit + 5)
                    V.scalar_tensor_tensor(out=MM[:, b], in0=GT[:, b], scalar=1.0, in1=acc[b][:], op0=ALU.add,
                                           op1=ALU.mult).then_inc(acc_out[b], 1)
                for b in range(4):
                    wait_bank(eng, b, slab + 3, unit + 11)
                    V.scalar_tensor_tensor(out=TM[:, b % 2], in0=GT[:, b], scalar=1.0, in1=acc[b][:],
                                           op0=ALU.add, op1=ALU.mult).then_inc(acc_out[b], 1)
                    eng.wait_ge(acc_out[b], slab + 4)
                    V.tensor_tensor(MM[:, b], MM[:, b], TM[:, b % 2], ALU.add).then_inc(on["m_merged"], 1)
                    eng.wait_ge(on["mt_hi_s"], s * 4 + (b + 1))
                    V.scalar_tensor_tensor(out=mt_lo[:, s * 4 + b], in0=MM[:, b], scalar=0.5,
                                           in1=mt_hi[:, s * 4 + b].bitcast(F32), op0=ALU.mult,
                                           op1=ALU.subtract).then_inc(on["mt_lo_s"], 1)

            def add_to_residual(slab, last_unit, n):
                for b in range(4):
                    wait_bank(eng, b, slab, last_unit)
                    cols = X[:, b, bass.ts(n, NC)]
                    V.tensor_tensor(cols, cols, acc[b][:], ALU.add).then_inc(acc_out[b], 1)

            with eng.Fori(0, O2_SLABS) as i:
                add_to_residual(i + SLAB_O2, i * UPS + (U_O2 + UPS - 1), i)
            normalize(on["x3_squares"], on["normalized3"])
            flip_lo_part(eng, ht_hi, ht_lo, KD, FLIP3, lambda k: param("norm2", k))
            with eng.Fori(0, FF_HALVES) as f:
                with eng.Fori(0, FF1_SLABS) as i:
                    for b in range(4):
                        eng.wait_ge(acc_out[b], f * SLABS_HALF + i + (SLAB_FF + 1))
                        V.tensor_tensor(ff_s[:, b], ff_r[:, b], ff_r[:, b], ALU.mult).then_inc(on["square_s"], 1)
                    for b in range(4):
                        eng.wait_ge(on["ffhi_s"], f * 16 + i * 4 + (b + 1))
                        V.tensor_tensor(ff_lo[:, i * 4 + b], ff_s[:, b], ff_hi[:, i * 4 + b].bitcast(F32),
                                        ALU.subtract).then_inc(on["fflo_s"], 1)
                with eng.Fori(0, 2) as n:
                    add_to_residual(f * SLABS_HALF + n + (SLAB_FF + FF1_SLABS),
                                    f * U_HALF + n * FF2_UNITS + (U_FF + UPS * FF1_SLABS + FF2_UNITS - 1), n)
            eng.wait_ge(on["x4_squares"], NT)
            eng.wait_ge(fin_in, 16)
            step(V.tensor_scalar(ss, ss, 1.0 / D, EPS, ALU.mult, ALU.add))
            rsqrt(step, ss, rstd, tmp4)
            for t in range(NT):
                V.scalar_tensor_tensor(out=xn[:, t], in0=X[:, t], scalar=rstd[:, t:t + 1], in1=fin_w[:],
                                       op0=ALU.mult, op1=ALU.mult).then_inc(on["final_s"], 1)

        def sp_rest(sp):
            rows = out.rearrange("(t p) d -> p t d", p=P)
            for t in range(NT):
                sp.wait_ge(on["final_s"], t + 1)
                sp.dma_start(rows[:, t], xn[:, t]).then_inc(stored, 16)
            sp.wait_ge(stored, 16 * NT)

        def each_of_8(table):
            return table.unsqueeze(1).to_broadcast([P, 8, CMP_C])


        block = ctx.enter_context(nc.Block())

        @block.sync
        def _(sp):
            sp.dma_start(X[:], x.rearrange("(t p) d -> p t d", p=P)).then_inc(x_in, 16)
            sp.dma_start(C[:], consts).then_inc(consts_in, 16)
            sp.dma_start(PAR[:], params).then_inc(consts_in, 16)
            for j in range(RING):
                sp.dma_start(raw[:, j].rearrange("p k n -> p (k n)"), units[j]).then_inc(raw_in[j], 16)
            sp.dma_start(wba[:].rearrange("p k n -> p (k n)"), w_ba).then_inc(small_in, 16)
            with sp.Fori(1, N_UNITS // RING) as i:
                for j in range(RING):
                    sp.wait_ge(w_split, i * RING + (j - RING + 1))
                    sp.dma_start(raw[:, j].rearrange("p k n -> p (k n)"),
                                 units[i * RING + j]).then_inc(raw_in[j], 16)
            sp_rest(sp)

        @block.gpsimd
        def _(pool):
            def split(unit, i, j, reused):
                pool.wait_ge(raw_in[j], i * 16 + 16)
                if reused:
                    pool.wait_ge(unit_used, unit - (RING - 1))
                alone(pool)
                nc.gpsimd.tensor_scalar(w_hi[:, j], raw[:, j], 1.0, None, ALU.mult).then_inc(hi_split, 1)
                pool.wait_ge(hi_split, unit + 1)
                nc.gpsimd.tensor_tensor(w_lo[:, j], raw[:, j], w_hi[:, j].bitcast(F32),
                                        ALU.subtract).then_inc(w_split, 1)

            for j in range(RING):
                split(j, 0, j, False)
            with pool.Fori(1, N_UNITS // RING) as i:
                for j in range(RING):
                    split(i * RING + j, i, j, True)

        @block.tensor
        def _(pe):
            for count in (*acc_ready, scored):
                pe.sem_inc(count, 1)
            pe.wait_ge(consts_in, 32)
            pe.wait_ge(on["normalized"], NT)
            flip_on_tensor(pe, lambda t, k: xn[:, t, k * P:(k + 1) * P], KD, FLIP1)
            pe.wait_ge(flip_lo, FLIP1 + KD)
            with pe.Fori(0, B1_SLABS) as i:
                for j in range(UPS):
                    weight_unit(pe, i * UPS + (U_B1 + j), j, 2 * j, ht_hi, ht_lo, i + SLAB_B1,
                                j == 0, j == UPS - 1, False)
            pe.wait_ge(on["ba_split"], 2)
            for k in range(KD):
                done = split_product(pe, aux[0][:], (wba_hi[:, k], wba_lo[:, k]),
                                     (ht_hi[:, k], ht_lo[:, k]), k == 0, k == KD - 1)
            done.then_inc(on["ba_product"], 1)
            with pe.Fori(0, A1_SLABS) as i:
                for j in range(UPS):
                    weight_unit(pe, i * UPS + (U_A1 + j), j, 2 * j, ht_hi, ht_lo, i + SLAB_A1,
                                j == 0, j == UPS - 1, True)
            pe.wait_ge(on["ba_row_out"], 1)
            for t in range(NT):
                done = nc.tensor.transpose(aux[1][:, t * 8:(t + 1) * 8], ba_row[0:8, t * P:(t + 1) * P],
                                           ident[0:8, 0:8])
            done.then_inc(on["ba_flipped"], 1)
            pe.wait_ge(on["ba_in"], 1)
            pe.wait_ge(on["k_padded"], 1)
            for b in range(4):
                pe.wait_ge(acc_out[b], SLAB_O1)
            attention_on_tensor(pe, MOBA, q_st, lambda c, h: kz[:, c, h],
                                lambda c, h, j: V1[:, j, bass.ds(c * P + h * DH, DH)])
            for n in range(12):
                if n >= 2:
                    pe.wait_ge(on["g_copy"], n - 1)
                for t in range(NT):
                    done = nc.tensor.transpose(acc[n % 2][:, t * P:(t + 1) * P],
                                               PB[:, 8 + n, t * P:(t + 1) * P], ident)
                done.then_inc(on["g_flip"], 1)
            pe.wait_ge(on["gate_sums"], 1)
            nc.tensor.matmul(acc[2][:, 0:16], const("tri"), gcol, start=True, stop=True)
            nc.tensor.matmul(acc[2][:, 16:32], const("ones"), gcol, start=True,
                             stop=True).then_inc(on["gate_cols"], 1)
            with pe.Fori(0, NT) as n:
                pe.wait_ge(on["tg_ready"], n + 1)
                nc.tensor.matmul(aux[0][:], const("ones"), G["TG"][:], start=True, stop=True)
                nc.tensor.matmul(aux[1][:], const("ones"), G["IB"][:], start=True,
                                 stop=True).then_inc(on["row_sums"], 1)
                for h in range(HG):
                    nc.tensor.matmul(aux[2][:, h * P:(h + 1) * P], G["KT"][:, h], G["KT"][:, h],
                                     start=True, stop=True)
                for h in range(HG):
                    done = nc.tensor.matmul(aux[3][:, h * P:(h + 1) * P], G["KT"][:, h],
                                            PB[:, 8 + h, bass.ts(n, P)], start=True, stop=True)
                done.then_inc(on["qk_ready"], 1)
                pe.wait_ge(on["u0"], n + 1)
                for h in range(HG):
                    done = nc.tensor.transpose(acc[0][:, h * P:(h + 1) * P], G["U"][:, h], ident)
                done.then_inc(on["t0"], 1)
                for m in range(6):
                    pe.wait_ge(on["masked"], n * 6 + m + 1)
                    for h in range(HG):
                        done = nc.tensor.matmul(acc[1][:, h * P:(h + 1) * P], G["MA"][:, h], G["TI"][:, h],
                                                start=True, stop=True)
                    done.then_inc(on["x_ready"], 1)
                    pe.wait_ge(on["x_out"], n * 6 + m + 1)
                    for h in range(HG):
                        done = nc.tensor.matmul(acc[2][:, h * P:(h + 1) * P], G["U"][:, h], G["XS"][:, h],
                                                start=True, stop=True)
                    for h in range(HG):
                        done = nc.tensor.matmul(acc[3][:, h * P:(h + 1) * P], G["XS"][:, h], G["U"][:, h],
                                                start=True, stop=True)
                    done.then_inc(on["tx_ready"], 1)
                pe.wait_ge(on["solved"], n + 1)
                for h in range(HG):
                    done = nc.tensor.matmul(acc[0][:, h * P:(h + 1) * P], G["KBG"][:, h], G["U"][:, h],
                                            start=True, stop=True)
                done.then_inc(on["wt_ready"], 1)
                pe.wait_ge(on["wn_out"], n + 1)
                for h in range(HG):
                    nc.tensor.matmul(acc[1][:, h * P:(h + 1) * P], G["U"][:, h], G["VB"][:, h],
                                     start=True, stop=False)
                    done = nc.tensor.matmul(acc[1][:, h * P:(h + 1) * P], G["WN"][:, h], G["S"][:, h],
                                            start=False, stop=True)
                done.then_inc(on["vn_ready"], 1)
                pe.wait_ge(on["vn_out"], n + 1)
                for h in range(HG):
                    nc.tensor.matmul(acc[2][:, h * P:(h + 1) * P], G["QD"][:, h], G["S"][:, h],
                                     start=True, stop=False)
                    nc.tensor.matmul(acc[2][:, h * P:(h + 1) * P], G["INT"][:, h], G["VN"][:, h],
                                     start=False, stop=True)
                for h in range(HG):
                    done = nc.tensor.matmul(acc[3][:, h * P:(h + 1) * P], G["KDEC"][:, h], G["VN"][:, h],
                                            start=True, stop=True)
                done.then_inc(on["o_ready"], 1)
            pe.wait_ge(on["go_done"], 1)
            pe.wait_ge(values_used, MOBA + STEPS + 1)
            flip_on_tensor(pe, lambda t, k: PA[:, 1 + k // 4, t, (k % 4) * P:(k % 4 + 1) * P], KD, FLIP_MIXED)
            pe.wait_ge(flip_lo, FLIP_MIXED + KD)
            with pe.Fori(0, O1_SLABS) as i:
                for j in range(UPS):
                    weight_unit(pe, i * UPS + (U_O1 + j), j, 2 * j, ht_hi, ht_lo, i + SLAB_O1,
                                j == 0, j == UPS - 1, True)
            pe_second(pe)

        @block.scalar
        def _(act):
            for count in (*acc_out, on["conv_silu"]):
                act.sem_inc(count, 1)
            act.wait_ge(x_in, 16)
            for t in range(NT):
                nc.scalar.activation(xn[:, t], X[:, t], ACT.Square,
                                     accum_out=ss[:, t:t + 1]).then_inc(on["x_squares"], 1)
            act.wait_ge(consts_in, 32)
            flip_hi_part(act, ht_hi, KD, FLIP1, lambda k: param("norm_pre", k))
            with act.Fori(0, B1_SLABS) as i:
                for b in range(4):
                    wait_bank(act, b, i + SLAB_B1, i * UPS + (U_B1 + UPS - 1))
                    nc.scalar.activation(PB[:, i * 4 + b], acc[b][:], ACT.Copy).then_inc(acc_out[b], 1)
            act.wait_ge(on["ba_product"], 1)
            nc.scalar.activation(ba_row[0:8], aux[0][0:8, :], ACT.Copy).then_inc(on["ba_row_out"], 1)
            for s in range(A1_SLABS):
                for b in range(4):
                    act.wait_ge(on["conv_done"], 4 * s + b + 1)
                    nc.scalar.activation(PB[:, 8 + 4 * s + b], conv4[:, b], ACT.Silu).then_inc(on["conv_silu"], 1)
                for b in range(4):
                    wait_bank(act, b, SLAB_A1 + s, U_A1 + UPS * s + UPS - 1)
                    nc.scalar.activation(PA[:, s, b], acc[b][:], ACT.Silu if s else ACT.Copy)\
                        .then_inc(acc_out[b], 1)
            act.wait_ge(on["ba_in"], 1)
            bv = ba.rearrange("p (t c) -> p t c", c=8)
            nc.scalar.activation(heads(beta), bv[:, :, 0:4], ACT.Tanh, scale=0.5).then_inc(on["ba_tanh"], 1)
            nc.scalar.activation(nega, param("a_log", 0, HG), ACT.Exp).then_inc(on["ba_tanh"], 1)
            nc.scalar.activation(t32[:, 0:16], t32[:, 0:16], ACT.Exp, scale=-1.0).then_inc(on["ba_exps"], 1)
            act.wait_ge(on["ba_exps"], 1)
            nc.scalar.activation(t32[:, 16:32], t32[:, 0:16], ACT.Ln, bias=1.0).then_inc(on["sp_log"], 1)
            attention_on_scalar(act, MOBA)
            for n in range(12):
                act.wait_ge(on["g_flip"], n + 1)
                if n < 4:
                    act.wait_ge(on["g_reduced"], n)
                    nc.scalar.activation(sq[:], acc[n % 2][:], ACT.Square).then_inc(on["g_copy"], 1)
                elif n < 8:
                    act.wait_ge(on["g_reduced"], n)
                    nc.scalar.activation(sq[:], acc[n % 2][:], ACT.Square).then_inc(on["g_square"], 1)
                    nc.scalar.activation(KM[:, n - 4], acc[n % 2][:], ACT.Copy).then_inc(on["g_copy"], 1)
                else:
                    nc.scalar.activation(VM[:, n - 8], acc[n % 2][:], ACT.Copy).then_inc(on["g_copy"], 1)
            act.wait_ge(on["gate_cols"], 1)
            nc.scalar.activation(eg, acc[2][:, 0:16], ACT.Exp).then_inc(on["gate_exps"], 1)
            nc.scalar.activation(egl, acc[2][:, 16:32], ACT.Exp).then_inc(on["gate_exps"], 1)
            act.wait_ge(on["gate_done"], 1)
            nc.scalar.activation(dl, dl, ACT.Exp).then_inc(on["gate_exps"], 1)
            with act.Fori(0, NT) as n:
                act.wait_ge(on["row_sums"], n + 1)
                nc.scalar.activation(G["EG"][:], aux[0][:], ACT.Exp).then_inc(on["e_ready"], 1)
                act.wait_ge(on["dec_in"], n + 1)
                nc.scalar.activation(G["DEC"][:], G["DEC"][:], ACT.Exp).then_inc(on["dec_ready"], 1)
                act.wait_ge(on["t0"], n + 1)
                nc.scalar.activation(G["TI"][:], acc[0][:], ACT.Copy).then_inc(on["t0_out"], 1)
                for m in range(6):
                    act.wait_ge(on["x_ready"], n * 6 + m + 1)
                    nc.scalar.activation(G["XS"][:], acc[1][:], ACT.Copy).then_inc(on["x_out"], 1)
                act.wait_ge(on["wt_ready"], n + 1)
                nc.scalar.activation(G["WN"][:], acc[0][:], ACT.Copy, scale=-1.0).then_inc(on["wn_out"], 1)
                act.wait_ge(on["vn_ready"], n + 1)
                nc.scalar.activation(G["VN"][:], acc[1][:], ACT.Copy).then_inc(on["vn_out"], 1)
                act.wait_ge(on["o_out"], n + 1)
                nc.scalar.activation(G["XS"][:], GO[:, n], ACT.Square).then_inc(on["o_square"], 1)
            act.wait_ge(on["go_done"], 1)
            act.dma_start(post_w[:], norm_post).then_inc(post_in, 16)
            flip_hi_part(act, ht_hi, KD, FLIP_MIXED, lambda k: param("gdn_norm") if k >= 4 else 1.0)
            with act.Fori(0, O1_SLABS) as i:
                for b in range(4):
                    wait_bank(act, b, i + SLAB_O1, i * UPS + (U_O1 + UPS - 1))
                    nc.scalar.activation(mixed[:, b, bass.ts(i, NC)], acc[b][:], ACT.Copy).then_inc(acc_out[b], 1)
            for b in range(4):
                act.wait_ge(acc_out[b], SLAB_B2)
                nc.scalar.activation(xn[:, b], mixed[:, b], ACT.Square,
                                     accum_out=ss[:, b:b + 1]).then_inc(on["mixed_squares"], 1)
            act_second(act)

        @block.vector
        def _(eng):
            step = Steps(eng, dve)
            for count in (values_used, on["h_summed"], on["mt_lo_s"], on["fflo_s"]):
                eng.sem_inc(count, 1)
            V = nc.vector

            def row_norm(squares, n, width):
                step(V.tensor_scalar(ss, ss, 1.0 / width, EPS, ALU.mult, ALU.add))
                rsqrt(step, ss, rstd, tmp4)

            eng.wait_ge(small_in, 16)
            step(V.memset(wba_hi[:].bitcast(F32), 0.0))
            step(V.memset(wba_lo[:].bitcast(F32), 0.0))
            V.tensor_copy(wba_hi[:, :, 0:8], wba[:]).then_inc(on["ba_split"], 1)
            eng.wait_ge(on["ba_split"], 1)
            V.tensor_tensor(wba_lo[:, :, 0:8], wba[:], wba_hi[:, :, 0:8].bitcast(F32),
                            ALU.subtract).then_inc(on["ba_split"], 1)
            eng.wait_ge(on["x_squares"], NT)
            row_norm(ss, NT, D)
            for t in range(NT):
                V.tensor_scalar(xn[:, t], X[:, t], rstd[:, t:t + 1], None, ALU.mult).then_inc(on["normalized"], 1)
            eng.wait_ge(consts_in, 32)
            flip_lo_part(eng, ht_hi, ht_lo, KD, FLIP1, lambda k: param("norm_pre", k))
            for i in step.loop(3, 12):
                eng.wait_ge(on["conv_silu"], i * 4 + 1)
                for b in range(4):
                    eng.wait_ge(acc_out[b], i + (SLAB_B1 + 3))
                    src = PB[:, i * 4 + (8 + b)]
                    taps = PAR[:, bass.ds(i * 16 + (PARAM_COLS["conv"][0] + 4 * b), 4)]
                    step(V.tensor_scalar(conv4[:, b], src, taps[:, 3:4], None, ALU.mult))
                    for back in (1, 2):
                        step(V.scalar_tensor_tensor(out=conv4[:, b, back:], in0=src[:, :T - back],
                                                    scalar=taps[:, 3 - back:4 - back], in1=conv4[:, b, back:],
                                                    op0=ALU.mult, op1=ALU.add))
                    V.scalar_tensor_tensor(out=conv4[:, b, 3:], in0=src[:, :T - 3], scalar=taps[:, 0:1],
                                           in1=conv4[:, b, 3:], op0=ALU.mult,
                                           op1=ALU.add).then_inc(on["conv_done"], 1)
            eng.wait_ge(on["conv_silu"], 13)
            step(V.memset(kz[:], 0.0))
            for c in range(4):
                for h in range(2):
                    step(V.tensor_copy(kz[h * DH:(h + 1) * DH, c, h], PB[h * DH:(h + 1) * DH, 4 + c]))
            step(V.tensor_copy(alibi[:, 0], const("alibi")))
            V.tensor_scalar(alibi[:, 1], const("alibi"), 0.5, None, ALU.mult).then_inc(on["k_padded"], 1)
            eng.wait_ge(on["k_padded"], 1)
            eng.wait_ge(on["ba_flipped"], 1)
            bv = ba.rearrange("p (t c) -> p t c", c=8)
            step(V.tensor_copy(ba, aux[1][:, 0:32]))
            step(V.tensor_tensor(bv[:, :, 4:8], bv[:, :, 4:8],
                                 param("dt_bias", 0, HG).unsqueeze(1).to_broadcast([P, NT, HG]), ALU.add))
            V.scalar_tensor_tensor(out=heads(t32[:, 0:16]), in0=bv[:, :, 4:8], scalar=-1.0, in1=bv[:, :, 4:8],
                                   op0=ALU.mult, op1=ALU.max).then_inc(on["ba_in"], 1)
            for b in range(4):
                eng.wait_ge(acc_out[b], SLAB_O1)

            def halve_alibi():
                for h in range(2):
                    step(V.tensor_scalar(alibi[:, h], alibi[:, h], 0.25, None, ALU.mult))

            attention_on_vector(eng, MOBA, step, q_st, lambda c: PB[:, c], lambda h: alibi[:, h], None,
                                lambda c, h, t: Z1[:, t, bass.ds(c * P + h * DH, DH)], halve_alibi, 2)
            eng.wait_ge(on["sp_log"], 1)
            eng.wait_ge(on["ba_tanh"], 2)
            step(V.tensor_scalar(beta, beta, 0.5, 0.5, ALU.mult, ALU.add))
            step(V.scalar_tensor_tensor(out=heads(gcol), in0=bv[:, :, 4:8], scalar=0.0,
                                        in1=heads(t32[:, 16:32]), op0=ALU.max, op1=ALU.add))
            V.scalar_tensor_tensor(out=heads(gcol), in0=heads(gcol), scalar=-1.0,
                                   in1=nega.unsqueeze(1).to_broadcast([P, NT, HG]), op0=ALU.mult,
                                   op1=ALU.mult).then_inc(on["gate_sums"], 1)
            sums = ssq.rearrange("p (s t h) -> p s t h", s=2, h=HG)
            for n in range(8):
                eng.wait_ge(on["g_copy"] if n < 4 else on["g_square"], n + 1 if n < 4 else n - 3)
                V.tensor_reduce(sums[:, n // 4, :, n % 4], sq[:], AX, ALU.add).then_inc(on["g_reduced"], 1)
            eng.wait_ge(on["g_reduced"], 8)
            step(V.tensor_scalar(ssq, ssq, EPS, None, ALU.add))
            rsqrt(step, ssq, rkq, t32)
            rq, rk = rkq[:, 0:16], rkq[:, 16:32]
            step(V.tensor_tensor(c_bk, beta, rk, ALU.mult))
            step(V.tensor_scalar(c_rq, rq, DG ** -0.5, None, ALU.mult))
            eng.wait_ge(on["gate_exps"], 2)
            step(V.tensor_tensor(c_kbg, c_bk, eg, ALU.mult))
            step(V.tensor_copy(t32, acc[2][:, 0:32]))
            V.tensor_tensor(dl, t32[:, 16:32], t32[:, 0:16], ALU.subtract).then_inc(on["gate_done"], 1)
            eng.wait_ge(on["gate_exps"], 3)
            step(V.tensor_tensor(c_kdec, rk, dl, ALU.mult))
            step(V.memset(G["S"][:], 0.0))
            gc_col = t32[:, 0:16]
            eng.wait_ge(on["g_copy"], 12)
            for n in step.loop(NT, 25):
                four = bass.ts(n, HG)
                step(V.tensor_copy(G["KT"][:], tile_of(PB, 12, n)))
                step(V.tensor_tensor(G["TG"][:], each_head(const("tri")), spread(gcol[:, four], P), ALU.mult))
                V.tensor_tensor(G["IB"][:], each_head(ident), spread(c_bk[:, four], P),
                                ALU.mult).then_inc(on["tg_ready"], 1)
                step(V.tensor_tensor(G["KBG"][:], KM[:, :, n], spread(c_kbg[:, four], DG), ALU.mult))
                step(V.tensor_tensor(G["KDEC"][:], KM[:, :, n], spread(c_kdec[:, four], DG), ALU.mult))
                step(V.tensor_tensor(G["VB"][:], VM[:, :, n], spread(beta[:, four], DG), ALU.mult))
                eng.wait_ge(on["qk_ready"], n + 1)
                eng.wait_ge(on["e_ready"], n + 1)
                row_decay = aux[0][:].rearrange("p (h t) -> p h t", h=HG)
                step(V.tensor_tensor(G["DEC"][:], row_decay, spread(gc_col[:, four], P), ALU.subtract))
                V.tensor_tensor(G["DEC"][:], G["DEC"][:], each_head(const("future")),
                                ALU.add).then_inc(on["dec_in"], 1)
                step(V.tensor_tensor(G["QD"][:], tile_of(PB, 8, n), G["EG"][:], ALU.mult))
                eng.wait_ge(on["dec_ready"], n + 1)
                step(V.tensor_tensor(G["DEC"][:], G["DEC"][:], spread(rk[:, four], P), ALU.mult))
                step(V.tensor_tensor(G["INT"][:], as_heads(aux[3]), G["DEC"][:], ALU.mult))
                step(V.tensor_tensor(G["AT"][:], as_heads(aux[2]), G["DEC"][:], ALU.mult))
                step(V.tensor_tensor(G["AT"][:], as_heads(aux[1]), G["AT"][:], ALU.mult))
                step(V.tensor_tensor(G["MA"][:], G["AT"][:], each_head(const("level1")), ALU.mult))
                V.tensor_tensor(G["U"][:], each_head(ident), G["MA"][:], ALU.subtract).then_inc(on["u0"], 1)
                eng.wait_ge(on["t0_out"], n + 1)
                for m in range(6):
                    V.tensor_tensor(G["MA"][:], G["AT"][:], each_head(const(f"level{LEVELS[m + 1]}")),
                                    ALU.mult).then_inc(on["masked"], 1)
                    eng.wait_ge(on["tx_ready"], n * 6 + m + 1)
                    if m < 5:
                        step(V.tensor_tensor(G["TI"][:], G["TI"][:], as_heads(acc[2]), ALU.subtract))
                        step(V.tensor_tensor(G["U"][:], G["U"][:], as_heads(acc[3]), ALU.subtract))
                    else:
                        V.tensor_tensor(G["U"][:], G["U"][:], as_heads(acc[3]),
                                        ALU.subtract).then_inc(on["solved"], 1)
                eng.wait_ge(on["o_ready"], n + 1)
                step(V.tensor_tensor(G["S"][:], G["S"][:], spread(egl[:, four], DG), ALU.mult))
                step(V.tensor_tensor(G["S"][:], G["S"][:], as_heads(acc[3]), ALU.add))
                V.tensor_tensor(GO[:, n], as_heads(acc[2]), spread(c_rq[:, four], DG),
                                ALU.mult).then_inc(on["o_out"], 1)
                eng.wait_ge(on["o_square"], n + 1)
                step(V.tensor_reduce(go_ss[:, four], G["XS"][:], AX, ALU.add))
            step(V.tensor_scalar(go_ss, go_ss, 1.0 / DG, EPS, ALU.mult, ALU.add))
            rsqrt(step, go_ss, go_rs, t32[:, 0:16])
            for t in range(NT):
                step(V.tensor_tensor(GO[:, t], GO[:, t], spread(go_rs[:, t * HG:(t + 1) * HG], DG), ALU.mult))
                done = V.tensor_tensor(DZ[:, t], DZ[:, t], GO[:, t].rearrange("p h d -> p (h d)"), ALU.mult)
                if t < NT - 1:
                    step(done)
            done.then_inc(on["go_done"], 1)
            flip_lo_part(eng, ht_hi, ht_lo, KD, FLIP_MIXED, lambda k: param("gdn_norm") if k >= 4 else 1.0)
            eng.wait_ge(on["mixed_squares"], NT)
            eng.wait_ge(post_in, 16)
            row_norm(ss, NT, D)
            for t in range(NT):
                step(V.scalar_tensor_tensor(out=mixed[:, t], in0=mixed[:, t], scalar=rstd[:, t:t + 1],
                                            in1=post_w[:], op0=ALU.mult, op1=ALU.mult))
                V.tensor_tensor(X[:, t], X[:, t], mixed[:, t], ALU.add).then_inc(on["post_done"], 1)
            dve_second(eng, step)


def kernel(**inputs):
    import concourse.bacc as bacc
    from concourse.bass_utils import run_bass_kernel_spmd

    a = {k: np.asarray(v) for k, v in inputs.items()}
    w, w2 = a["w_in"][0], a["w_in_2"][0]
    q2 = w2[:, 2048:2560].reshape(D, 2, 4, DH).transpose(0, 2, 1, 3).reshape(D, NC)
    kv = w2[:, 2560:3328]
    gate = w2[:, 3352:5400]
    slabs = [w[:, 0:512], w[:, 512:1024], w[:, 2048:2560], w[:, 2560:3072], w[:, 3072:3584],
             w[:, 1024:1536], w[:, 1536:2048], w[:, 3584:4096]]
    slabs += [a["w_out"][0][:, n:n + NC] for n in (0, NC)]
    slabs += [w2[:, 0:512], w2[:, 512:1024], q2,
              np.concatenate([kv[:, 0:256], kv[:, 256:384], kv[:, 512:640]], axis=1)]
    slabs += [w2[:, 1024:1536], w2[:, 1536:2048],
              np.concatenate([kv[:, 384:512], kv[:, 640:768], w2[:, 3328:3352]], axis=1)]
    for s in range(2):
        cols = slice(s * NC, (s + 1) * NC)
        slabs += [gate[:, cols], a["w_br_a_2"][0][:, cols],
                  gate[:, D + s * NC:D + (s + 1) * NC], a["w_br_b_2"][0][:, cols]]
    slabs += [a["w_out_2"][0][:, n:n + NC] for n in (0, NC)]
    for f in range(FF_HALVES):
        half = slice(f * FF // 2, (f + 1) * FF // 2)
        slabs += [a["w_ff1_2"][0][:, half][:, i * NC:(i + 1) * NC] for i in range(FF1_SLABS)]
        slabs += [a["w_ff2_2"][0][half, n:n + NC] for n in (0, NC)]
    params = np.zeros((P, N_PARAM), np.float32)

    def put(name, value):
        p, q = PARAM_COLS[name]
        params[:, p:q] = value

    put("norm_pre", by_partition(a["norm_pre_w"][0]))
    put("norm1", by_partition(a["norm1_g_2"][0]))
    put("norm2", by_partition(a["norm2_g_2"][0]))
    put("conv", a["conv_w"][0].reshape(4, 12, P).transpose(2, 1, 0).reshape(P, 48))
    put("gdn_norm", a["gdn_norm_w"][0][:, None])
    put("hgrn_norm", a["hgrn_norm_g_2"][0][:, None])
    put("lb", np.concatenate([by_partition(a["lb_param_2"][0]), by_partition(a["lb_param_2"][1])], axis=1))
    put("a_log", a["a_log"][0][None, :])
    put("dt_bias", a["dt_bias"][0][None, :])
    pe = np.stack([a["cmp_pe_k_2"][0], a["cmp_pe_v_2"][0]]).reshape(2, 16, P).transpose(2, 0, 1)
    w1 = np.stack([a["cmp_w1_k_2"][0], a["cmp_w1_v_2"][0]]).reshape(2, 2, 8, P, 256).transpose(0, 1, 3, 2, 4)
    w2c = np.stack([a["cmp_w2_k_2"][0], a["cmp_w2_v_2"][0]]).reshape(2, 2, P, DH).transpose(2, 0, 1, 3)
    arrays = {
        "units": np.concatenate([slab_units(s) for s in slabs]),
        "consts": constant_table(),
        "params": params,
        "x": a["x"][0],
        "w_ba": w[:, 4096:4104].reshape(KD, P, 8).transpose(1, 0, 2).reshape(P, 8 * KD),
        "norm_post": np.broadcast_to(a["norm_post_w"][0], (P, D)),
        "final_g": np.broadcast_to(a["final_g_2"], (P, D)),
        "positions": np.broadcast_to(a["positions_2"][0], (P, T)),
        "pe_kv": pe.reshape(P, 32),
        "w1_kv": w1.reshape(2, 2, P, 8 * 256),
        "w2_kv": np.concatenate([w2c, w2c], axis=3).reshape(P, 4 * P),
    }
    arrays = {k: np.ascontiguousarray(v) for k, v in arrays.items()}
    nc = bacc.Bacc("TRN2", target_bir_lowering=False, num_devices=1)
    aps = {k: nc.dram_tensor(k, v.shape, mybir.dt.from_np(v.dtype), kind="ExternalInput").ap()
           for k, v in arrays.items()}
    result = nc.dram_tensor("result", (T, D), F32, kind="ExternalOutput").ap()
    two_blocks(nc, out=result, **aps)
    r = run_bass_kernel_spmd(nc, [arrays], core_ids=[0])
    return r.results[0]["result"].reshape(1, T, D)
```

```python
from contextlib import ExitStack

import numpy as np
import concourse.bass as bass
from concourse import mybir

F32 = mybir.dt.float32
F32R = mybir.dt.float32r
I32 = mybir.dt.int32
ALU = mybir.AluOpType
ACT = mybir.ActivationFunctionType
AX = mybir.AxisListType.X

P = 128
T = 512
NT = T // P
D = 1024
KD = D // P
NC = 512
EPS = 1e-6
BIG = 1e30

H1, DH = 8, 64
HG, DG = 4, 128
N_CMP, CMP_C = 31, 32
N_GATE = 24
FF = 4096
LEVELS = (1, 2, 4, 8, 16, 32, 64)
HG_CHUNK = 64

UPS = 4
D1_SLABS = 3
Q1_SLABS = 4
O1_SLABS = 2
B2_SLABS = 2
Q2_SLABS = 4
GATE_SLABS = 4
BR_UNITS = 8
O2_SLABS = 2
FF_HALVES, FF1_SLABS, FF2_UNITS = 2, 4, 8
U_D1 = 0
U_DZ = U_D1 + UPS * D1_SLABS
U_Q1 = U_DZ + UPS
U_O1 = U_Q1 + UPS * Q1_SLABS
U_B2 = U_O1 + UPS * O1_SLABS
U_AI = U_B2 + UPS * B2_SLABS
U_Q2 = U_AI + UPS
U_GATE = U_Q2 + UPS * Q2_SLABS
U_BR = U_GATE + UPS * GATE_SLABS
U_O2 = U_BR + BR_UNITS
U_FF = U_O2 + UPS * O2_SLABS
SLAB_D1 = 1
SLAB_DZ = SLAB_D1 + D1_SLABS
SLAB_Q1 = SLAB_DZ + 1
SLAB_O1 = SLAB_Q1 + Q1_SLABS
SLAB_B2 = SLAB_O1 + O1_SLABS
SLAB_AI = SLAB_B2 + B2_SLABS
SLAB_Q2 = SLAB_AI + 1
SLAB_GATE = SLAB_Q2 + Q2_SLABS
SLAB_BR = SLAB_GATE + GATE_SLABS
SLAB_O2 = SLAB_BR + 4
SLAB_FF = SLAB_O2 + O2_SLABS
SLABS_HALF = FF1_SLABS + 2
U_HALF = UPS * FF1_SLABS + 2 * FF2_UNITS
N_UNITS = U_FF + FF_HALVES * U_HALF
RING = 4
PARTS = 2

def _columns(parts):
    at, out = 0, {}
    for name, n in parts:
        out[name] = (at, at + n)
        at += n
    return out, at

CONST_COLS, N_CONST = _columns(
    [("ident", P), ("tri", P), ("ones", P), ("future", P), ("rope_swap", P)]
    + [(f"level{s}", P) for s in LEVELS]
    + [("alibi", T), ("causal", T), ("restart", T), ("cmp_hide", NT * CMP_C), ("cmp_keep", NT * CMP_C),
       ("inv_freq", 1)])
PARAM_COLS, N_PARAM = _columns(
    [("norm_pre", KD), ("norm1", KD), ("norm2", KD), ("conv", 48), ("gdn_norm", 1), ("hgrn_norm", 1),
     ("lb", 8), ("a_log", HG), ("dt_bias", HG)])


def constant_table():
    c = np.zeros((P, N_CONST), np.float32)

    def put(name, value):
        a, b = CONST_COLS[name]
        c[:, a:b] = value

    row, col = np.arange(P)[:, None], np.arange(P)[None, :]
    put("ident", row == col)
    put("tri", row <= col)
    put("ones", 1.0)
    put("future", np.where(col >= row, 0.0, -BIG))
    swap = np.zeros((P, P), np.float32)
    for g in (0, DH):
        for d in range(8):
            swap[g + d + 8, g + d] = -1.0
            swap[g + d, g + d + 8] = 1.0
    put("rope_swap", swap)
    for s in LEVELS:
        put(f"level{s}", (col // (2 * s) == row // (2 * s)) & (col // s % 2 == 1) & (row // s % 2 == 0))
    dist = row + (T - P) - np.arange(T)[None, :]
    put("alibi", np.where(dist >= 0, 0.5 * dist, BIG))
    put("causal", np.where(dist >= 0, 0.0, BIG))
    put("restart", np.arange(T)[None, :] % HG_CHUNK != 0)
    t = np.arange(NT)[None, :, None] * P + np.arange(P)[:, None, None]
    cc = np.arange(CMP_C)[None, None, :]
    seen = (16 * cc + 31 <= t) & (cc < N_CMP)
    put("cmp_hide", np.where(seen, 0.0, BIG).reshape(P, -1))
    put("cmp_keep", seen.reshape(P, -1))
    inv = (500000.0 ** (-np.arange(0, 16, 2) / 16)).astype(np.float32)
    d = np.arange(P) % DH
    put("inv_freq", np.where(d < 16, inv[d % 8], 0.0)[:, None])
    return c


def slab_units(w):
    k, n = w.shape
    w = np.pad(w, ((0, 0), (0, NC - n))) if n < NC else w
    return w.reshape(k // (2 * P), 2, P, NC).transpose(0, 2, 1, 3).reshape(-1, P, 2 * NC)


def by_partition(v):
    return v.reshape(-1, P).T


def two_blocks(nc, units, consts, params, x, w_ba, norm_post, final_g, positions, pe_kv, w1_kv, w2_kv, out):
    ctx = ExitStack()
    base = (nc.sbuf_base + 31) // 32 * 32
    KB = 1024

    def sb(name, shape, dtype, at):
        return nc.alloc_sbuf_tensor_at(name, shape, dtype, offset=base + int(at * KB))

    with ctx:
        def sem(name):
            return ctx.enter_context(nc.semaphore(name))

        C = sb("consts_sb", [P, N_CONST], F32, 0)
        PAR = sb("params_sb", [P, N_PARAM], F32, 14)
        SMALL = sb("small", [P, 384], F32, 14.5)
        raw = sb("w_raw", [P, RING, 2, NC], F32, 16)
        w_hi = sb("w_hi", [P, PARTS, 2, NC], F32R, 32)
        w_lo = sb("w_lo", [P, PARTS, 2, NC], F32R, 40)
        X = sb("residual", [P, NT, D], F32, 48)
        ht_hi = sb("ht_hi", [P, KD, T], F32R, 64)
        ht_lo = sb("ht_lo", [P, KD, T], F32R, 80)

        def const(name):
            a, b = CONST_COLS[name]
            return C[:, a:b]

        def param(name, k=0, n=1):
            a = PARAM_COLS[name][0] + k
            return PAR[:, a:a + n]

        ident = const("ident")

        PB = sb("feature_major", [P, 20, T], F32, 96)
        PA = sb("token_major", [P, 3, NT, NC], F32, 136)
        V1, Z1, DZ = PA[:, 0], PA[:, 1], PA[:, 2]
        xn = sb("normalized", [P, NT, D], F32, 160)
        wba = sb("w_ba_sb", [P, KD, 8], F32, 176)
        wba_hi = sb("w_ba_hi", [P, KD, P], F32R, 177)
        wba_lo = sb("w_ba_lo", [P, KD, P], F32R, 181)
        ba_row = sb("ba_row", [P, T], F32, 185)
        conv4 = sb("conv_sum", [P, 4, T], F32, 188)
        KM = sb("gdn_k_tok", [P, HG, NT, DG], F32, 160)
        VM = sb("gdn_v_tok", [P, HG, NT, DG], F32, 168)
        GO = sb("gdn_out", [P, NT, HG, DG], F32, 112)
        g_names = ("KT", "TG", "IB", "EG", "DEC", "AT", "INT", "QD", "KBG", "KDEC", "VB", "U", "TI", "S")
        G = {n: sb(f"gdn_{n}", [P, HG, DG], F32, 176 + 2 * i) for i, n in enumerate(g_names)}
        sq = sb("gdn_squares", [P, NT, DG], F32, 204)
        G["MA0"], G["MA1"], G["XS"], G["WN"], G["VN"] = G["TG"], G["IB"], G["EG"], G["DEC"], G["TG"]
        kz = sb("k_padded", [P, 4, 2, T], F32, 96)
        q_st1 = sb("q_staged", [P, 2, T], F32, 176)
        pr1 = sb("probs", [P, 4, T], F32, 180)
        pt1 = sb("probs_t", [P, 2, T], F32, 188)
        alibi = sb("alibi_bias", [P, 2, T], F32, 192)
        mixed = sb("mixed", [P, NT, D], F32, 96)
        post_w = sb("norm_post_sb", [P, D], F32, 196)

        acc = [nc.alloc_psum_tensor(f"acc{b}", [P, NC], F32) for b in range(4)]
        aux = [nc.alloc_psum_tensor(f"aux{b}", [P, NC], F32) for b in range(4)]

        consts_in = sem("consts_in")
        x_in = sem("x_in")
        wait_passed = sem("wait_passed")
        small_in = sem("small_in")
        raw_in = [sem(f"raw_in{j}") for j in range(RING)]
        hi_split = sem("hi_split")
        w_split = sem("w_split")
        unit_used = sem("unit_used")
        acc_ready = [sem(f"acc_ready{b}") for b in range(3)]
        acc_out = [sem(f"acc_out{b}") for b in range(4)]
        dve = sem("dve_step")
        flipped = sem("flipped")
        flip_hi = sem("flip_hi")
        flip_lo = sem("flip_lo")
        stored = sem("stored")

        class Steps:

            def __init__(self, eng, semaphore):
                self.eng, self.sem, self.at, self.made = eng, semaphore, 0, 0

            def __call__(self, instruction):
                self.at = self.at + 1
                self.made += 1
                instruction.then_inc(self.sem, 1)
                self.eng.wait_ge(self.sem, self.at)

            def loop(self, count, per):
                start = self.at
                with self.eng.Fori(0, count) as i:
                    self.at = i * per + start
                    before = self.made
                    yield i
                    assert self.made - before == per, (self.made - before, per)
                self.at = start + count * per

        def alone(eng):
            eng.sem_inc(wait_passed, 1)

        def split_product(pe, bank, first_operand, second_operand, start, stop):
            (ah, al), (bh, bl) = first_operand, second_operand
            nc.tensor.matmul(bank, ah, bh, start=start, stop=False)
            nc.tensor.matmul(bank, ah, bl, start=False, stop=False)
            return nc.tensor.matmul(bank, al, bh, start=False, stop=stop)

        def weight_piece(pe, unit, j, b, k0, hi, lo, slab, first, last, tokens_out):
            slot = j % PARTS
            if b == 0:
                pe.wait_ge(w_split, unit + 1)
            if first:
                pe.wait_ge(acc_out[b], slab)
            for kk in range(2):
                k = k0 + kk
                cols = slice(b * P, (b + 1) * P)
                if tokens_out:
                    w = (w_hi[:, slot, kk], w_lo[:, slot, kk])
                    a = (hi[:, k, cols], lo[:, k, cols])
                    done = split_product(pe, acc[b][:], a, w, first and kk == 0, last and kk == 1)
                else:
                    w = (w_hi[:, slot, kk, cols], w_lo[:, slot, kk, cols])
                    a = (hi[:, k], lo[:, k])
                    done = split_product(pe, acc[b][:], w, a, first and kk == 0, last and kk == 1)
            if b == 3:
                done.then_inc(unit_used, 1)
            elif last:
                done.then_inc(acc_ready[b], 1)

        def weight_slab(pe, unit, hi, lo, slab, tokens_out, units=UPS, operand=None, in_turn=False):
            together = units - 2 if in_turn else units
            order = [(j, b) for j in range(together) for b in range(4)]
            order += [(j, b) for b in range(4) for j in range(together, units)]
            for j, b in order:
                if operand is not None and b == 0:
                    pe.wait_ge(operand[0], operand[1] + (2 * j + 2))
                weight_piece(pe, unit + j, j, b, 2 * j, hi, lo, slab, j == 0, j == units - 1, tokens_out)

        def slab_in_pieces(pe, unit, hi, lo, slab, tokens_out):
            at = [0]

            def fill(n):
                for p in range(at[0], min(at[0] + n, 4 * UPS)):
                    j, b = divmod(p, 4)
                    weight_piece(pe, unit + j, j, b, 2 * j, hi, lo, slab, j == 0, j == UPS - 1, tokens_out)
                at[0] += n
            return fill

        def wait_bank(eng, b, slab, last_unit):
            if b < 3:
                eng.wait_ge(acc_ready[b], slab + 1)
            else:
                eng.wait_ge(unit_used, last_unit + 1)

        def flip_on_tensor(pe, source, chunks, count, tiles_ready):
            for k in range(chunks):
                n = count + k
                if n >= 4:
                    pe.wait_ge(flip_lo, n - 3)
                    pe.wait_ge(flip_hi, n - 3)
                for t in range(NT):
                    if k == 0 and tiles_ready is not None:
                        pe.wait_ge(tiles_ready, t + 1)
                    done = nc.tensor.transpose(aux[k % 4][:, t * P:(t + 1) * P], source(t, k), ident)
                done.then_inc(flipped, 1)

        def flip_hi_part(act, hi, chunks, count, weight):
            for k in range(chunks):
                act.wait_ge(flipped, count + k + 1)
                nc.scalar.activation(hi[:, k], aux[k % 4][:], ACT.Copy, scale=weight(k)).then_inc(flip_hi, 1)

        def flip_lo_part(eng, hi, lo, chunks, count, weight):
            for k in range(chunks):
                eng.wait_ge(flip_hi, count + k + 1)
                nc.vector.scalar_tensor_tensor(out=lo[:, k], in0=aux[k % 4][:], scalar=weight(k),
                                               in1=hi[:, k].bitcast(F32), op0=ALU.mult,
                                               op1=ALU.subtract).then_inc(flip_lo, 1)

        FLIP1, FLIP_MIXED = 0, KD
        FLIP2 = FLIP_MIXED + KD
        FLIP_A, FLIP_B = FLIP2 + KD, FLIP2 + KD + 4
        FLIP3 = FLIP_B + 4

        def rsqrt(step, v, y, t):
            step(nc.vector.tensor_scalar(y.bitcast(I32), v.bitcast(I32), -0.5, float(0x5f3759df),
                                         ALU.mult, ALU.add))
            for _ in range(3):
                step(nc.vector.scalar_tensor_tensor(out=t, in0=y, scalar=-0.5, in1=y,
                                                    op0=ALU.mult, op1=ALU.mult))
                step(nc.vector.tensor_tensor(t, t, v, ALU.mult))
                step(nc.vector.scalar_tensor_tensor(out=y, in0=t, scalar=1.5, in1=y,
                                                    op0=ALU.add, op1=ALU.mult))

        def small(a, n):
            return SMALL[:, a:a + n]
        ss, rstd, tmp4 = small(0, 4), small(4, 4), small(8, 4)
        beta, gcol, ba, rkq, ssq = small(16, 16), small(32, 16), small(48, 32), small(80, 32), small(112, 32)
        eg, egl, dl, c_bk = small(144, 16), small(160, 16), small(176, 16), small(192, 16)
        c_kbg, c_kdec, c_rq, rk_c = small(208, 16), small(224, 16), small(240, 16), small(256, 16)
        half_ss = small(340, 8)
        go_ss, go_rs, t32, nega = small(272, 16), small(288, 16), small(304, 32), small(336, 4)
        nmin, psum_, rs8 = small(0, 16), small(48, 16), small(80, 16)

        q_staged = sem("q_staged")
        scored = sem("scored")
        biased = sem("biased")
        probs = sem("probs_ready")
        probs_flipped = sem("probs_flipped")
        probs_out = sem("probs_out")
        weighed = sem("weighed")
        values_used = sem("values_used")
        STEPS = H1 * NT
        MOBA, SELECTED, WINDOW = 0, STEPS, 2 * STEPS

        class Banks:

            def __init__(self, scores, flips, values, q_st, pr, pt):
                self.scores, self.flips, self.values = scores, flips, values
                self.q_st, self.pr, self.pt, self.ring = q_st, pr, pt, len(scores)
                self.lag = max(1, self.ring - 2)

        BODY = 2 * 8

        def attention_on_tensor(pe, first, B, keys, values, filler):
            with pe.Fori(0, 2) as i:
                fill = filler(i)

                def scores(n):
                    if n >= BODY:
                        return
                    pair, (h, t) = n // 8, divmod(n % 8, NT)
                    if n % 8 == 0:
                        pe.wait_ge(q_staged, i * 2 + (first // 8 + pair + 1))
                    if n >= B.ring:
                        pe.wait_ge(biased, i * BODY + (first + n - B.ring + 1))
                    w = (t + 1) * P
                    nc.tensor.matmul(B.scores[n % B.ring][:, :w], B.q_st[:, pair, t * P:(t + 1) * P],
                                     keys(i, pair, h)[:, :w], start=True, stop=True).then_inc(scored, 1)

                def flip(n):
                    t = n % NT
                    pe.wait_ge(probs, i * BODY + (first + n + 1))
                    if n >= len(B.flips):
                        pe.wait_ge(probs_out, i * BODY + (first + n - len(B.flips) + 1))
                    for j in range(t + 1):
                        done = nc.tensor.transpose(B.flips[n % len(B.flips)][:, j * P:(j + 1) * P],
                                                   B.pr[:, n % B.ring, j * P:(j + 1) * P], ident)
                    done.then_inc(probs_flipped, 1)

                def weigh(n):
                    pair, (h, t) = n // 8, divmod(n % 8, NT)
                    pe.wait_ge(probs_out, i * BODY + (first + n + 1))
                    back = min(n, len(B.values) - 1)
                    pe.wait_ge(values_used, i * BODY + (first + n - back + 1))
                    for j in range(t + 1):
                        done = nc.tensor.matmul(B.values[n % len(B.values)][:, :DH],
                                                B.pt[:, n % 2, j * P:(j + 1) * P],
                                                values(i, pair, h, j), start=j == 0, stop=j == t)
                    done.then_inc(weighed, 1)

                for n in range(B.ring - 1):
                    scores(n)
                for n in range(BODY):
                    scores(n + B.ring - 1)
                    fill(1)
                    flip(n)
                    if n:
                        weigh(n - 1)
                weigh(BODY - 1)

        def attention_on_scalar(act, first, B, after_body):
            with act.Fori(0, 2) as i:
                def move(n):
                    w = (n % NT + 1) * P
                    act.wait_ge(probs_flipped, i * BODY + (first + n + 1))
                    nc.scalar.activation(B.pt[:, n % 2, :w], B.flips[n % len(B.flips)][:, :w],
                                         ACT.Copy).then_inc(probs_out, 1)

                for n in range(BODY + B.lag):
                    if n < BODY:
                        w = (n % NT + 1) * P
                        act.wait_ge(biased, i * BODY + (first + n + 1))
                        nc.scalar.activation(B.pr[:, n % B.ring, :w], B.pr[:, n % B.ring, :w], ACT.Exp,
                                             scale=-1.0, bias=nmin[:, n:n + 1],
                                             accum_out=psum_[:, n:n + 1]).then_inc(probs, 1)
                    if n >= B.lag:
                        move(n - B.lag)
                after_body(i)

        def attention_on_vector(eng, first, B, step, queries, bias, gate, result, after_pair, extra):
            for i in step.loop(2, (16 if gate is None else 32) + 2 * extra):
                for pair in range(2):
                    nc.vector.tensor_scalar(B.q_st[:, pair], queries(i, pair), -DH ** -0.5, None,
                                            ALU.mult).then_inc(q_staged, 1)

                def negate(n):
                    h, t = divmod(n % 8, NT)
                    w = (t + 1) * P
                    eng.wait_ge(scored, i * BODY + (first + n + 2))
                    if n >= B.ring:
                        eng.wait_ge(probs_flipped, i * BODY + (first + n - B.ring + 1))
                    alone(eng)
                    nc.vector.tensor_tensor_reduce(
                        out=B.pr[:, n % B.ring, :w], in0=B.scores[n % B.ring][:, :w], in1=bias(h)[:, T - w:],
                        scale=1.0, scalar=3.0e38, op0=ALU.add, op1=ALU.min,
                        accum_out=nmin[:, n:n + 1]).then_inc(biased, 1)

                def finish(n):
                    pair, (h, t) = n // 8, divmod(n % 8, NT)
                    eng.wait_ge(weighed, i * BODY + (first + n + 1))
                    step(nc.vector.reciprocal(rs8[:, n:n + 1], psum_[:, n:n + 1]))
                    op = ALU.mult
                    if gate is not None:
                        op = ALU.add
                        step(nc.vector.tensor_tensor(rs8[:, n:n + 1], rs8[:, n:n + 1], gate(i, pair, h, t),
                                                     ALU.mult))
                    nc.vector.scalar_tensor_tensor(out=result(i, pair, h, t),
                                                   in0=B.values[n % len(B.values)][:, :DH],
                                                   scalar=rs8[:, n:n + 1], in1=result(i, pair, h, t),
                                                   op0=ALU.mult, op1=op).then_inc(values_used, 1)

                for n in range(BODY + B.ring):
                    if n < BODY:
                        negate(n)
                        if n % 8 == 7:
                            after_pair(i, n // 8)
                    if n >= B.ring:
                        finish(n - B.ring)

        post_in = sem("post_in")
        names = ("x_squares normalized ba_split ba_product ba_row_out ba_flipped ba_tanh ba_in ba_exps "
                 "sp_log conv_done conv_silu k_padded g_flip g_copy g_square g_reduced gate_sums "
                 "gate_cols gate_exps gate_done tg_ready row_sums qk_ready e_ready dec_in dec_ready u0 "
                 "t0 t0_out masked merged x_ready x_out tx_ready solved wt_ready wn_out vn_ready vn_out "
                 "o_ready o_out o_square z_silu mixed_squares post_done go_done ").split()
        on = {n: sem(n) for n in names}

        def as_heads(bank):
            return bank[:].rearrange("p (h t) -> p h t", h=HG)


        def tile_of(buf, first, n):
            return buf[:, first:first + HG, bass.ts(n, P)]

        def heads(column):
            return column.rearrange("p (t h) -> p t h", h=HG)

        def spread(column, n):
            return column.unsqueeze(2).to_broadcast([P, HG, n])

        def each_head(table):
            return table.unsqueeze(1).to_broadcast([P, HG, table.shape[1]])

        moba_banks = Banks([aux[0], aux[1], acc[0], acc[1]], [aux[2], acc[2]], [aux[3], acc[3]], q_st1, pr1, pt1)

        PB2 = sb("feature_major_2", [P, 16, T], F32, 96)
        PA2 = sb("token_major_2", [P, 3, NT, NC], F32, 128)
        VH, AG, VSW = PA2[:, 0], PA2[:, 1], PA2[:, 2]
        YB = sb("y_b", [P, NT, NC], F32, 152)
        OA = sb("hgrn_out", [P, NT, HG, DG], F32, 152)
        hn = ("F", "LF", "KK", "B", "E", "EI", "ET", "QD", "KD", "KL", "QL", "KTM", "AM", "SS", "SQ")
        HB = {n: sb(f"hgrn_{n}", [P, T], F32, 160 + 2 * i) for i, n in enumerate(hn)}
        HB["KT"] = HB["F"]
        rope = sb("rope_tables", [P, 2, T], F32, 190)
        rope_t = sb("rope_temp", [P, 4, T], F32, 194)
        pos = sb("positions_sb", [P, T], I32, 202)
        kz2 = sb("k_padded_2", [P, 2, 2, T], F32, 160)
        kc2 = sb("cmp_tokens", [P, 2, 2, T], F32, 168)
        xc = sb("cmp_blocks", [P, 2, 2, 8, 2, CMP_C], F32, 176)
        w1 = sb("cmp_w1", [P, 2, 8, 256], F32, 96)
        w2 = sb("cmp_w2", [P, 2, 2, P], F32, 128)
        hid4 = sb("cmp_hidden_4", [P, 2, 2, 4, CMP_C], F32, 130)
        hid = sb("cmp_hidden", [P, 2, 2, 2, CMP_C], F32, 132)
        pe = sb("cmp_positions", [P, 2, 16], F32, 133)
        kcz = sb("cmp_keys", [P, 2, CMP_C], F32, 133.25)
        sg = sb("branch_gates", [P, NT, N_GATE], F32, 133.5)
        vcz = sb("cmp_values", [P, 2, 4, DH], F32, 134)
        lc = sb("cmp_logits", [P, 8, CMP_C], F32, 184)
        pc = sb("cmp_probs", [P, 8, CMP_C], F32, 185)
        pct = sb("cmp_probs_t", [P, 2, P], F32, 186)
        q_st2 = sb("q_staged_2", [P, 2, T], F32, 168)
        pr2 = sb("probs_2", [P, 2, T], F32, 172)
        pt2 = sb("probs_t_2", [P, 2, T], F32, 176)
        branch_banks = Banks([aux[0], aux[1]], [aux[2]], [aux[3]], q_st2, pr2, pt2)
        gate_a = sb("gate_tanh_a", [P, 8, T], F32, 96)
        gate_b = sb("gate_tanh_b", [P, 8, T], F32, 184)
        ya_hi, ya_lo = sb("ya_hi", [P, 4, T], F32R, 160), sb("ya_lo", [P, 4, T], F32R, 168)
        yb_hi, yb_lo = sb("yb_hi", [P, 4, T], F32R, 112), sb("yb_lo", [P, 4, T], F32R, 120)
        MM = sb("merged", [P, 4, T], F32, 176)
        mt_hi, mt_lo = sb("mt_hi", [P, KD, T], F32R, 128), sb("mt_lo", [P, KD, T], F32R, 144)
        TM = sb("merged_b", [P, 2, T], F32, 200)
        ff_hi, ff_lo = sb("ff_hi", [P, 16, T], F32R, 96), sb("ff_lo", [P, 16, T], F32R, 128)
        ff_r, ff_s = sb("ff_relu", [P, 4, T], F32, 176), sb("ff_square", [P, 4, T], F32, 184)
        fin_w = sb("final_sb", [P, D], F32, 192)

        c1, c2, dec, h_ss, h_rs = small(16, 4), small(20, 4), small(24, 4), small(32, 16), small(48, 16)
        mn8, sm8 = small(64, 8), small(72, 8)
        names2 = ("x2_squares normalized2 lb_in lb_tanh gate_th h_th h_f h_lf h_b h_exps h_tail h_et "
                 "h_kl h_ktflip h_ktm h_attn h_kv h_states h_o h_oa h_summed rot_ready rot_used roped "
                 "cmp_moved cmp_blocks hid_out hid4_ready cmp_kv cmp_z c_scores c_shift c_exp c_probs "
                 "c_flip c_flip_out c_values c_out gates_in sine m_merged mt_hi_s mt_lo_s x3_squares "
                 "normalized3 square_s ffhi_s fflo_s x4_squares final_s trig_in rope_done g_silu ").split()
        for n in names2:
            on[n] = sem(n)
        pos_in, fin_in, pe_in, w2_in = sem("pos_in"), sem("fin_in"), sem("pe_in"), sem("w2_in")
        w1_in = [sem(f"w1_in{j}") for j in range(2)]
        w1_used = sem("w1_used")
        CHUNKS = HG_CHUNK

        def chunked(buf):
            return buf[:].rearrange("p (t c s) -> p t c s", c=2, s=CHUNKS)

        ROPED = (8, 9, 10, 11, 12, 14, 15)

        def hgrn_head_on_tensor(pe, h, fill):
            fill(8)
            pe.wait_ge(on["h_kl"], h + 1)
            for t in range(NT):
                done = nc.tensor.transpose(aux[0][:, t * P:(t + 1) * P], HB["KL"][:, t * P:(t + 1) * P], ident)
            done.then_inc(on["h_ktflip"], 1)
            for t in range(NT):
                a, m, z = t * P, t * P + CHUNKS, (t + 1) * P
                nc.tensor.matmul(aux[1][0:CHUNKS, a:m], HB["KD"][:, a:m], HB["QD"][:, a:m], start=True, stop=True)
                nc.tensor.matmul(aux[1][0:CHUNKS, m:z], HB["KT"][:, a:m], HB["QD"][:, m:z], start=True, stop=True)
                done = nc.tensor.matmul(aux[1][CHUNKS:P, m:z], HB["KD"][:, m:z], HB["QD"][:, m:z],
                                        start=True, stop=True)
            done.then_inc(on["h_attn"], 1)
            fill(2)
            pe.wait_ge(on["h_ktm"], h + 1)
            for t in range(NT - 1):
                done = nc.tensor.matmul(aux[2][:, t * P:(t + 1) * P], HB["KTM"][:, t * P:(t + 1) * P],
                                        VH[:, t, bass.ts(h, P)], start=True, stop=True)
            done.then_inc(on["h_kv"], 1)
            fill(3)
            pe.wait_ge(on["h_states"], h + 1)
            for t in range(NT):
                o = aux[3][:, t * P:(t + 1) * P]
                done = nc.tensor.matmul(o, HB["AM"][:, t * P:(t + 1) * P], VH[:, t, bass.ts(h, P)],
                                        start=True, stop=t == 0)
                if t:
                    done = nc.tensor.matmul(o, HB["QL"][:, t * P:(t + 1) * P], HB["SS"][:, (t - 1) * P:t * P],
                                            start=False, stop=True)
            done.then_inc(on["h_o"], 1)
            fill(3)

        def pe_second(pe):
            flip_on_tensor(pe, lambda t, k: xn[:, t, k * P:(k + 1) * P], KD, FLIP2, on["normalized2"])
            with pe.Fori(0, B2_SLABS) as i:
                weight_slab(pe, i * UPS + U_B2, ht_hi, ht_lo, i + SLAB_B2, False, operand=(flip_lo, FLIP2))
            weight_slab(pe, U_AI, ht_hi, ht_lo, SLAB_AI, True)
            for b in range(4):
                pe.wait_ge(acc_out[b], SLAB_Q2)
            for by_token in (False, True):
                with pe.Fori(2 * by_token, 2 * by_token + 2) as h:
                    fill = slab_in_pieces(pe, h * UPS + U_Q2, ht_hi, ht_lo, h + SLAB_Q2, by_token)
                    hgrn_head_on_tensor(pe, h, fill)
            pe.wait_ge(on["rope_done"], 1)
            for n, ch in enumerate(ROPED):
                if n >= 2:
                    pe.wait_ge(on["rot_used"], n - 1)
                nc.tensor.matmul(aux[n % 2][:], const("rope_swap"), PB2[:, ch], start=True,
                                 stop=True).then_inc(on["rot_ready"], 1)
            for kv in range(2):
                pe.wait_ge(on["cmp_blocks"], kv + 1)
                if kv:
                    pe.wait_ge(on["hid_out"], 1)
                for ab in range(2):
                    n = 2 * kv + ab
                    pe.wait_ge(w1_in[ab], 16 * (kv + 1))
                    for hh in range(2):
                        for lp in range(8):
                            o = aux[2 + hh][:, 0:2 * CMP_C].rearrange("p (g c) -> p g c", g=2)[:, :, 0:N_CMP]
                            done = nc.tensor.matmul(o, w1[:, ab, lp, hh * P:(hh + 1) * P],
                                                    xc[:, kv, ab, lp, :, ab:ab + N_CMP],
                                                    start=ab == 0 and lp == 0, stop=ab == 1 and lp == 7)
                    done.then_inc(w1_used, 1)
            pe.wait_ge(on["hid_out"], 2)
            pe.wait_ge(w2_in, 16)
            for hh in range(2):
                done = nc.tensor.matmul(aux[0][:, 0:2 * CMP_C], w2[:, 0, hh], hid[:, 0, hh], start=hh == 0,
                                        stop=hh == 1)
            pe.wait_ge(on["hid4_ready"], 1)
            for g in range(2):
                for hh in range(2):
                    done = nc.tensor.matmul(aux[1][:, g * DH:(g + 1) * DH], hid4[:, hh, g], w2[:, 1, hh, 0:DH],
                                            start=hh == 0, stop=hh == 1)
            done.then_inc(on["cmp_kv"], 1)
            pe.wait_ge(on["cmp_z"], 1)
            for t in range(NT):
                for c in range(4):
                    o = aux[0][:, 0:256].rearrange("p (g c k) -> p c g k", g=2, c=4)[:, c]
                    done = nc.tensor.matmul(o, PB2[:, 8 + c, t * P:(t + 1) * P], kcz[:], start=True, stop=True)
                done.then_inc(on["c_scores"], 1)
                pe.wait_ge(on["c_probs"], t + 1)
                for g in range(2):
                    done = nc.tensor.transpose(aux[1][:, g * P:(g + 1) * P], pc[:, 4 * g:4 * g + 4], ident)
                done.then_inc(on["c_flip"], 1)
                pe.wait_ge(on["c_flip_out"], t + 1)
                if t:
                    pe.wait_ge(on["c_out"], t)
                for g in range(2):
                    done = nc.tensor.matmul(aux[2][:, g * 256:(g + 1) * 256], pct[:, g], vcz[:, g],
                                            start=True, stop=True)
                done.then_inc(on["c_values"], 1)
            pe.wait_ge(on["c_out"], NT)
            for first, s in ((SELECTED, 0), (WINDOW, 1)):
                attention_on_tensor(
                    pe, first, branch_banks, lambda i, pair, h: kz2[:, s, h],
                    lambda i, pair, h, j: VSW[:, j, s * P + h * DH:s * P + (h + 1) * DH],
                    lambda i: slab_in_pieces(pe, i * UPS + (U_GATE + 2 * UPS * s), ht_hi, ht_lo,
                                             i + (SLAB_GATE + 2 * s), False))
            pe.wait_ge(values_used, WINDOW + STEPS + 1)
            for b in range(4):
                pe.wait_ge(acc_out[b], SLAB_BR)
            flip_on_tensor(pe, lambda t, k: AG[:, t, k * P:(k + 1) * P], 4, FLIP_A, None)
            flip_on_tensor(pe, lambda t, k: YB[:, t, k * P:(k + 1) * P], 4, FLIP_B, None)
            with pe.Fori(0, 2) as s:
                for part, (hi, lo) in enumerate(((ya_hi, ya_lo), (yb_hi, yb_lo))):
                    weight_slab(pe, s * 4 + (U_BR + 2 * part), hi, lo, s * 2 + (SLAB_BR + part), False, units=2,
                                operand=(flip_lo, (FLIP_A, FLIP_B)[part]))
            for i in range(O2_SLABS):
                weight_slab(pe, i * UPS + U_O2, mt_hi, mt_lo, i + SLAB_O2, True, operand=(on["mt_lo_s"], 1),
                            in_turn=i == O2_SLABS - 1)
            flip_on_tensor(pe, lambda t, k: xn[:, t, k * P:(k + 1) * P], KD, FLIP3, on["normalized3"])
            with pe.Fori(0, FF_HALVES) as f:
                with pe.Fori(0, FF1_SLABS) as i:
                    weight_slab(pe, f * U_HALF + i * UPS + U_FF, ht_hi, ht_lo, f * SLABS_HALF + i + SLAB_FF, False,
                                operand=(flip_lo, FLIP3))
                with pe.Fori(0, 2) as n:
                    weight_slab(pe, f * U_HALF + n * FF2_UNITS + (U_FF + UPS * FF1_SLABS), ff_hi, ff_lo,
                                f * SLABS_HALF + n + (SLAB_FF + FF1_SLABS), True, units=FF2_UNITS,
                                operand=(on["fflo_s"], f * 16 + 1))

        def hgrn_head_on_scalar(act, h):
            act.wait_ge(on["h_summed"], h + 1)
            nc.scalar.activation(HB["F"][:], PB2[:, h + 4], ACT.Tanh, scale=0.5).then_inc(on["h_th"], 1)
            act.wait_ge(on["h_f"], h + 1)
            nc.scalar.activation(HB["LF"][:], HB["F"][:], ACT.Ln).then_inc(on["h_lf"], 1)
            act.wait_ge(on["h_b"], h + 1)
            nc.scalar.activation(HB["E"][:], HB["B"][:], ACT.Exp).then_inc(on["h_exps"], 1)
            nc.scalar.activation(HB["EI"][:], HB["B"][:], ACT.Exp, scale=-1.0).then_inc(on["h_exps"], 1)
            act.wait_ge(on["h_tail"], h + 1)
            nc.scalar.activation(HB["ET"][:], HB["ET"][:], ACT.Exp).then_inc(on["h_et"], 1)
            act.wait_ge(on["h_ktflip"], h + 1)
            nc.scalar.activation(HB["KTM"][:], aux[0][:], ACT.Copy).then_inc(on["h_ktm"], 1)
            act.wait_ge(on["h_o"], h + 1)
            nc.scalar.activation(OA[:, :, h], aux[3][:].rearrange("p (t d) -> p t d", t=NT),
                                 ACT.Copy).then_inc(on["h_oa"], 1)
            nc.scalar.activation(HB["SQ"][:], aux[3][:], ACT.Square).then_inc(on["h_oa"], 1)

        def act_second(act):
            for t in range(NT):
                act.wait_ge(on["post_done"], t + 1)
                nc.scalar.activation(xn[:, t], X[:, t], ACT.Square,
                                     accum_out=ss[:, t:t + 1]).then_inc(on["x2_squares"], 1)
            act.dma_start(pos[:], positions).then_inc(pos_in, 16)
            flip_hi_part(act, ht_hi, KD, FLIP2, lambda k: param("norm1", k))
            with act.Fori(0, B2_SLABS) as i:
                for b in range(4):
                    wait_bank(act, b, i + SLAB_B2, i * UPS + (U_B2 + UPS - 1))
                    nc.scalar.activation(PB2[:, i * 4 + b], acc[b][:], ACT.Copy).then_inc(acc_out[b], 1)
            for b in range(4):
                wait_bank(act, b, SLAB_AI, U_AI + UPS - 1)
                nc.scalar.activation(VH[:, b], acc[b][:], ACT.Copy).then_inc(acc_out[b], 1)
            act.wait_ge(on["trig_in"], 1)
            nc.scalar.activation(rope[:], rope[:], ACT.Sin).then_inc(on["sine"], 1)
            act.wait_ge(on["lb_in"], 1)
            nc.scalar.activation(c1, c1, ACT.Tanh, scale=0.5).then_inc(on["lb_tanh"], 1)
            for by_token in (False, True):
                with act.Fori(2 * by_token, 2 * by_token + 2) as h:
                    hgrn_head_on_scalar(act, h)
                    for b in range(4):
                        wait_bank(act, b, h + SLAB_Q2, h * UPS + (U_Q2 + UPS - 1))
                        target = PA2[:, h + -1, b] if by_token else PB2[:, h * 4 + (8 + b)]
                        nc.scalar.activation(target, acc[b][:], ACT.Copy).then_inc(acc_out[b], 1)
            for b in range(4):
                act.wait_ge(acc_out[b], SLAB_GATE)
            nc.scalar.activation(AG, AG, ACT.Silu).then_inc(on["g_silu"], 1)
            act.wait_ge(on["h_summed"], HG + 1)
            act.dma_start(pe[:].rearrange("p a b -> p (a b)"), pe_kv).then_inc(pe_in, 16)
            act.dma_start(w2[:].rearrange("p a b c -> p (a b c)"), w2_kv).then_inc(w2_in, 16)
            for ab in range(2):
                act.dma_start(w1[:, ab].rearrange("p a b -> p (a b)"), w1_kv[0, ab]).then_inc(w1_in[ab], 16)
            nc.scalar.activation(sg[:], VSW[:, :, 2 * P:2 * P + N_GATE], ACT.Tanh, scale=0.5)\
                .then_inc(on["gate_th"], 1)
            act.wait_ge(on["rope_done"], 2)
            for kv in range(2):
                for g in range(2):
                    src = PB2[g * DH:(g + 1) * DH, 12 + kv]
                    act.dma_start(kc2[0:DH, kv, g], src).then_inc(on["cmp_moved"], 16)
                    act.dma_start(kc2[DH:P, kv, g, 0:T - 1], src[:, 1:T]).then_inc(on["cmp_moved"], 16)
            for kv in range(2):
                if kv == 0:
                    for ab in range(2):
                        act.wait_ge(w1_used, ab + 1)
                        act.dma_start(w1[:, ab].rearrange("p a b -> p (a b)"), w1_kv[1, ab])\
                            .then_inc(w1_in[ab], 16)
                else:
                    act.wait_ge(w1_used, 4)
                for hh in range(2):
                    done = nc.scalar.activation(
                        hid[:, kv, hh, :, 0:N_CMP],
                        aux[2 + hh][:, 0:2 * CMP_C].rearrange("p (g c) -> p g c", g=2)[:, :, 0:N_CMP],
                        ACT.Gelu_apprx_tanh)
                done.then_inc(on["hid_out"], 1)
            for t in range(NT):
                act.wait_ge(on["c_shift"], t + 1)
                nc.scalar.activation(pc[:], lc[:], ACT.Exp).then_inc(on["c_exp"], 1)
                act.wait_ge(on["c_flip"], t + 1)
                nc.scalar.activation(pct[:].rearrange("p g q -> p (g q)"), aux[1][:, 0:2 * P],
                                     ACT.Copy).then_inc(on["c_flip_out"], 1)
                act.wait_ge(on["c_values"], t + 1)
                nc.scalar.activation(YB[:, t], aux[2][:], ACT.Copy).then_inc(on["c_out"], 1)
            for first, s, gate in ((SELECTED, 0, gate_a), (WINDOW, 1, gate_b)):
                def gates_out(i):
                    for b in range(4):
                        wait_bank(act, b, i + (SLAB_GATE + 2 * s), i * UPS + (U_GATE + 2 * UPS * s + UPS - 1))
                        alone(act)
                        nc.scalar.activation(gate[:, i * 4 + b], acc[b][:], ACT.Tanh,
                                             scale=0.5).then_inc(acc_out[b], 1)
                attention_on_scalar(act, first, branch_banks, gates_out)
            flip_hi_part(act, ya_hi, 4, FLIP_A, lambda k: param("hgrn_norm"))
            flip_hi_part(act, yb_hi, 4, FLIP_B, lambda k: 1.0)
            with act.Fori(0, 2) as s:
                for b in range(4):
                    act.wait_ge(on["m_merged"], s * 4 + (b + 1))
                    nc.scalar.activation(mt_hi[:, s * 4 + b], MM[:, b], ACT.Copy, scale=0.5)\
                        .then_inc(on["mt_hi_s"], 1)
            for t in range(NT):
                act.wait_ge(acc_out[t], SLAB_FF)
                nc.scalar.activation(xn[:, t], X[:, t], ACT.Square,
                                     accum_out=ss[:, t:t + 1]).then_inc(on["x3_squares"], 1)
            flip_hi_part(act, ht_hi, KD, FLIP3, lambda k: param("norm2", k))
            with act.Fori(0, FF_HALVES) as f:
                with act.Fori(0, FF1_SLABS) as i:
                    for b in range(4):
                        act.wait_ge(on["fflo_s"], f * 16 + i * 4 + 1)
                        wait_bank(act, b, f * SLABS_HALF + i + SLAB_FF, f * U_HALF + i * UPS + (U_FF + UPS - 1))
                        nc.scalar.activation(ff_r[:, b], acc[b][:], ACT.Relu).then_inc(acc_out[b], 1)
                    for b in range(4):
                        act.wait_ge(on["square_s"], f * 16 + i * 4 + (b + 1))
                        nc.scalar.activation(ff_hi[:, i * 4 + b], ff_s[:, b], ACT.Copy).then_inc(on["ffhi_s"], 1)
            act.dma_start(fin_w[:], final_g).then_inc(fin_in, 16)
            for t in range(NT):
                act.wait_ge(acc_out[t], SLAB_FF + FF_HALVES * SLABS_HALF)
                nc.scalar.activation(xn[:, t], X[:, t], ACT.Square,
                                     accum_out=ss[:, t:t + 1]).then_inc(on["x4_squares"], 1)

        TWO_PI_PARTS = (6.28125, 2029.0 / 2 ** 20, 2 * np.pi - 6.28125 - 2029.0 / 2 ** 20)
        ROUND = 1.5 * 2 ** 23

        def dve_second(eng, step):
            V = nc.vector

            def normalize(squares, target):
                eng.wait_ge(squares, NT)
                step(V.tensor_scalar(ss, ss, 1.0 / D, EPS, ALU.mult, ALU.add))
                rsqrt(step, ss, rstd, tmp4)
                for t in range(NT):
                    V.tensor_scalar(xn[:, t], X[:, t], rstd[:, t:t + 1], None, ALU.mult).then_inc(target, 1)

            def rotary_tables():
                eng.wait_ge(pos_in, 16)
                ang, turns = rope_t[:, 0], rope_t[:, 1]
                step(V.tensor_copy(turns, pos[:]))
                step(V.tensor_scalar(ang, turns, const("inv_freq"), None, ALU.mult))
                for s, quarter in ((0, 0.25), (1, 0.0)):
                    red = rope[:, s]
                    step(V.tensor_scalar(turns, ang, float(1 / (2 * np.pi)), quarter, ALU.mult, ALU.add))
                    step(V.tensor_scalar(turns, turns, ROUND, -ROUND, ALU.add, ALU.add))
                    step(V.scalar_tensor_tensor(out=red, in0=turns, scalar=-TWO_PI_PARTS[0], in1=ang,
                                                op0=ALU.mult, op1=ALU.add))
                    for part in TWO_PI_PARTS[1:]:
                        step(V.scalar_tensor_tensor(out=red, in0=turns, scalar=-float(part), in1=red,
                                                    op0=ALU.mult, op1=ALU.add))
                    if s == 0:
                        step(V.tensor_scalar(red, red, float(np.pi / 2), None, ALU.add))
                    done = V.tensor_scalar(red, red, 3.1415925, -3.1415925, ALU.min, ALU.max)
                    if s == 0:
                        step(done)
                done.then_inc(on["trig_in"], 1)

            normalize(on["x2_squares"], on["normalized2"])
            flip_lo_part(eng, ht_hi, ht_lo, KD, FLIP2, lambda k: param("norm1", k))
            rotary_tables()
            V.tensor_tensor(c1, param("lb", 0, 4), param("lb", 4, 4), ALU.subtract).then_inc(on["lb_in"], 1)
            eng.wait_ge(on["lb_tanh"], 1)
            step(V.tensor_scalar(c1, c1, 0.5, 0.5, ALU.mult, ALU.add))
            step(V.tensor_scalar(c2, c1, 0.5, 0.5, ALU.mult, ALU.add))
            step(V.tensor_scalar(c1, c1, -0.5, 0.5, ALU.mult, ALU.add))
            for b in range(4):
                eng.wait_ge(acc_out[b], SLAB_AI)
            step(V.memset(HB["AM"][:], 0.0))
            for h in step.loop(HG, 12):
                one = bass.ds(h, 1)
                eng.wait_ge(on["h_th"], h + 1)
                V.tensor_scalar(HB["F"][:], HB["F"][:], c1[:, one], c2[:, one], ALU.mult,
                                ALU.add).then_inc(on["h_f"], 1)
                eng.wait_ge(on["h_lf"], h + 1)
                step(V.tensor_scalar(HB["KK"][:], HB["F"][:], -1.0, 1.0, ALU.mult, ALU.add))
                V.tensor_tensor_scan(HB["B"][:], const("restart"), HB["LF"][:], 0.0, ALU.mult,
                                     ALU.add).then_inc(on["h_b"], 1)
                eng.wait_ge(on["h_b"], h + 1)
                b8 = HB["B"][:].rearrange("p (n s) -> p n s", s=CHUNKS)
                V.tensor_tensor(HB["ET"][:].rearrange("p (n s) -> p n s", s=CHUNKS),
                                b8[:, :, CHUNKS - 1:CHUNKS].to_broadcast([P, T // CHUNKS, CHUNKS]), b8,
                                ALU.subtract).then_inc(on["h_tail"], 1)
                eng.wait_ge(on["h_exps"], h * 2 + 2)
                step(V.tensor_tensor(HB["QD"][:], PB2[:, h], HB["E"][:], ALU.mult))
                step(V.tensor_tensor(HB["KD"][:], HB["KK"][:], HB["EI"][:], ALU.mult))
                eng.wait_ge(on["h_et"], h + 1)
                step(V.tensor_tensor(HB["KT"][:], HB["KK"][:], HB["ET"][:], ALU.mult))
                e4, kt4, kl4 = chunked(HB["E"]), chunked(HB["KT"]), chunked(HB["KL"])
                qd4, ql4 = chunked(HB["QD"]), chunked(HB["QL"])
                last = slice(CHUNKS - 1, CHUNKS)
                shape = [P, NT, CHUNKS]
                step(V.tensor_tensor(ql4[:, :, 1], qd4[:, :, 1], e4[:, :, 0, last].to_broadcast(shape), ALU.mult))
                step(V.tensor_copy(ql4[:, :, 0], qd4[:, :, 0]))
                step(V.tensor_tensor(dec.unsqueeze(2), e4[:, :, 0, last], e4[:, :, 1, last], ALU.mult))
                step(V.tensor_copy(kl4[:, :, 1], kt4[:, :, 1]))
                V.tensor_tensor(kl4[:, :, 0], kt4[:, :, 0], e4[:, :, 1, last].to_broadcast(shape),
                                ALU.mult).then_inc(on["h_kl"], 1)
                eng.wait_ge(on["h_attn"], h + 1)
                alone(eng)
                attn = aux[1][:].rearrange("p (t s) -> p t s", t=NT)
                am = HB["AM"][:].rearrange("p (t s) -> p t s", t=NT)
                mask = const("tri").bitcast(I32)
                step(V.copy_predicated(am[0:CHUNKS],
                                       mask[0:CHUNKS].unsqueeze(1).to_broadcast([CHUNKS, NT, P]), attn[0:CHUNKS]))
                alone(eng)
                step(V.copy_predicated(am[CHUNKS:P, :, CHUNKS:P],
                                       mask[CHUNKS:P, CHUNKS:P].unsqueeze(1).to_broadcast([CHUNKS, NT, CHUNKS]),
                                       attn[CHUNKS:P, :, CHUNKS:P]))
                eng.wait_ge(on["h_kv"], h + 1)
                step(V.tensor_copy(HB["SS"][:, 0:P], aux[2][:, 0:P]))
                step(V.scalar_tensor_tensor(out=HB["SS"][:, P:2 * P], in0=HB["SS"][:, 0:P], scalar=dec[:, 1:2],
                                            in1=aux[2][:, P:2 * P], op0=ALU.mult, op1=ALU.add))
                V.scalar_tensor_tensor(out=HB["SS"][:, 2 * P:3 * P], in0=HB["SS"][:, P:2 * P],
                                       scalar=dec[:, 2:3], in1=aux[2][:, 2 * P:3 * P], op0=ALU.mult,
                                       op1=ALU.add).then_inc(on["h_states"], 1)
                eng.wait_ge(on["h_oa"], h * 2 + 2)
                V.tensor_reduce(heads(h_ss)[:, :, one], HB["SQ"][:].rearrange("p (t d) -> p t d", t=NT),
                                AX, ALU.add).then_inc(on["h_summed"], 1)
            eng.wait_ge(on["h_summed"], HG + 1)
            step(V.tensor_scalar(h_ss, h_ss, 1.0 / DG, EPS, ALU.mult, ALU.add))
            rsqrt(step, h_ss, h_rs, t32[:, 0:16])
            eng.wait_ge(on["g_silu"], 1)
            for t in range(NT):
                step(V.tensor_tensor(OA[:, t], OA[:, t], spread(h_rs[:, t * HG:(t + 1) * HG], DG), ALU.mult))
                step(V.tensor_tensor(AG[:, t], AG[:, t], OA[:, t].rearrange("p h d -> p (h d)"), ALU.mult))
            step(V.memset(kz2[:], 0.0))
            eng.wait_ge(on["sine"], 1)
            V.memset(hid[:], 0.0).then_inc(on["rope_done"], 1)
            for n, ch in enumerate(ROPED):
                eng.wait_ge(on["rot_ready"], n + 1)
                turned = rope_t[:, n % 2]
                V.tensor_tensor(turned, aux[n % 2][:], rope[:, 1], ALU.mult).then_inc(on["rot_used"], 1)
                step(V.tensor_tensor(PB2[:, ch], PB2[:, ch], rope[:, 0], ALU.mult))
                eng.wait_ge(on["rot_used"], n + 1)
                if ch < 14:
                    V.tensor_tensor(PB2[:, ch], PB2[:, ch], turned, ALU.add).then_inc(on["roped"], 1)
                else:
                    for g in range(2):
                        rows = slice(g * DH, (g + 1) * DH)
                        step(V.tensor_tensor(kz2[rows, ch - 14, g], PB2[rows, ch], rope_t[rows, n % 2], ALU.add))
            eng.wait_ge(on["gate_th"], 1)
            V.tensor_scalar(sg[:], sg[:], 0.5, 0.5, ALU.mult, ALU.add).then_inc(on["gates_in"], 1)
            eng.wait_ge(on["roped"], 5)
            V.memset(kcz[:], 0.0).then_inc(on["rope_done"], 1)
            step(V.memset(vcz[:], 0.0))
            eng.wait_ge(pe_in, 16)
            eng.wait_ge(on["cmp_moved"], 16 * 8)
            for kv in range(2):
                tokens = kc2[:, kv].rearrange("p g (c l two) -> p l (g c) two", l=8, two=2)[:, :, :, 0]
                for ab in range(2):
                    done = V.tensor_tensor(
                        xc[:, kv, ab].rearrange("p l g c -> p l (g c)"), tokens,
                        pe[:, kv, 8 * ab:8 * ab + 8].unsqueeze(2).to_broadcast([P, 8, 2 * CMP_C]), ALU.add)
                    if ab == 0:
                        step(done)
                done.then_inc(on["cmp_blocks"], 1)
            eng.wait_ge(on["hid_out"], 2)
            for hh in range(2):
                done = V.tensor_copy(hid4[:, hh], hid[:, 1, hh].unsqueeze(2).to_broadcast([P, 2, 4, CMP_C]))
                if hh == 0:
                    step(done)
            done.then_inc(on["hid4_ready"], 1)
            eng.wait_ge(on["cmp_kv"], 1)
            for g in range(2):
                rows = slice(g * DH, (g + 1) * DH)
                step(V.tensor_copy(kcz[rows, g], aux[0][rows, g * CMP_C:(g + 1) * CMP_C]))
            for h in range(4):
                rows = slice(h * CMP_C, (h + 1) * CMP_C)
                done = V.tensor_copy(vcz[rows, :, h], aux[1][rows, 0:2 * DH].rearrange("p (g d) -> p g d", g=2))
                if h < 3:
                    step(done)
            done.then_inc(on["cmp_z"], 1)
            eng.wait_ge(on["gates_in"], 1)
            for t in range(NT):
                hide = each_of_8(const("cmp_hide")[:, t * CMP_C:(t + 1) * CMP_C])
                keep = each_of_8(const("cmp_keep")[:, t * CMP_C:(t + 1) * CMP_C])
                eng.wait_ge(on["c_scores"], t + 1)
                step(V.scalar_tensor_tensor(out=lc[:], in0=aux[0][:, 0:256].rearrange("p (h c) -> p h c", h=8),
                                            scalar=-DH ** -0.5, in1=hide, op0=ALU.mult, op1=ALU.add))
                step(V.tensor_reduce(mn8, lc[:], AX, ALU.min))
                V.tensor_tensor(lc[:], mn8.unsqueeze(2).to_broadcast([P, 8, CMP_C]), lc[:],
                                ALU.subtract).then_inc(on["c_shift"], 1)
                eng.wait_ge(on["c_exp"], t + 1)
                step(V.tensor_tensor(pc[:], pc[:], keep, ALU.mult))
                step(V.tensor_reduce(sm8, pc[:], AX, ALU.add))
                step(V.tensor_scalar(sm8, sm8, 1e-30, None, ALU.max))
                step(V.reciprocal(sm8, sm8))
                step(V.tensor_tensor(sm8, sm8, sg[:, t].rearrange("p (h b) -> p h b", b=3)[:, :, 0], ALU.mult))
                V.tensor_tensor(pc[:], pc[:], sm8.unsqueeze(2).to_broadcast([P, 8, CMP_C]),
                                ALU.mult).then_inc(on["c_probs"], 1)
            eng.wait_ge(on["c_out"], NT)
            for first, branch in ((SELECTED, 1), (WINDOW, 2)):
                eng.wait_ge(values_used, first + 1)
                attention_on_vector(
                    eng, first, branch_banks, step, lambda i, pair: PB2[:, i * 2 + (8 + pair)],
                    lambda h: const("causal"),
                    lambda i, pair, h, t: sg[:, t, bass.ds(i * 6 + (3 * pair + 12 * h + branch), 1)],
                    lambda i, pair, h, t: YB[:, t, bass.ds(i * 2 * DH + (pair * DH + 4 * DH * h), DH)],
                    lambda i, pair: None, 0)
            flip_lo_part(eng, ya_hi, ya_lo, 4, FLIP_A, lambda k: param("hgrn_norm"))
            flip_lo_part(eng, yb_hi, yb_lo, 4, FLIP_B, lambda k: 1.0)
            with eng.Fori(0, 2) as s:
                slab, unit = s * 2 + SLAB_BR, s * 4 + U_BR
                eng.wait_ge(on["mt_lo_s"], s * 4 + 1)
                for b in range(4):
                    wait_bank(eng, b, slab, unit + 1)
                    V.scalar_tensor_tensor(out=MM[:, b], in0=gate_a[:, s * 4 + b], scalar=1.0, in1=acc[b][:],
                                           op0=ALU.add, op1=ALU.mult).then_inc(acc_out[b], 1)
                for b in range(4):
                    wait_bank(eng, b, slab + 1, unit + 3)
                    V.scalar_tensor_tensor(out=TM[:, b % 2], in0=gate_b[:, s * 4 + b], scalar=1.0, in1=acc[b][:],
                                           op0=ALU.add, op1=ALU.mult).then_inc(acc_out[b], 1)
                    eng.wait_ge(acc_out[b], slab + 2)
                    V.tensor_tensor(MM[:, b], MM[:, b], TM[:, b % 2], ALU.add).then_inc(on["m_merged"], 1)
                    eng.wait_ge(on["mt_hi_s"], s * 4 + (b + 1))
                    V.scalar_tensor_tensor(out=mt_lo[:, s * 4 + b], in0=MM[:, b], scalar=0.5,
                                           in1=mt_hi[:, s * 4 + b].bitcast(F32), op0=ALU.mult,
                                           op1=ALU.subtract).then_inc(on["mt_lo_s"], 1)

            def add_to_residual(slab, last_unit, n):
                for b in range(4):
                    wait_bank(eng, b, slab, last_unit)
                    cols = X[:, b, bass.ts(n, NC)]
                    V.tensor_tensor(cols, cols, acc[b][:], ALU.add).then_inc(acc_out[b], 1)

            with eng.Fori(0, O2_SLABS) as i:
                add_to_residual(i + SLAB_O2, i * UPS + (U_O2 + UPS - 1), i)
            normalize(on["x3_squares"], on["normalized3"])
            flip_lo_part(eng, ht_hi, ht_lo, KD, FLIP3, lambda k: param("norm2", k))
            with eng.Fori(0, FF_HALVES) as f:
                with eng.Fori(0, FF1_SLABS) as i:
                    for b in range(4):
                        eng.wait_ge(acc_out[b], f * SLABS_HALF + i + (SLAB_FF + 1))
                        V.tensor_tensor(ff_s[:, b], ff_r[:, b], ff_r[:, b], ALU.mult).then_inc(on["square_s"], 1)
                    for b in range(4):
                        eng.wait_ge(on["ffhi_s"], f * 16 + i * 4 + (b + 1))
                        V.tensor_tensor(ff_lo[:, i * 4 + b], ff_s[:, b], ff_hi[:, i * 4 + b].bitcast(F32),
                                        ALU.subtract).then_inc(on["fflo_s"], 1)
                with eng.Fori(0, 2) as n:
                    add_to_residual(f * SLABS_HALF + n + (SLAB_FF + FF1_SLABS),
                                    f * U_HALF + n * FF2_UNITS + (U_FF + UPS * FF1_SLABS + FF2_UNITS - 1), n)
            eng.wait_ge(on["x4_squares"], NT)
            eng.wait_ge(fin_in, 16)
            step(V.tensor_scalar(ss, ss, 1.0 / D, EPS, ALU.mult, ALU.add))
            rsqrt(step, ss, rstd, tmp4)
            for t in range(NT):
                V.scalar_tensor_tensor(out=xn[:, t], in0=X[:, t], scalar=rstd[:, t:t + 1], in1=fin_w[:],
                                       op0=ALU.mult, op1=ALU.mult).then_inc(on["final_s"], 1)

        def sp_rest(sp):
            rows = out.rearrange("(t p) d -> p t d", p=P)
            for t in range(NT):
                sp.wait_ge(on["final_s"], t + 1)
                sp.dma_start(rows[:, t], xn[:, t]).then_inc(stored, 16)
            sp.wait_ge(stored, 16 * NT)

        def each_of_8(table):
            return table.unsqueeze(1).to_broadcast([P, 8, CMP_C])


        block = ctx.enter_context(nc.Block())

        @block.sync
        def _(sp):
            sp.dma_start(X[:], x.rearrange("(t p) d -> p t d", p=P)).then_inc(x_in, 16)
            sp.dma_start(C[:], consts).then_inc(consts_in, 16)
            sp.dma_start(PAR[:], params).then_inc(consts_in, 16)
            for j in range(RING):
                sp.dma_start(raw[:, j].rearrange("p k n -> p (k n)"), units[j]).then_inc(raw_in[j], 16)
            sp.dma_start(wba[:].rearrange("p k n -> p (k n)"), w_ba).then_inc(small_in, 16)
            with sp.Fori(1, N_UNITS // RING) as i:
                for j in range(RING):
                    sp.wait_ge(w_split, i * RING + (j - RING + 1))
                    sp.dma_start(raw[:, j].rearrange("p k n -> p (k n)"),
                                 units[i * RING + j]).then_inc(raw_in[j], 16)
            sp_rest(sp)

        @block.gpsimd
        def _(pool):
            one = const("ones")[:, 0:1].unsqueeze(2).to_broadcast([P, 2, NC])

            def split(unit, i, j, reused):
                pool.wait_ge(raw_in[j], i * 16 + 16)
                if reused:
                    pool.wait_ge(unit_used, unit - (PARTS - 1))
                    alone(pool)
                slot = j % PARTS
                nc.gpsimd.tensor_tensor(w_hi[:, slot], raw[:, j], one, ALU.mult).then_inc(hi_split, 1)
                pool.wait_ge(hi_split, unit + 1)
                nc.gpsimd.tensor_tensor(w_lo[:, slot], raw[:, j], w_hi[:, slot].bitcast(F32),
                                        ALU.subtract).then_inc(w_split, 1)

            pool.wait_ge(consts_in, 32)
            for j in range(RING):
                split(j, 0, j, j >= PARTS)
            with pool.Fori(1, N_UNITS // RING) as i:
                for j in range(RING):
                    split(i * RING + j, i, j, True)

        def delta_tile_on_tensor(pe, n, fill):
            def per_head(bank, left, right, start=True, stop=True):
                for h in range(HG):
                    done = nc.tensor.matmul(bank[:, h * P:(h + 1) * P], left(h), right(h), start=start, stop=stop)
                return done

            pe.wait_ge(on["tg_ready"], n + 1)
            nc.tensor.matmul(aux[0][:], const("ones"), G["TG"][:], start=True, stop=True)
            nc.tensor.matmul(aux[1][:], const("ones"), G["IB"][:], start=True, stop=True).then_inc(on["row_sums"], 1)
            per_head(aux[2], lambda h: G["KT"][:, h], lambda h: G["KT"][:, h])
            per_head(aux[3], lambda h: G["KT"][:, h],
                     lambda h: PB[:, h, bass.ts(n, P)]).then_inc(on["qk_ready"], 1)
            fill(4)
            pe.wait_ge(on["u0"], n + 1)
            for h in range(HG):
                done = nc.tensor.transpose(aux[0][:, h * P:(h + 1) * P], G["U"][:, h], ident)
            done.then_inc(on["t0"], 1)
            fill(1)
            pe.wait_ge(on["t0_out"], n + 1)
            for m in range(6):
                mask = G[f"MA{(m + 1) % 2}"]
                pe.wait_ge(on["masked"], n * 6 + m + 1)
                if m:
                    pe.wait_ge(on["merged"], n * 10 + 2 * m - 1)
                per_head(aux[1], lambda h: mask[:, h], lambda h: G["TI"][:, h]).then_inc(on["x_ready"], 1)
                fill(1)
                pe.wait_ge(on["x_out"], n * 6 + m + 1)
                if m:
                    pe.wait_ge(on["merged"], n * 10 + 2 * m)
                if m < 5:
                    per_head(aux[2], lambda h: G["U"][:, h], lambda h: G["XS"][:, h]).then_inc(on["tx_ready"], 1)
                per_head(aux[3], lambda h: G["XS"][:, h], lambda h: G["U"][:, h]).then_inc(on["tx_ready"], 1)
            pe.wait_ge(on["solved"], n + 1)
            per_head(aux[0], lambda h: G["KBG"][:, h], lambda h: G["U"][:, h]).then_inc(on["wt_ready"], 1)
            fill(2)
            pe.wait_ge(on["wn_out"], n + 1)
            for h in range(HG):
                nc.tensor.matmul(aux[1][:, h * P:(h + 1) * P], G["U"][:, h], G["VB"][:, h],
                                 start=True, stop=False)
                done = nc.tensor.matmul(aux[1][:, h * P:(h + 1) * P], G["WN"][:, h], G["S"][:, h],
                                        start=False, stop=True)
            done.then_inc(on["vn_ready"], 1)
            fill(3)
            pe.wait_ge(on["vn_out"], n + 1)
            for h in range(HG):
                nc.tensor.matmul(aux[2][:, h * P:(h + 1) * P], G["QD"][:, h], G["S"][:, h],
                                 start=True, stop=False)
                nc.tensor.matmul(aux[2][:, h * P:(h + 1) * P], G["INT"][:, h], G["VN"][:, h],
                                 start=False, stop=True)
            per_head(aux[3], lambda h: G["KDEC"][:, h], lambda h: G["VN"][:, h]).then_inc(on["o_ready"], 1)

        @block.tensor
        def _(pe):
            for count in (*acc_ready, scored):
                pe.sem_inc(count, 1)
            pe.wait_ge(consts_in, 32)
            flip_on_tensor(pe, lambda t, k: xn[:, t, k * P:(k + 1) * P], KD, FLIP1, on["normalized"])
            with pe.Fori(0, D1_SLABS) as i:
                weight_slab(pe, i * UPS + U_D1, ht_hi, ht_lo, i + SLAB_D1, False, operand=(flip_lo, FLIP1))
            pe.wait_ge(on["ba_split"], 2)
            for k in range(KD):
                done = split_product(pe, aux[2][:], (wba_hi[:, k], wba_lo[:, k]),
                                     (ht_hi[:, k], ht_lo[:, k]), k == 0, k == KD - 1)
            done.then_inc(on["ba_product"], 1)
            fill = slab_in_pieces(pe, U_DZ, ht_hi, ht_lo, SLAB_DZ, True)
            fill(2)
            pe.wait_ge(on["ba_row_out"], 1)
            for t in range(NT):
                done = nc.tensor.transpose(aux[3][:, t * 8:(t + 1) * 8], ba_row[0:8, t * P:(t + 1) * P],
                                           ident[0:8, 0:8])
            done.then_inc(on["ba_flipped"], 1)
            for n in range(12):
                fill(1)
                pe.wait_ge(on["conv_silu"], n + 2)
                if n >= 2:
                    pe.wait_ge(on["g_copy"], n - 1)
                for t in range(NT):
                    done = nc.tensor.transpose(aux[n % 2][:, t * P:(t + 1) * P],
                                               PB[:, n, t * P:(t + 1) * P], ident)
                done.then_inc(on["g_flip"], 1)
            pe.wait_ge(on["gate_sums"], 1)
            nc.tensor.matmul(aux[2][:, 0:16], const("tri"), gcol, start=True, stop=True)
            nc.tensor.matmul(aux[2][:, 16:32], const("ones"), gcol, start=True,
                             stop=True).then_inc(on["gate_cols"], 1)
            fill(2)
            for by_token in (False, True):
                with pe.Fori(2 * by_token, 2 * by_token + 2) as n:
                    fill = slab_in_pieces(pe, n * UPS + U_Q1, ht_hi, ht_lo, n + SLAB_Q1, by_token)
                    delta_tile_on_tensor(pe, n, fill)
            pe.wait_ge(on["k_padded"], 1)
            for b in range(4):
                pe.wait_ge(acc_out[b], SLAB_O1)
            attention_on_tensor(pe, MOBA, moba_banks, lambda i, pair, h: kz[:, i * 2 + pair, h],
                                lambda i, pair, h, j: V1[:, j, bass.ds(i * 2 * P + (pair * P + h * DH), DH)],
                                lambda i: lambda n: None)
            pe.wait_ge(on["go_done"], NT)
            pe.wait_ge(values_used, MOBA + STEPS + 1)
            flip_on_tensor(pe, lambda t, k: PA[:, 1 + k // 4, t, (k % 4) * P:(k % 4 + 1) * P], KD, FLIP_MIXED, None)
            for i in range(O1_SLABS):
                weight_slab(pe, i * UPS + U_O1, ht_hi, ht_lo, i + SLAB_O1, True, operand=(flip_lo, FLIP_MIXED),
                            in_turn=i == O1_SLABS - 1)
            pe_second(pe)

        def delta_tile_on_scalar(act, n):
            act.wait_ge(on["row_sums"], n + 1)
            nc.scalar.activation(G["EG"][:], aux[0][:], ACT.Exp).then_inc(on["e_ready"], 1)
            act.wait_ge(on["dec_in"], n + 1)
            nc.scalar.activation(G["DEC"][:], G["DEC"][:], ACT.Exp).then_inc(on["dec_ready"], 1)
            act.wait_ge(on["t0"], n + 1)
            nc.scalar.activation(G["TI"][:], aux[0][:], ACT.Copy).then_inc(on["t0_out"], 1)
            for m in range(6):
                act.wait_ge(on["x_ready"], n * 6 + m + 1)
                nc.scalar.activation(G["XS"][:], aux[1][:], ACT.Copy).then_inc(on["x_out"], 1)
            act.wait_ge(on["wt_ready"], n + 1)
            nc.scalar.activation(G["WN"][:], aux[0][:], ACT.Copy, scale=-1.0).then_inc(on["wn_out"], 1)
            act.wait_ge(on["vn_ready"], n + 1)
            nc.scalar.activation(G["VN"][:], aux[1][:], ACT.Copy).then_inc(on["vn_out"], 1)

        @block.scalar
        def _(act):
            for count in (*acc_out, on["conv_silu"]):
                act.sem_inc(count, 1)
            act.wait_ge(x_in, 16)
            for t in range(NT):
                nc.scalar.activation(xn[:, t], X[:, t], ACT.Square,
                                     accum_out=ss[:, t:t + 1]).then_inc(on["x_squares"], 1)
            act.wait_ge(consts_in, 32)
            flip_hi_part(act, ht_hi, KD, FLIP1, lambda k: param("norm_pre", k))
            with act.Fori(0, D1_SLABS) as i:
                for b in range(4):
                    wait_bank(act, b, i + SLAB_D1, i * UPS + (U_D1 + UPS - 1))
                    nc.scalar.activation(PB[:, i * 4 + b], acc[b][:], ACT.Copy).then_inc(acc_out[b], 1)
                for b in range(4):
                    act.wait_ge(on["conv_done"], i * 4 + (b + 1))
                    alone(act)
                    nc.scalar.activation(PB[:, i * 4 + b], conv4[:, b], ACT.Silu).then_inc(on["conv_silu"], 1)
            act.wait_ge(on["ba_product"], 1)
            nc.scalar.activation(ba_row[0:8], aux[2][0:8, :], ACT.Copy).then_inc(on["ba_row_out"], 1)
            act.wait_ge(on["ba_in"], 1)
            bv = ba.rearrange("p (t c) -> p t c", c=8)
            nc.scalar.activation(heads(beta), bv[:, :, 0:4], ACT.Tanh, scale=0.5).then_inc(on["ba_tanh"], 1)
            nc.scalar.activation(nega, param("a_log", 0, HG), ACT.Exp).then_inc(on["ba_tanh"], 1)
            nc.scalar.activation(t32[:, 0:16], t32[:, 0:16], ACT.Exp, scale=-1.0).then_inc(on["ba_exps"], 1)
            act.wait_ge(on["ba_exps"], 1)
            nc.scalar.activation(t32[:, 16:32], t32[:, 0:16], ACT.Ln, bias=1.0).then_inc(on["sp_log"], 1)
            for n in range(12):
                act.wait_ge(on["g_flip"], n + 1)
                if n < 8:
                    act.wait_ge(on["g_reduced"], n + 1)
                if n < 4:
                    nc.scalar.activation(sq[:], aux[n % 2][:], ACT.Square).then_inc(on["g_copy"], 1)
                elif n < 8:
                    nc.scalar.activation(sq[:], aux[n % 2][:], ACT.Square).then_inc(on["g_square"], 1)
                    nc.scalar.activation(KM[:, n - 4], aux[n % 2][:], ACT.Copy).then_inc(on["g_copy"], 1)
                else:
                    nc.scalar.activation(VM[:, n - 8], aux[n % 2][:], ACT.Copy).then_inc(on["g_copy"], 1)
            for b in range(4):
                wait_bank(act, b, SLAB_DZ, U_DZ + UPS - 1)
                nc.scalar.activation(DZ[:, b], acc[b][:], ACT.Silu).then_inc(acc_out[b], 1)
            act.wait_ge(on["gate_cols"], 1)
            nc.scalar.activation(eg, aux[2][:, 0:16], ACT.Exp).then_inc(on["gate_exps"], 1)
            nc.scalar.activation(egl, aux[2][:, 16:32], ACT.Exp).then_inc(on["gate_exps"], 1)
            act.wait_ge(on["gate_done"], 1)
            nc.scalar.activation(dl, dl, ACT.Exp).then_inc(on["gate_exps"], 1)
            for by_token in (False, True):
                with act.Fori(2 * by_token, 2 * by_token + 2) as n:
                    delta_tile_on_scalar(act, n)
                    for b in range(4):
                        wait_bank(act, b, n + SLAB_Q1, n * UPS + (U_Q1 + UPS - 1))
                        target = PA[:, n + -2, b] if by_token else PB[:, n * 4 + (12 + b)]
                        nc.scalar.activation(target, acc[b][:], ACT.Copy).then_inc(acc_out[b], 1)
                    act.wait_ge(on["o_out"], n + 1)
                    nc.scalar.activation(G["XS"][:], GO[:, n], ACT.Square).then_inc(on["o_square"], 1)
            for b in range(4):
                act.wait_ge(acc_out[b], SLAB_O1)
            nc.scalar.activation(Z1, Z1, ACT.Silu).then_inc(on["z_silu"], 1)
            act.wait_ge(on["o_out"], NT)
            act.dma_start(post_w[:], norm_post).then_inc(post_in, 16)
            attention_on_scalar(act, MOBA, moba_banks, lambda i: None)
            flip_hi_part(act, ht_hi, KD, FLIP_MIXED, lambda k: param("gdn_norm") if k >= 4 else 1.0)
            for n in range(O1_SLABS):
                for b in range(4):
                    wait_bank(act, b, n + SLAB_O1, n * UPS + (U_O1 + UPS - 1))
                    nc.scalar.activation(xn[:, b, n * NC:(n + 1) * NC], acc[b][:], ACT.Square,
                                         accum_out=half_ss[:, 4 * n + b:4 * n + b + 1])\
                        .then_inc(on["mixed_squares"], 1)
            act_second(act)

        @block.vector
        def _(eng):
            step = Steps(eng, dve)
            for count in (values_used, on["g_reduced"], on["h_summed"], on["mt_lo_s"], on["fflo_s"]):
                eng.sem_inc(count, 1)
            V = nc.vector

            def row_norm(squares, n, width):
                step(V.tensor_scalar(ss, ss, 1.0 / width, EPS, ALU.mult, ALU.add))
                rsqrt(step, ss, rstd, tmp4)

            eng.wait_ge(small_in, 16)
            step(V.memset(wba_hi[:].bitcast(F32), 0.0))
            step(V.memset(wba_lo[:].bitcast(F32), 0.0))
            V.tensor_copy(wba_hi[:, :, 0:8], wba[:]).then_inc(on["ba_split"], 1)
            eng.wait_ge(on["ba_split"], 1)
            V.tensor_tensor(wba_lo[:, :, 0:8], wba[:], wba_hi[:, :, 0:8].bitcast(F32),
                            ALU.subtract).then_inc(on["ba_split"], 1)
            eng.wait_ge(on["x_squares"], NT)
            row_norm(ss, NT, D)
            for t in range(NT):
                V.tensor_scalar(xn[:, t], X[:, t], rstd[:, t:t + 1], None, ALU.mult).then_inc(on["normalized"], 1)
            eng.wait_ge(consts_in, 32)
            flip_lo_part(eng, ht_hi, ht_lo, KD, FLIP1, lambda k: param("norm_pre", k))
            for i in step.loop(3, 12):
                eng.wait_ge(on["conv_silu"], i * 4 + 1)
                for b in range(4):
                    eng.wait_ge(acc_out[b], i + (SLAB_D1 + 1))
                    src = PB[:, i * 4 + b]
                    taps = PAR[:, bass.ds(i * 16 + (PARAM_COLS["conv"][0] + 4 * b), 4)]
                    step(V.tensor_scalar(conv4[:, b], src, taps[:, 3:4], None, ALU.mult))
                    for back in (1, 2):
                        step(V.scalar_tensor_tensor(out=conv4[:, b, back:], in0=src[:, :T - back],
                                                    scalar=taps[:, 3 - back:4 - back], in1=conv4[:, b, back:],
                                                    op0=ALU.mult, op1=ALU.add))
                    V.scalar_tensor_tensor(out=conv4[:, b, 3:], in0=src[:, :T - 3], scalar=taps[:, 0:1],
                                           in1=conv4[:, b, 3:], op0=ALU.mult,
                                           op1=ALU.add).then_inc(on["conv_done"], 1)
            eng.wait_ge(on["ba_flipped"], 1)
            bv = ba.rearrange("p (t c) -> p t c", c=8)
            step(V.tensor_copy(ba, aux[3][:, 0:32]))
            step(V.tensor_tensor(bv[:, :, 4:8], bv[:, :, 4:8],
                                 param("dt_bias", 0, HG).unsqueeze(1).to_broadcast([P, NT, HG]), ALU.add))
            V.scalar_tensor_tensor(out=heads(t32[:, 0:16]), in0=bv[:, :, 4:8], scalar=-1.0, in1=bv[:, :, 4:8],
                                   op0=ALU.mult, op1=ALU.max).then_inc(on["ba_in"], 1)
            eng.wait_ge(on["sp_log"], 1)
            eng.wait_ge(on["ba_tanh"], 2)
            step(V.tensor_scalar(beta, beta, 0.5, 0.5, ALU.mult, ALU.add))
            step(V.scalar_tensor_tensor(out=heads(gcol), in0=bv[:, :, 4:8], scalar=0.0,
                                        in1=heads(t32[:, 16:32]), op0=ALU.max, op1=ALU.add))
            V.scalar_tensor_tensor(out=heads(gcol), in0=heads(gcol), scalar=-1.0,
                                   in1=nega.unsqueeze(1).to_broadcast([P, NT, HG]), op0=ALU.mult,
                                   op1=ALU.mult).then_inc(on["gate_sums"], 1)
            sums = ssq.rearrange("p (s t h) -> p s t h", s=2, h=HG)
            for n in range(8):
                eng.wait_ge(on["g_copy"] if n < 4 else on["g_square"], n + 1 if n < 4 else n - 3)
                V.tensor_reduce(sums[:, n // 4, :, n % 4], sq[:], AX, ALU.add).then_inc(on["g_reduced"], 1)
            eng.wait_ge(on["g_reduced"], 9)
            step(V.tensor_scalar(ssq, ssq, EPS, None, ALU.add))
            rsqrt(step, ssq, rkq, t32)
            rq, rk = rkq[:, 0:16], rkq[:, 16:32]
            step(V.tensor_tensor(c_bk, beta, rk, ALU.mult))
            step(V.tensor_scalar(c_rq, rq, DG ** -0.5, None, ALU.mult))
            eng.wait_ge(on["gate_exps"], 2)
            step(V.tensor_tensor(c_kbg, c_bk, eg, ALU.mult))
            step(V.tensor_copy(t32, aux[2][:, 0:32]))
            V.tensor_tensor(dl, t32[:, 16:32], t32[:, 0:16], ALU.subtract).then_inc(on["gate_done"], 1)
            eng.wait_ge(on["gate_exps"], 3)
            step(V.tensor_tensor(c_kdec, rk, dl, ALU.mult))
            step(V.memset(G["S"][:], 0.0))
            gc_col = t32[:, 0:16]
            eng.wait_ge(on["g_copy"], 12)
            def delta_tile_on_vector(n, beside):
                four = bass.ts(n, HG)
                step(V.tensor_copy(G["KT"][:], tile_of(PB, 4, n)))
                step(V.tensor_tensor(G["TG"][:], each_head(const("tri")), spread(gcol[:, four], P), ALU.mult))
                V.tensor_tensor(G["IB"][:], each_head(ident), spread(c_bk[:, four], P),
                                ALU.mult).then_inc(on["tg_ready"], 1)
                step(V.tensor_tensor(G["KBG"][:], KM[:, :, n], spread(c_kbg[:, four], DG), ALU.mult))
                step(V.tensor_tensor(G["KDEC"][:], KM[:, :, n], spread(c_kdec[:, four], DG), ALU.mult))
                step(V.tensor_tensor(G["VB"][:], VM[:, :, n], spread(beta[:, four], DG), ALU.mult))
                eng.wait_ge(on["qk_ready"], n + 1)
                eng.wait_ge(on["e_ready"], n + 1)
                row_decay = aux[0][:].rearrange("p (h t) -> p h t", h=HG)
                step(V.tensor_tensor(G["DEC"][:], row_decay, spread(gc_col[:, four], P), ALU.subtract))
                V.tensor_tensor(G["DEC"][:], G["DEC"][:], each_head(const("future")),
                                ALU.add).then_inc(on["dec_in"], 1)
                step(V.tensor_tensor(G["QD"][:], tile_of(PB, 0, n), G["EG"][:], ALU.mult))
                eng.wait_ge(on["dec_ready"], n + 1)
                step(V.tensor_tensor(G["DEC"][:], G["DEC"][:], spread(rk[:, four], P), ALU.mult))
                step(V.tensor_tensor(G["INT"][:], as_heads(aux[3]), G["DEC"][:], ALU.mult))
                step(V.tensor_tensor(G["AT"][:], as_heads(aux[2]), G["DEC"][:], ALU.mult))
                step(V.tensor_tensor(G["AT"][:], as_heads(aux[1]), G["AT"][:], ALU.mult))
                step(V.tensor_tensor(G["MA0"][:], G["AT"][:], each_head(const("level1")), ALU.mult))
                V.tensor_tensor(G["U"][:], each_head(ident), G["MA0"][:], ALU.subtract).then_inc(on["u0"], 1)

                def mask_level(m):
                    V.tensor_tensor(G[f"MA{(m + 1) % 2}"][:], G["AT"][:], each_head(const(f"level{LEVELS[m + 1]}")),
                                    ALU.mult).then_inc(on["masked"], 1)

                mask_level(0)
                eng.wait_ge(on["u0"], n + 1)
                mask_level(1)
                eng.wait_ge(on["t0_out"], n + 1)
                for m in range(5):
                    eng.wait_ge(on["tx_ready"], n * 11 + 2 * m + 1)
                    V.tensor_tensor(G["TI"][:], G["TI"][:], as_heads(aux[2]), ALU.subtract).then_inc(on["merged"], 1)
                    eng.wait_ge(on["tx_ready"], n * 11 + 2 * m + 2)
                    V.tensor_tensor(G["U"][:], G["U"][:], as_heads(aux[3]), ALU.subtract).then_inc(on["merged"], 1)
                    if m < 4:
                        mask_level(m + 2)
                    beside(m)
                eng.wait_ge(on["tx_ready"], n * 11 + 11)
                V.tensor_tensor(G["U"][:], G["U"][:], as_heads(aux[3]), ALU.subtract).then_inc(on["solved"], 1)
                eng.wait_ge(on["o_ready"], n + 1)
                step(V.tensor_tensor(G["S"][:], G["S"][:], spread(egl[:, four], DG), ALU.mult))
                step(V.tensor_tensor(G["S"][:], G["S"][:], as_heads(aux[3]), ALU.add))
                V.tensor_tensor(GO[:, n], as_heads(aux[2]), spread(c_rq[:, four], DG),
                                ALU.mult).then_inc(on["o_out"], 1)
                eng.wait_ge(on["o_square"], n + 1)
                step(V.tensor_reduce(go_ss[:, four], G["XS"][:], AX, ALU.add))

            def pad_keys(m):
                if m < 4:
                    step(V.memset(kz[:, m], 0.0))
                    for h in range(2):
                        step(V.tensor_copy(kz[h * DH:(h + 1) * DH, m, h], PB[h * DH:(h + 1) * DH, 16 + m]))

            for n in step.loop(NT - 1, 15):
                delta_tile_on_vector(n, lambda m: None)
            for b in range(4):
                eng.wait_ge(acc_out[b], SLAB_Q1 + 2)
            delta_tile_on_vector(NT - 1, pad_keys)
            step(V.tensor_copy(alibi[:, 0], const("alibi")))
            V.tensor_scalar(alibi[:, 1], const("alibi"), 0.5, None, ALU.mult).then_inc(on["k_padded"], 1)
            step(V.tensor_scalar(go_ss, go_ss, 1.0 / DG, EPS, ALU.mult, ALU.add))
            rsqrt(step, go_ss, go_rs, t32[:, 0:16])
            eng.wait_ge(on["k_padded"], 1)
            eng.wait_ge(on["z_silu"], 1)

            def after_pair(i, pair):
                for h in range(2):
                    step(V.tensor_scalar(alibi[:, h], alibi[:, h], 0.25, None, ALU.mult))
                t = i * 2 + pair
                step(V.tensor_tensor(GO[:, t], GO[:, t], spread(go_rs[:, bass.ts(t, HG)], DG), ALU.mult))
                V.tensor_tensor(DZ[:, t], DZ[:, t], GO[:, t].rearrange("p h d -> p (h d)"),
                                ALU.mult).then_inc(on["go_done"], 1)

            attention_on_vector(eng, MOBA, moba_banks, step, lambda i, pair: PB[:, i * 2 + (12 + pair)],
                                lambda h: alibi[:, h], None,
                                lambda i, pair, h, t: Z1[:, t, bass.ds(i * 2 * P + (pair * P + h * DH), DH)],
                                after_pair, 3)
            flip_lo_part(eng, ht_hi, ht_lo, KD, FLIP_MIXED, lambda k: param("gdn_norm") if k >= 4 else 1.0)
            eng.wait_ge(post_in, 16)
            for n in range(O1_SLABS):
                cols = slice(n * NC, (n + 1) * NC)
                for b in range(4):
                    eng.wait_ge(on["mixed_squares"], 4 * n + b + 1)
                    V.tensor_tensor(mixed[:, b, cols], acc[b][:], post_w[:, cols], ALU.mult)\
                        .then_inc(acc_out[b], 1)
            step(V.tensor_tensor(ss, half_ss[:, 0:4], half_ss[:, 4:8], ALU.add))
            row_norm(ss, NT, D)
            for t in range(NT):
                eng.wait_ge(acc_out[t], SLAB_B2)
                V.scalar_tensor_tensor(out=X[:, t], in0=mixed[:, t], scalar=rstd[:, t:t + 1], in1=X[:, t],
                                       op0=ALU.mult, op1=ALU.add).then_inc(on["post_done"], 1)
            dve_second(eng, step)


def kernel(**inputs):
    import concourse.bacc as bacc
    from concourse.bass_utils import run_bass_kernel_spmd

    a = {k: np.asarray(v) for k, v in inputs.items()}
    w, w2 = a["w_in"][0], a["w_in_2"][0]
    q2 = w2[:, 2048:2560].reshape(D, 2, 4, DH).transpose(0, 2, 1, 3).reshape(D, NC)
    kv = w2[:, 2560:3328]
    gate = w2[:, 3352:5400]
    at = lambda m, *starts: [m[:, c:c + NC] for c in starts]
    slabs = at(w, 2048, 2560, 3072, 3584, 0, 512, 1024, 1536)
    slabs += at(a["w_out"][0], 0, NC)
    slabs += at(w2, 0, 512, 1024)
    slabs += [q2, np.concatenate([kv[:, 0:256], kv[:, 256:384], kv[:, 512:640]], axis=1), w2[:, 1536:2048],
              np.concatenate([kv[:, 384:512], kv[:, 640:768], w2[:, 3328:3352]], axis=1)]
    slabs += at(gate, 0, NC, D, D + NC)
    for s in range(2):
        slabs += at(a["w_br_a_2"][0], s * NC) + at(a["w_br_b_2"][0], s * NC)
    slabs += [a["w_out_2"][0][:, n:n + NC] for n in (0, NC)]
    for f in range(FF_HALVES):
        half = slice(f * FF // 2, (f + 1) * FF // 2)
        slabs += [a["w_ff1_2"][0][:, half][:, i * NC:(i + 1) * NC] for i in range(FF1_SLABS)]
        slabs += [a["w_ff2_2"][0][half, n:n + NC] for n in (0, NC)]
    params = np.zeros((P, N_PARAM), np.float32)

    def put(name, value):
        p, q = PARAM_COLS[name]
        params[:, p:q] = value

    put("norm_pre", by_partition(a["norm_pre_w"][0]))
    put("norm1", by_partition(a["norm1_g_2"][0]))
    put("norm2", by_partition(a["norm2_g_2"][0]))
    put("conv", a["conv_w"][0].reshape(4, 12, P).transpose(2, 1, 0).reshape(P, 48))
    put("gdn_norm", a["gdn_norm_w"][0][:, None])
    put("hgrn_norm", a["hgrn_norm_g_2"][0][:, None])
    put("lb", np.concatenate([by_partition(a["lb_param_2"][0]), by_partition(a["lb_param_2"][1])], axis=1))
    put("a_log", a["a_log"][0][None, :])
    put("dt_bias", a["dt_bias"][0][None, :])
    pe = np.stack([a["cmp_pe_k_2"][0], a["cmp_pe_v_2"][0]]).reshape(2, 16, P).transpose(2, 0, 1)
    w1 = np.stack([a["cmp_w1_k_2"][0], a["cmp_w1_v_2"][0]]).reshape(2, 2, 8, P, 256).transpose(0, 1, 3, 2, 4)
    w2c = np.stack([a["cmp_w2_k_2"][0], a["cmp_w2_v_2"][0]]).reshape(2, 2, P, DH).transpose(2, 0, 1, 3)
    arrays = {
        "units": np.concatenate([slab_units(s) for s in slabs]),
        "consts": constant_table(),
        "params": params,
        "x": a["x"][0],
        "w_ba": w[:, 4096:4104].reshape(KD, P, 8).transpose(1, 0, 2).reshape(P, 8 * KD),
        "norm_post": np.broadcast_to(a["norm_post_w"][0], (P, D)),
        "final_g": np.broadcast_to(a["final_g_2"], (P, D)),
        "positions": np.broadcast_to(a["positions_2"][0], (P, T)),
        "pe_kv": pe.reshape(P, 32),
        "w1_kv": w1.reshape(2, 2, P, 8 * 256),
        "w2_kv": np.concatenate([w2c, w2c], axis=3).reshape(P, 4 * P),
    }
    arrays = {k: np.ascontiguousarray(v) for k, v in arrays.items()}
    nc = bacc.Bacc("TRN2", target_bir_lowering=False, num_devices=1)
    aps = {k: nc.dram_tensor(k, v.shape, mybir.dt.from_np(v.dtype), kind="ExternalInput").ap()
           for k, v in arrays.items()}
    result = nc.dram_tensor("result", (T, D), F32, kind="ExternalOutput").ap()
    two_blocks(nc, out=result, **aps)
    r = run_bass_kernel_spmd(nc, [arrays], core_ids=[0])
    return r.results[0]["result"].reshape(1, T, D)
```

```python
from contextlib import ExitStack

import numpy as np
import concourse.bass as bass
from concourse import mybir

F32 = mybir.dt.float32
F32R = mybir.dt.float32r
I32 = mybir.dt.int32
ALU = mybir.AluOpType
ACT = mybir.ActivationFunctionType
AX = mybir.AxisListType.X

P = 128
T = 512
NT = T // P
D = 1024
KD = D // P
NC = 512
EPS = 1e-6
BIG = 1e30

H1, DH = 8, 64
HG, DG = 4, 128
N_CMP, CMP_C = 31, 32
N_GATE = 24
FF = 4096
LEVELS = (1, 2, 4, 8, 16, 32, 64)
HG_CHUNK = 64

UPS = 4
D1_SLABS = 3
Q1_SLABS = 4
O1_SLABS = 2
B2_SLABS = 2
Q2_SLABS = 4
GATE_SLABS = 4
BR_UNITS = 8
O2_SLABS = 2
FF_HALVES, FF1_SLABS, FF2_UNITS = 2, 4, 8
U_D1 = 0
U_DZ = U_D1 + UPS * D1_SLABS
U_Q1 = U_DZ + UPS
U_O1 = U_Q1 + UPS * Q1_SLABS
U_B2 = U_O1 + UPS * O1_SLABS
U_AI = U_B2 + UPS * B2_SLABS
U_Q2 = U_AI + UPS
U_GATE = U_Q2 + UPS * Q2_SLABS
U_BR = U_GATE + UPS * GATE_SLABS
U_O2 = U_BR + BR_UNITS
U_FF = U_O2 + UPS * O2_SLABS
SLAB_D1 = 1
SLAB_DZ = SLAB_D1 + D1_SLABS
SLAB_Q1 = SLAB_DZ + 1
SLAB_O1 = SLAB_Q1 + Q1_SLABS
SLAB_B2 = SLAB_O1 + O1_SLABS
SLAB_AI = SLAB_B2 + B2_SLABS
SLAB_Q2 = SLAB_AI + 1
SLAB_GATE = SLAB_Q2 + Q2_SLABS
SLAB_BR = SLAB_GATE + GATE_SLABS
SLAB_O2 = SLAB_BR + 4
SLAB_FF = SLAB_O2 + O2_SLABS
SLABS_HALF = FF1_SLABS + 2
U_HALF = UPS * FF1_SLABS + 2 * FF2_UNITS
N_UNITS = U_FF + FF_HALVES * U_HALF
RING = 4
PARTS = 2

def _columns(parts):
    at, out = 0, {}
    for name, n in parts:
        out[name] = (at, at + n)
        at += n
    return out, at

CONST_COLS, N_CONST = _columns(
    [("ident", P), ("tri", P), ("ones", P), ("future", P), ("rope_swap", P)]
    + [(f"level{s}", P) for s in LEVELS]
    + [("alibi", T), ("causal", T), ("restart", T), ("cmp_hide", NT * CMP_C), ("cmp_keep", NT * CMP_C),
       ("inv_freq", 1)])
PARAM_COLS, N_PARAM = _columns(
    [("norm_pre", KD), ("norm1", KD), ("norm2", KD), ("conv", 48), ("gdn_norm", 1), ("hgrn_norm", 1),
     ("lb", 8), ("a_log", HG), ("dt_bias", HG)])


def constant_table():
    c = np.zeros((P, N_CONST), np.float32)

    def put(name, value):
        a, b = CONST_COLS[name]
        c[:, a:b] = value

    row, col = np.arange(P)[:, None], np.arange(P)[None, :]
    put("ident", row == col)
    put("tri", row <= col)
    put("ones", 1.0)
    put("future", np.where(col >= row, 0.0, -BIG))
    swap = np.zeros((P, P), np.float32)
    for g in (0, DH):
        for d in range(8):
            swap[g + d + 8, g + d] = -1.0
            swap[g + d, g + d + 8] = 1.0
    put("rope_swap", swap)
    for s in LEVELS:
        put(f"level{s}", (col // (2 * s) == row // (2 * s)) & (col // s % 2 == 1) & (row // s % 2 == 0))
    dist = row + (T - P) - np.arange(T)[None, :]
    put("alibi", np.where(dist >= 0, 0.5 * dist, BIG))
    put("causal", np.where(dist >= 0, 0.0, BIG))
    put("restart", np.arange(T)[None, :] % HG_CHUNK != 0)
    t = np.arange(NT)[None, :, None] * P + np.arange(P)[:, None, None]
    cc = np.arange(CMP_C)[None, None, :]
    seen = (16 * cc + 31 <= t) & (cc < N_CMP)
    put("cmp_hide", np.where(seen, 0.0, BIG).reshape(P, -1))
    put("cmp_keep", seen.reshape(P, -1))
    inv = (500000.0 ** (-np.arange(0, 16, 2) / 16)).astype(np.float32)
    d = np.arange(P) % DH
    put("inv_freq", np.where(d < 16, inv[d % 8], 0.0)[:, None])
    return c


def slab_units(w):
    k, n = w.shape
    w = np.pad(w, ((0, 0), (0, NC - n))) if n < NC else w
    return w.reshape(k // (2 * P), 2, P, NC).transpose(0, 2, 1, 3).reshape(-1, P, 2 * NC)


def by_partition(v):
    return v.reshape(-1, P).T


def two_blocks(nc, units, consts, params, x, w_ba, norm_post, final_g, positions, pe_kv, w1_kv, w2_kv, out):
    ctx = ExitStack()
    base = (nc.sbuf_base + 31) // 32 * 32
    KB = 1024

    def sb(name, shape, dtype, at):
        return nc.alloc_sbuf_tensor_at(name, shape, dtype, offset=base + int(at * KB))

    with ctx:
        def sem(name):
            return ctx.enter_context(nc.semaphore(name))

        C = sb("consts_sb", [P, N_CONST], F32, 0)
        PAR = sb("params_sb", [P, N_PARAM], F32, 14)
        SMALL = sb("small", [P, 384], F32, 14.5)
        raw = sb("w_raw", [P, RING, 2, NC], F32, 16)
        w_hi = sb("w_hi", [P, PARTS, 2, NC], F32R, 32)
        w_lo = sb("w_lo", [P, PARTS, 2, NC], F32R, 40)
        X = sb("residual", [P, NT, D], F32, 48)
        ht_hi = sb("ht_hi", [P, KD, T], F32R, 64)
        ht_lo = sb("ht_lo", [P, KD, T], F32R, 80)

        def const(name):
            a, b = CONST_COLS[name]
            return C[:, a:b]

        def param(name, k=0, n=1):
            a = PARAM_COLS[name][0] + k
            return PAR[:, a:a + n]

        ident = const("ident")

        PB = sb("feature_major", [P, 20, T], F32, 96)
        PA = sb("token_major", [P, 3, NT, NC], F32, 136)
        V1, Z1, DZ = PA[:, 0], PA[:, 1], PA[:, 2]
        xn = sb("normalized", [P, NT, D], F32, 160)
        wba = sb("w_ba_sb", [P, KD, 8], F32, 176)
        wba_hi = sb("w_ba_hi", [P, KD, P], F32R, 177)
        wba_lo = sb("w_ba_lo", [P, KD, P], F32R, 181)
        ba_row = sb("ba_row", [P, T], F32, 185)
        conv4 = sb("conv_sum", [P, 4, T], F32, 188)
        KM = sb("gdn_k_tok", [P, HG, NT, DG], F32, 160)
        VM = sb("gdn_v_tok", [P, HG, NT, DG], F32, 168)
        GO = sb("gdn_out", [P, NT, HG, DG], F32, 112)
        g_names = ("KT", "TG", "IB", "EG", "DEC", "AT", "INT", "QD", "KBG", "KDEC", "VB", "U", "TI", "S")
        G = {n: sb(f"gdn_{n}", [P, HG, DG], F32, 176 + 2 * i) for i, n in enumerate(g_names)}
        sq = sb("gdn_squares", [P, NT, DG], F32, 204)
        G["VN"] = sb("gdn_new_values", [P, HG, DG], F32, 204)
        G["MA0"], G["MA1"], G["XS"], G["WN"] = G["TG"], G["IB"], G["EG"], G["DEC"]
        kz = sb("k_padded", [P, 4, 2, T], F32, 96)
        q_st1 = sb("q_staged", [P, 2, T], F32, 192)
        pr1 = sb("probs", [P, 4, T], F32, 180)
        pt1 = sb("probs_t", [P, 2, T], F32, 188)
        alibi = [sb("alibi_even", [P, T], F32, 176), sb("alibi_odd", [P, T], F32, 200)]
        mixed = sb("mixed", [P, NT, D], F32, 96)
        post_w = sb("norm_post_sb", [P, D], F32, 196)

        acc = [nc.alloc_psum_tensor(f"acc{b}", [P, NC], F32) for b in range(4)]
        aux = [nc.alloc_psum_tensor(f"aux{b}", [P, NC], F32) for b in range(4)]

        consts_in = sem("consts_in")
        x_in = [sem(f"x_in{t}") for t in range(NT)]
        wait_passed = sem("wait_passed")
        small_in = sem("small_in")
        raw_in = [sem(f"raw_in{j}") for j in range(RING)]
        hi_split = sem("hi_split")
        w_split = sem("w_split")
        unit_used = sem("unit_used")
        acc_ready = [sem(f"acc_ready{b}") for b in range(3)]
        acc_out = [sem(f"acc_out{b}") for b in range(4)]
        dve = sem("dve_step")
        flipped = sem("flipped")
        flip_hi = sem("flip_hi")
        flip_lo = sem("flip_lo")
        stored = sem("stored")

        class Steps:

            def __init__(self, eng, semaphore):
                self.eng, self.sem, self.at, self.made = eng, semaphore, 0, 0

            def __call__(self, instruction):
                self.at = self.at + 1
                self.made += 1
                instruction.then_inc(self.sem, 1)
                self.eng.wait_ge(self.sem, self.at)

            def loop(self, count, per, first=0):
                start = self.at
                with self.eng.Fori(first, first + count) as i:
                    self.at = i * per + (start - first * per)
                    before = self.made
                    yield i
                    assert self.made - before == per, (self.made - before, per)
                self.at = start + count * per

        def alone(eng):
            eng.sem_inc(wait_passed, 1)

        def split_product(pe, bank, first_operand, second_operand, start, stop):
            (ah, al), (bh, bl) = first_operand, second_operand
            nc.tensor.matmul(bank, ah, bh, start=start, stop=False)
            nc.tensor.matmul(bank, ah, bl, start=False, stop=False)
            return nc.tensor.matmul(bank, al, bh, start=False, stop=stop)

        def weight_piece(pe, unit, j, b, k0, hi, lo, slab, first, last, tokens_out):
            slot = j % PARTS
            if b == 0:
                pe.wait_ge(w_split, unit + 1)
            if first:
                pe.wait_ge(acc_out[b], slab)
            for kk in range(2):
                k = k0 + kk
                cols = slice(b * P, (b + 1) * P)
                if tokens_out:
                    w = (w_hi[:, slot, kk], w_lo[:, slot, kk])
                    a = (hi[:, k, cols], lo[:, k, cols])
                    done = split_product(pe, acc[b][:], a, w, first and kk == 0, last and kk == 1)
                else:
                    w = (w_hi[:, slot, kk, cols], w_lo[:, slot, kk, cols])
                    a = (hi[:, k], lo[:, k])
                    done = split_product(pe, acc[b][:], w, a, first and kk == 0, last and kk == 1)
            if b == 3:
                done.then_inc(unit_used, 1)
            elif last:
                done.then_inc(acc_ready[b], 1)

        def weight_slab(pe, unit, hi, lo, slab, tokens_out, units=UPS, operand=None):
            for j in range(units):
                if operand is not None:
                    pe.wait_ge(operand[0], operand[1] + (2 * j + 2))
                for b in range(4):
                    weight_piece(pe, unit + j, j, b, 2 * j, hi, lo, slab, j == 0, j == units - 1, tokens_out)

        def slab_in_pieces(pe, unit, hi, lo, slab, tokens_out, units=UPS):
            at = [0]

            def fill(n):
                for p in range(at[0], min(at[0] + n, 4 * units)):
                    j, b = divmod(p, 4)
                    weight_piece(pe, unit + j, j, b, 2 * j, hi, lo, slab, j == 0, j == units - 1, tokens_out)
                at[0] += n
            return fill

        def wait_bank(eng, b, slab, last_unit):
            if b < 3:
                eng.wait_ge(acc_ready[b], slab + 1)
            else:
                eng.wait_ge(unit_used, last_unit + 1)

        def flip_on_tensor(pe, source, chunks, count, tiles_ready):
            for k in range(chunks):
                n = count + k
                if n >= 4:
                    pe.wait_ge(flip_lo, n - 3)
                    pe.wait_ge(flip_hi, n - 3)
                for t in range(NT):
                    if k == 0 and tiles_ready is not None:
                        pe.wait_ge(tiles_ready, t + 1)
                    done = nc.tensor.transpose(aux[k % 4][:, t * P:(t + 1) * P], source(t, k), ident)
                done.then_inc(flipped, 1)

        def flip_hi_part(act, hi, chunks, count, weight):
            for k in range(chunks):
                act.wait_ge(flipped, count + k + 1)
                nc.scalar.activation(hi[:, k], aux[k % 4][:], ACT.Copy, scale=weight(k)).then_inc(flip_hi, 1)

        def flip_lo_part(eng, hi, lo, chunks, count, weight):
            for k in range(chunks):
                eng.wait_ge(flip_hi, count + k + 1)
                nc.vector.scalar_tensor_tensor(out=lo[:, k], in0=aux[k % 4][:], scalar=weight(k),
                                               in1=hi[:, k].bitcast(F32), op0=ALU.mult,
                                               op1=ALU.subtract).then_inc(flip_lo, 1)

        FLIP1, FLIP_MIXED = 0, KD
        FLIP2 = FLIP_MIXED + KD
        FLIP_A, FLIP_B = FLIP2 + KD, FLIP2 + KD + 4
        FLIP3 = FLIP_B + 4

        def rsqrt(step, v, y, t):
            step(nc.vector.tensor_scalar(y.bitcast(I32), v.bitcast(I32), -0.5, float(0x5f3759df),
                                         ALU.mult, ALU.add))
            for _ in range(3):
                step(nc.vector.scalar_tensor_tensor(out=t, in0=y, scalar=-0.5, in1=y,
                                                    op0=ALU.mult, op1=ALU.mult))
                step(nc.vector.tensor_tensor(t, t, v, ALU.mult))
                step(nc.vector.scalar_tensor_tensor(out=y, in0=t, scalar=1.5, in1=y,
                                                    op0=ALU.add, op1=ALU.mult))

        def small(a, n):
            return SMALL[:, a:a + n]
        ss, rstd, tmp4 = small(0, 4), small(4, 4), small(8, 4)
        beta, gcol, ba, rkq, ssq = small(16, 16), small(32, 16), small(48, 32), small(80, 32), small(112, 32)
        eg, egl, dl, c_bk = small(144, 16), small(160, 16), small(176, 16), small(192, 16)
        c_kbg, c_kdec, c_rq = small(208, 16), small(224, 16), small(240, 16)
        half_ss = small(340, 8)
        go_ss, go_rs, t32, nega = small(272, 16), small(288, 16), small(304, 32), small(336, 4)
        nmin, psum_, rs8 = small(0, 16), small(48, 16), small(80, 16)

        q_staged = sem("q_staged")
        scored = sem("scored")
        biased = sem("biased")
        probs = sem("probs_ready")
        probs_flipped = sem("probs_flipped")
        probs_out = sem("probs_out")
        weighed = sem("weighed")
        values_used = sem("values_used")
        STEPS = H1 * NT
        MOBA, SELECTED, WINDOW = 0, STEPS, 2 * STEPS

        class Banks:

            def __init__(self, scores, flips, values, q_st, pr, pt):
                self.scores, self.flips, self.values = scores, flips, values
                self.q_st, self.pr, self.pt, self.ring = q_st, pr, pt, len(scores)
                self.lag = max(1, self.ring - 2)

        BODY = 2 * 8

        def attention_on_tensor(pe, first, B, keys, values, filler, bodies=(0, 2)):
            with pe.Fori(*bodies) as i:
                fill = filler(i)

                def scores(n):
                    if n >= BODY:
                        return
                    pair, (h, t) = n // 8, divmod(n % 8, NT)
                    if n % 8 == 0:
                        pe.wait_ge(q_staged, i * 2 + (first // 8 + pair + 1))
                    if n >= B.ring:
                        pe.wait_ge(biased, i * BODY + (first + n - B.ring + 1))
                    w = (t + 1) * P
                    nc.tensor.matmul(B.scores[n % B.ring][:, :w], B.q_st[:, pair, t * P:(t + 1) * P],
                                     keys(i, pair, h)[:, :w], start=True, stop=True).then_inc(scored, 1)

                def flip(n):
                    t = n % NT
                    pe.wait_ge(probs, i * BODY + (first + n + 1))
                    if n >= len(B.flips):
                        pe.wait_ge(probs_out, i * BODY + (first + n - len(B.flips) + 1))
                    for j in range(t + 1):
                        done = nc.tensor.transpose(B.flips[n % len(B.flips)][:, j * P:(j + 1) * P],
                                                   B.pr[:, n % B.ring, j * P:(j + 1) * P], ident)
                    done.then_inc(probs_flipped, 1)

                def weigh(n):
                    pair, (h, t) = n // 8, divmod(n % 8, NT)
                    pe.wait_ge(probs_out, i * BODY + (first + n + 1))
                    back = min(n, len(B.values) - 1)
                    pe.wait_ge(values_used, i * BODY + (first + n - back + 1))
                    for j in range(t + 1):
                        done = nc.tensor.matmul(B.values[n % len(B.values)][:, :DH],
                                                B.pt[:, n % 2, j * P:(j + 1) * P],
                                                values(i, pair, h, j), start=j == 0, stop=j == t)
                    done.then_inc(weighed, 1)

                for n in range(B.ring - 1):
                    scores(n)
                for n in range(BODY):
                    scores(n + B.ring - 1)
                    fill(1)
                    flip(n)
                    if n:
                        weigh(n - 1)
                weigh(BODY - 1)

        def attention_on_scalar(act, first, B, after_body, bodies=(0, 2)):
            with act.Fori(*bodies) as i:
                def move(n):
                    w = (n % NT + 1) * P
                    act.wait_ge(probs_flipped, i * BODY + (first + n + 1))
                    nc.scalar.activation(B.pt[:, n % 2, :w], B.flips[n % len(B.flips)][:, :w],
                                         ACT.Copy).then_inc(probs_out, 1)

                for n in range(BODY + B.lag):
                    if n < BODY:
                        w = (n % NT + 1) * P
                        act.wait_ge(biased, i * BODY + (first + n + 1))
                        nc.scalar.activation(B.pr[:, n % B.ring, :w], B.pr[:, n % B.ring, :w], ACT.Exp,
                                             scale=-1.0, bias=nmin[:, n:n + 1],
                                             accum_out=psum_[:, n:n + 1]).then_inc(probs, 1)
                    if n >= B.lag:
                        move(n - B.lag)
                after_body(i)

        def attention_on_vector(eng, first, B, step, queries, bias, gate, result, beside, extra,
                                bodies=(0, 2)):
            for i in step.loop(bodies[1] - bodies[0], (16 if gate is None else 32) + 2 * extra, first=bodies[0]):
                for pair in range(2):
                    nc.vector.tensor_scalar(B.q_st[:, pair], queries(i, pair), -DH ** -0.5, None,
                                            ALU.mult).then_inc(q_staged, 1)

                def negate(n):
                    h, t = divmod(n % 8, NT)
                    w = (t + 1) * P
                    eng.wait_ge(scored, i * BODY + (first + n + 2))
                    if n >= B.ring:
                        eng.wait_ge(probs_flipped, i * BODY + (first + n - B.ring + 1))
                    alone(eng)
                    nc.vector.tensor_tensor_reduce(
                        out=B.pr[:, n % B.ring, :w], in0=B.scores[n % B.ring][:, :w], in1=bias(h)[:, T - w:],
                        scale=1.0, scalar=3.0e38, op0=ALU.add, op1=ALU.min,
                        accum_out=nmin[:, n:n + 1]).then_inc(biased, 1)

                def finish(n):
                    pair, (h, t) = n // 8, divmod(n % 8, NT)
                    eng.wait_ge(weighed, i * BODY + (first + n + 1))
                    step(nc.vector.reciprocal(rs8[:, n:n + 1], psum_[:, n:n + 1]))
                    op = ALU.mult
                    if gate is not None:
                        op = ALU.add
                        step(nc.vector.tensor_tensor(rs8[:, n:n + 1], rs8[:, n:n + 1], gate(i, pair, h, t),
                                                     ALU.mult))
                    nc.vector.scalar_tensor_tensor(out=result(i, pair, h, t),
                                                   in0=B.values[n % len(B.values)][:, :DH],
                                                   scalar=rs8[:, n:n + 1], in1=result(i, pair, h, t),
                                                   op0=ALU.mult, op1=op).then_inc(values_used, 1)

                for n in range(BODY + B.ring):
                    if n < BODY:
                        negate(n)
                        beside(i, n // 8, n % 8)
                    if n >= B.ring:
                        finish(n - B.ring)

        post_in = sem("post_in")
        names = ("x_squares normalized ba_split ba_product ba_row_out ba_flipped ba_tanh ba_in ba_exps "
                 "sp_log conv_done conv_silu k_padded g_flip g_copy g_square g_reduced gate_sums "
                 "gate_cols gate_exps gate_done tg_ready row_sums qk_ready e_ready dec_in dec_ready u0 "
                 "t0 t0_out masked merged x_ready x_out tx_ready solved wt_ready wn_out vn_ready vn_out "
                 "o_ready o_out o_square z_silu mixed_squares post_done go_done ").split()
        on = {n: sem(n) for n in names}

        def as_heads(bank):
            return bank[:].rearrange("p (h t) -> p h t", h=HG)


        def tile_of(buf, first, n):
            return buf[:, first:first + HG, bass.ts(n, P)]

        def heads(column):
            return column.rearrange("p (t h) -> p t h", h=HG)

        def spread(column, n):
            return column.unsqueeze(2).to_broadcast([P, HG, n])

        def each_head(table):
            return table.unsqueeze(1).to_broadcast([P, HG, table.shape[1]])

        moba_banks = Banks([aux[0], aux[1], acc[0], acc[1]], [aux[2], acc[2]], [aux[3], acc[3]], q_st1, pr1, pt1)

        PB2 = sb("feature_major_2", [P, 16, T], F32, 96)
        PA2 = sb("token_major_2", [P, 3, NT, NC], F32, 128)
        VH, AG, VSW = PA2[:, 0], PA2[:, 1], PA2[:, 2]
        YB = sb("y_b", [P, NT, NC], F32, 152)
        OA = sb("hgrn_out", [P, NT, HG, DG], F32, 152)
        hn = ("F", "LF", "KK", "B", "E", "EI", "ET", "QD", "KD", "KL", "QL", "KTM", "AM", "SS", "SQ")
        HB = {n: sb(f"hgrn_{n}", [P, T], F32, 160 + 2 * i) for i, n in enumerate(hn)}
        HB["KT"] = HB["F"]
        rope = sb("rope_tables", [P, 2, T], F32, 190)
        rope_t = sb("rope_temp", [P, 2, T], F32, 194)
        pos = sb("positions_sb", [P, T], I32, 202)
        kz2 = sb("k_padded_2", [P, 2, 2, T], F32, 160)
        kc2 = sb("cmp_tokens", [P, 2, 2, T], F32, 198)
        xc = sb("cmp_blocks", [P, 2, 2, 8, 2, CMP_C], F32, 176)
        w1 = sb("cmp_w1", [P, 2, 8, 256], F32, 96)
        w2 = sb("cmp_w2", [P, 2, 2, P], F32, 128)
        hid4 = sb("cmp_hidden_4", [P, 2, 2, 4, CMP_C], F32, 130)
        hid = sb("cmp_hidden", [P, 2, 2, 2, CMP_C], F32, 132)
        pe = sb("cmp_positions", [P, 2, 16], F32, 133)
        kcz = sb("cmp_keys", [P, 2, CMP_C], F32, 133.25)
        sg = sb("branch_gates", [P, NT, N_GATE], F32, 133.5)
        vcz = sb("cmp_values", [P, 2, 4, DH], F32, 134)
        lc = sb("cmp_logits", [P, NT, 8, CMP_C], F32, 184)
        pc = sb("cmp_probs", [P, NT, 8, CMP_C], F32, 188)
        pct = sb("cmp_probs_t", [P, NT, 2, P], F32, 192)
        q_st2 = sb("q_staged_2", [P, 2, T], F32, 168)
        pr2 = sb("probs_2", [P, 2, T], F32, 172)
        pt2 = sb("probs_t_2", [P, 2, T], F32, 176)
        branch_banks = Banks([aux[0], aux[1]], [aux[2]], [aux[3]], q_st2, pr2, pt2)
        gate_a = sb("gate_tanh_a", [P, 8, T], F32, 96)
        gate_b = sb("gate_tanh_b", [P, 8, T], F32, 180)
        ya_hi, ya_lo = sb("ya_hi", [P, 4, T], F32R, 120), sb("ya_lo", [P, 4, T], F32R, 196)
        yb_hi, yb_lo = sb("yb_hi", [P, 4, T], F32R, 112), sb("yb_lo", [P, 4, T], F32R, 160)
        mt_hi, mt_lo = sb("mt_hi", [P, KD, T], F32R, 128), sb("mt_lo", [P, KD, T], F32R, 144)
        TM = sb("merged_b", [P, 2, T], F32, 168)
        ff_hi, ff_lo = sb("ff_hi", [P, 16, T], F32R, 96), sb("ff_lo", [P, 16, T], F32R, 128)
        ff_r, ff_s = sb("ff_relu", [P, 4, T], F32, 176), sb("ff_square", [P, 4, T], F32, 184)
        fin_w = sb("final_sb", [P, D], F32, 192)

        c1, c2, dec, h_ss, h_rs = small(16, 4), small(20, 4), small(24, 4), small(32, 16), small(48, 16)
        mn16, sm16 = small(64, 16), small(80, 16)
        names2 = ("x2_squares normalized2 lb_in lb_tanh gate_th h_th h_f h_lf h_b h_exps h_tail h_et "
                 "h_kl h_ktflip h_ktm h_attn h_kv h_states h_o h_oa h_summed rot_ready rot_used roped "
                 "cmp_moved cmp_blocks hid_out hid4_ready cmp_kv cmp_z c_scores c_shift c_exp c_probs "
                 "c_flip c_flip_out c_values c_out sine m_merged mt_hi_s mt_lo_s x3_squares "
                 "normalized3 square_s ffhi_s fflo_s x4_squares final_s trig_in g_silu ya_ready hid_zero ").split()
        for n in names2:
            on[n] = sem(n)
        pos_in, fin_in, pe_in, w2_in = sem("pos_in"), sem("fin_in"), sem("pe_in"), sem("w2_in")
        w1_in = [sem(f"w1_in{j}") for j in range(2)]
        w1_used = sem("w1_used")
        CHUNKS = HG_CHUNK

        def chunked(buf):
            return buf[:].rearrange("p (t c s) -> p t c s", c=2, s=CHUNKS)

        FIRST_ROPED, N_ROPED = 8, 7

        def rotate(pe, bank, ch):
            nc.tensor.matmul(bank[:], const("rope_swap"), PB2[:, ch], start=True, stop=True)\
                .then_inc(on["rot_ready"], 1)

        def hgrn_head_on_tensor(pe, h, fill, with_rotary):
            fill(9)
            if with_rotary:
                pe.wait_ge(on["rot_used"], h * 3 - 5)
            pe.wait_ge(on["h_kl"], h + 1)
            for t in range(NT):
                done = nc.tensor.transpose(aux[0][:, t * P:(t + 1) * P], HB["KL"][:, t * P:(t + 1) * P], ident)
            done.then_inc(on["h_ktflip"], 1)
            for t in range(NT):
                a, m, z = t * P, t * P + CHUNKS, (t + 1) * P
                nc.tensor.matmul(aux[1][0:CHUNKS, a:m], HB["KD"][:, a:m], HB["QD"][:, a:m], start=True, stop=True)
                nc.tensor.matmul(aux[1][0:CHUNKS, m:z], HB["KT"][:, a:m], HB["QD"][:, m:z], start=True, stop=True)
                done = nc.tensor.matmul(aux[1][CHUNKS:P, m:z], HB["KD"][:, m:z], HB["QD"][:, m:z],
                                        start=True, stop=True)
            done.then_inc(on["h_attn"], 1)
            fill(2)
            pe.wait_ge(on["h_ktm"], h + 1)
            for t in range(NT - 1):
                done = nc.tensor.matmul(aux[2][:, t * P:(t + 1) * P], HB["KTM"][:, t * P:(t + 1) * P],
                                        VH[:, t, bass.ts(h, P)], start=True, stop=True)
            done.then_inc(on["h_kv"], 1)
            fill(3)
            pe.wait_ge(on["h_states"], h + 1)
            for t in range(NT):
                o = aux[3][:, t * P:(t + 1) * P]
                done = nc.tensor.matmul(o, HB["AM"][:, t * P:(t + 1) * P], VH[:, t, bass.ts(h, P)],
                                        start=True, stop=t == 0)
                if t:
                    done = nc.tensor.matmul(o, HB["QL"][:, t * P:(t + 1) * P], HB["SS"][:, (t - 1) * P:t * P],
                                            start=False, stop=True)
            done.then_inc(on["h_o"], 1)
            if with_rotary:
                for k in range(3):
                    rotate(pe, aux[k], h * 3 + (FIRST_ROPED - 6 + k))
            fill(2)

        def pe_second(pe):
            flip_on_tensor(pe, lambda t, k: xn[:, t, k * P:(k + 1) * P], KD, FLIP2, on["normalized2"])
            with pe.Fori(0, B2_SLABS) as i:
                weight_slab(pe, i * UPS + U_B2, ht_hi, ht_lo, i + SLAB_B2, False, operand=(flip_lo, FLIP2))
            weight_slab(pe, U_AI, ht_hi, ht_lo, SLAB_AI, True)
            for b in range(4):
                pe.wait_ge(acc_out[b], SLAB_Q2)
            for by_token in (False, True):
                with pe.Fori(2 * by_token, 2 * by_token + 2) as h:
                    fill = slab_in_pieces(pe, h * UPS + U_Q2, ht_hi, ht_lo, h + SLAB_Q2, by_token)
                    hgrn_head_on_tensor(pe, h, fill, by_token)
            fill = slab_in_pieces(pe, U_GATE, ht_hi, ht_lo, SLAB_GATE, False)
            fill(1)
            pe.wait_ge(on["rot_used"], N_ROPED)
            rotate(pe, aux[0], FIRST_ROPED + N_ROPED - 1)
            fill(10)
            for kv in range(2):
                pe.wait_ge(on["cmp_blocks"], kv + 1)
                if kv:
                    pe.wait_ge(on["rot_used"], N_ROPED + 1)
                for ab in range(2):
                    pe.wait_ge(w1_in[ab], 16 * (kv + 1))
                    for hh in range(2):
                        for lp in range(8):
                            bank = aux[2 * (1 - kv) + hh]
                            o = bank[:, 0:2 * CMP_C].rearrange("p (g c) -> p g c", g=2)[:, :, 0:N_CMP]
                            done = nc.tensor.matmul(o, w1[:, ab, lp, hh * P:(hh + 1) * P],
                                                    xc[:, kv, ab, lp, :, ab:ab + N_CMP],
                                                    start=ab == 0 and lp == 0, stop=ab == 1 and lp == 7)
                    done.then_inc(w1_used, 1)
                if kv == 0:
                    fill(3)
                    pe.wait_ge(on["ya_ready"], 1)
                    pe.wait_ge(on["hid_out"], 1)
                    flip_on_tensor(pe, lambda t, k: AG[:, t, k * P:(k + 1) * P], 4, FLIP_A, None)
                    fill(1)
                    pe.wait_ge(flip_lo, FLIP_A + 2)
            pe.wait_ge(flip_lo, FLIP_A + 4)
            pe.wait_ge(w2_in, 16)
            for hh in range(2):
                done = nc.tensor.matmul(aux[2][:, 0:2 * CMP_C], w2[:, 0, hh], hid[:, 0, hh], start=hh == 0,
                                        stop=hh == 1)
            fill(1)
            pe.wait_ge(on["hid4_ready"], 1)
            for g in range(2):
                for hh in range(2):
                    done = nc.tensor.matmul(aux[3][:, g * DH:(g + 1) * DH], hid4[:, hh, g], w2[:, 1, hh, 0:DH],
                                            start=hh == 0, stop=hh == 1)
            done.then_inc(on["cmp_kv"], 1)
            pe.wait_ge(on["cmp_z"], 1)
            for t in range(NT):
                for c in range(4):
                    o = aux[t // 2][:].rearrange("p (t g c k) -> p t c g k", t=2, g=2, c=4)[:, t % 2, c]
                    done = nc.tensor.matmul(o, PB2[:, 8 + c, t * P:(t + 1) * P], kcz[:], start=True, stop=True)
                if t % 2:
                    done.then_inc(on["c_scores"], 1)
            fill(1)
            for a in range(2):
                pe.wait_ge(on["c_probs"], a + 1)
                for t in range(2):
                    for g in range(2):
                        done = nc.tensor.transpose(aux[2 + a][:, (2 * t + g) * P:(2 * t + g + 1) * P],
                                                   pc[:, 2 * a + t, 4 * g:4 * g + 4], ident)
                done.then_inc(on["c_flip"], 1)
            for t in range(NT):
                pe.wait_ge(on["c_flip_out"], t // 2 + 1)
                if t >= 2:
                    pe.wait_ge(on["c_out"], t - 1)
                for g in range(2):
                    done = nc.tensor.matmul(aux[t % 2][:, g * 256:(g + 1) * 256], pct[:, t, g], vcz[:, g],
                                            start=True, stop=True)
                done.then_inc(on["c_values"], 1)
            pe.wait_ge(on["c_out"], NT)

            def branch_attention(first, s, filler, bodies):
                attention_on_tensor(pe, first, branch_banks, lambda i, pair, h: kz2[:, s, h],
                                    lambda i, pair, h, j: VSW[:, j, s * P + h * DH:s * P + (h + 1) * DH],
                                    filler, bodies)

            def gate_filler(slabs_before):
                return lambda i: slab_in_pieces(pe, i * UPS + (U_GATE + UPS * slabs_before), ht_hi, ht_lo,
                                                i + (SLAB_GATE + slabs_before), False)

            branch_attention(SELECTED, 0, gate_filler(1), (0, 2))
            branch_attention(WINDOW, 1, gate_filler(3), (0, 1))

            def branch_a_filler(i):
                halves = [slab_in_pieces(pe, U_BR + 2 * s, ya_hi, ya_lo, SLAB_BR + s, False, units=2)
                          for s in range(2)]
                done = [0]

                def fill(n):
                    halves[done[0] // 8](n)
                    done[0] += n
                return fill

            branch_attention(WINDOW, 1, branch_a_filler, (1, 2))
            pe.wait_ge(values_used, WINDOW + STEPS + 1)
            flip_on_tensor(pe, lambda t, k: YB[:, t, k * P:(k + 1) * P], 4, FLIP_B, None)
            with pe.Fori(0, 2) as s:
                weight_slab(pe, s * 2 + (U_BR + 4), yb_hi, yb_lo, s + (SLAB_BR + 2), False, units=2,
                            operand=(flip_lo, FLIP_B))
            with pe.Fori(0, O2_SLABS) as i:
                weight_slab(pe, i * UPS + U_O2, mt_hi, mt_lo, i + SLAB_O2, True, operand=(on["mt_lo_s"], 1))
            flip_on_tensor(pe, lambda t, k: xn[:, t, k * P:(k + 1) * P], KD, FLIP3, on["normalized3"])
            with pe.Fori(0, FF_HALVES) as f:
                with pe.Fori(0, FF1_SLABS) as i:
                    weight_slab(pe, f * U_HALF + i * UPS + U_FF, ht_hi, ht_lo, f * SLABS_HALF + i + SLAB_FF, False,
                                operand=(flip_lo, FLIP3))
                with pe.Fori(0, 2) as n:
                    weight_slab(pe, f * U_HALF + n * FF2_UNITS + (U_FF + UPS * FF1_SLABS), ff_hi, ff_lo,
                                f * SLABS_HALF + n + (SLAB_FF + FF1_SLABS), True, units=FF2_UNITS,
                                operand=(on["fflo_s"], f * 16 + 1))

        def hgrn_head_on_scalar(act, h):
            act.wait_ge(on["h_summed"], h + 1)
            nc.scalar.activation(HB["F"][:], PB2[:, h + 4], ACT.Tanh, scale=0.5).then_inc(on["h_th"], 1)
            act.wait_ge(on["h_f"], h + 1)
            nc.scalar.activation(HB["LF"][:], HB["F"][:], ACT.Ln).then_inc(on["h_lf"], 1)
            act.wait_ge(on["h_b"], h + 1)
            nc.scalar.activation(HB["E"][:], HB["B"][:], ACT.Exp).then_inc(on["h_exps"], 1)
            nc.scalar.activation(HB["EI"][:], HB["B"][:], ACT.Exp, scale=-1.0).then_inc(on["h_exps"], 1)
            act.wait_ge(on["h_tail"], h + 1)
            nc.scalar.activation(HB["ET"][:], HB["ET"][:], ACT.Exp).then_inc(on["h_et"], 1)
            act.wait_ge(on["h_ktflip"], h + 1)
            nc.scalar.activation(HB["KTM"][:], aux[0][:], ACT.Copy).then_inc(on["h_ktm"], 1)
            act.wait_ge(on["h_o"], h + 1)
            nc.scalar.activation(OA[:, :, h], aux[3][:].rearrange("p (t d) -> p t d", t=NT),
                                 ACT.Copy).then_inc(on["h_oa"], 1)
            nc.scalar.activation(HB["SQ"][:], aux[3][:], ACT.Square).then_inc(on["h_oa"], 1)

        def act_second(act):
            for t in range(NT):
                act.wait_ge(on["post_done"], t + 1)
                nc.scalar.activation(xn[:, t], X[:, t], ACT.Square,
                                     accum_out=ss[:, t:t + 1]).then_inc(on["x2_squares"], 1)
            act.dma_start(pos[:], positions).then_inc(pos_in, 16)
            flip_hi_part(act, ht_hi, KD, FLIP2, lambda k: param("norm1", k))
            with act.Fori(0, B2_SLABS) as i:
                for b in range(4):
                    wait_bank(act, b, i + SLAB_B2, i * UPS + (U_B2 + UPS - 1))
                    nc.scalar.activation(PB2[:, i * 4 + b], acc[b][:], ACT.Copy).then_inc(acc_out[b], 1)
            for b in range(4):
                wait_bank(act, b, SLAB_AI, U_AI + UPS - 1)
                nc.scalar.activation(VH[:, b], acc[b][:], ACT.Copy).then_inc(acc_out[b], 1)
            act.wait_ge(on["trig_in"], 1)
            nc.scalar.activation(rope[:], rope[:], ACT.Sin).then_inc(on["sine"], 1)
            act.wait_ge(on["lb_in"], 1)
            nc.scalar.activation(c1, c1, ACT.Tanh, scale=0.5).then_inc(on["lb_tanh"], 1)
            for by_token in (False, True):
                with act.Fori(2 * by_token, 2 * by_token + 2) as h:
                    hgrn_head_on_scalar(act, h)
                    for b in range(4):
                        wait_bank(act, b, h + SLAB_Q2, h * UPS + (U_Q2 + UPS - 1))
                        target = PA2[:, h + -1, b] if by_token else PB2[:, h * 4 + (8 + b)]
                        nc.scalar.activation(target, acc[b][:], ACT.Copy).then_inc(acc_out[b], 1)
            for b in range(4):
                act.wait_ge(acc_out[b], SLAB_GATE)
            def move_tokens(kv, ch):
                for g in range(2):
                    src = PB2[g * DH:(g + 1) * DH, ch]
                    act.dma_start(kc2[0:DH, kv, g], src).then_inc(on["cmp_moved"], 16)
                    act.dma_start(kc2[DH:P, kv, g, 0:T - 1], src[:, 1:T]).then_inc(on["cmp_moved"], 16)

            act.wait_ge(on["roped"], 5)
            move_tokens(0, 12)
            for ab in range(2):
                act.dma_start(w1[:, ab].rearrange("p a b -> p (a b)"), w1_kv[0, ab]).then_inc(w1_in[ab], 16)
            act.dma_start(pe[:].rearrange("p a b -> p (a b)"), pe_kv).then_inc(pe_in, 16)
            move_tokens(1, 15)
            act.dma_start(w2[:].rearrange("p a b c -> p (a b c)"), w2_kv).then_inc(w2_in, 16)
            nc.scalar.activation(AG, AG, ACT.Silu).then_inc(on["g_silu"], 1)
            nc.scalar.activation(sg[:], VSW[:, :, 2 * P:2 * P + N_GATE], ACT.Tanh, scale=0.5)\
                .then_inc(on["gate_th"], 1)
            for kv in range(2):
                if kv == 0:
                    for ab in range(2):
                        act.wait_ge(w1_used, ab + 1)
                        act.dma_start(w1[:, ab].rearrange("p a b -> p (a b)"), w1_kv[1, ab])\
                            .then_inc(w1_in[ab], 16)
                else:
                    act.wait_ge(w1_used, 4)
                act.wait_ge(on["hid_zero"], 1)
                for hh in range(2):
                    done = nc.scalar.activation(
                        hid[:, kv, hh, :, 0:N_CMP],
                        aux[2 * (1 - kv) + hh][:, 0:2 * CMP_C].rearrange("p (g c) -> p g c", g=2)[:, :, 0:N_CMP],
                        ACT.Gelu_apprx_tanh)
                done.then_inc(on["hid_out"], 1)
                if kv == 0:
                    flip_hi_part(act, ya_hi, 4, FLIP_A, lambda k: param("hgrn_norm"))
            for a in range(2):
                half = slice(2 * a, 2 * a + 2)
                act.wait_ge(on["c_shift"], a + 1)
                nc.scalar.activation(pc[:, half], lc[:, half], ACT.Exp).then_inc(on["c_exp"], 1)
            for a in range(2):
                half = slice(2 * a, 2 * a + 2)
                act.wait_ge(on["c_flip"], a + 1)
                nc.scalar.activation(pct[:, half].rearrange("p t g q -> p (t g q)"), aux[2 + a][:],
                                     ACT.Copy).then_inc(on["c_flip_out"], 1)
            for t in range(NT):
                act.wait_ge(on["c_values"], t + 1)
                nc.scalar.activation(YB[:, t], aux[t % 2][:], ACT.Copy).then_inc(on["c_out"], 1)

            def gates_out(i, gate, at, slabs_before):
                for b in range(4):
                    wait_bank(act, b, i + (SLAB_GATE + slabs_before),
                              i * UPS + (U_GATE + UPS * slabs_before + UPS - 1))
                    alone(act)
                    nc.scalar.activation(gate[:, i * 4 + (at + b)], acc[b][:], ACT.Tanh,
                                         scale=0.5).then_inc(acc_out[b], 1)

            gates_out(0, gate_a, 0, 0)
            attention_on_scalar(act, SELECTED, branch_banks, lambda i: gates_out(i, gate_a, 4, 1), (0, 1))
            attention_on_scalar(act, SELECTED, branch_banks, lambda i: gates_out(i, gate_b, -4, 1), (1, 2))
            attention_on_scalar(act, WINDOW, branch_banks, lambda i: gates_out(i, gate_b, 4, 3), (0, 1))
            attention_on_scalar(act, WINDOW, branch_banks, lambda i: None, (1, 2))
            flip_hi_part(act, yb_hi, 4, FLIP_B, lambda k: 1.0)
            with act.Fori(0, 2) as s:
                for b in range(4):
                    act.wait_ge(on["m_merged"], s * 4 + (b + 1))
                    nc.scalar.activation(mt_hi[:, s * 4 + b], gate_b[:, s * 4 + b], ACT.Copy, scale=0.5)\
                        .then_inc(on["mt_hi_s"], 1)
            for t in range(NT):
                act.wait_ge(acc_out[t], SLAB_FF)
                nc.scalar.activation(xn[:, t], X[:, t], ACT.Square,
                                     accum_out=ss[:, t:t + 1]).then_inc(on["x3_squares"], 1)
            flip_hi_part(act, ht_hi, KD, FLIP3, lambda k: param("norm2", k))
            with act.Fori(0, FF_HALVES) as f:
                with act.Fori(0, FF1_SLABS) as i:
                    for b in range(4):
                        act.wait_ge(on["fflo_s"], f * 16 + i * 4 + 1)
                        wait_bank(act, b, f * SLABS_HALF + i + SLAB_FF, f * U_HALF + i * UPS + (U_FF + UPS - 1))
                        nc.scalar.activation(ff_r[:, b], acc[b][:], ACT.Relu).then_inc(acc_out[b], 1)
                    for b in range(4):
                        act.wait_ge(on["square_s"], f * 16 + i * 4 + (b + 1))
                        nc.scalar.activation(ff_hi[:, i * 4 + b], ff_s[:, b], ACT.Copy).then_inc(on["ffhi_s"], 1)
            act.dma_start(fin_w[:], final_g).then_inc(fin_in, 16)
            for t in range(NT):
                act.wait_ge(acc_out[t], SLAB_FF + FF_HALVES * SLABS_HALF)
                nc.scalar.activation(xn[:, t], X[:, t], ACT.Square,
                                     accum_out=ss[:, t:t + 1]).then_inc(on["x4_squares"], 1)

        TWO_PI_PARTS = (6.28125, 2029.0 / 2 ** 20, 2 * np.pi - 6.28125 - 2029.0 / 2 ** 20)
        ROUND = 1.5 * 2 ** 23

        def dve_second(eng, step):
            V = nc.vector

            def normalize(squares, target):
                eng.wait_ge(squares, NT)
                step(V.tensor_scalar(ss, ss, 1.0 / D, EPS, ALU.mult, ALU.add))
                rsqrt(step, ss, rstd, tmp4)
                for t in range(NT):
                    V.tensor_scalar(xn[:, t], X[:, t], rstd[:, t:t + 1], None, ALU.mult).then_inc(target, 1)

            def rotary_tables():
                eng.wait_ge(pos_in, 16)
                ang, turns = rope_t[:, 0], rope_t[:, 1]
                step(V.tensor_copy(turns, pos[:]))
                step(V.tensor_scalar(ang, turns, const("inv_freq"), None, ALU.mult))
                for s, quarter in ((0, 0.25), (1, 0.0)):
                    red = rope[:, s]
                    step(V.tensor_scalar(turns, ang, float(1 / (2 * np.pi)), quarter, ALU.mult, ALU.add))
                    step(V.tensor_scalar(turns, turns, ROUND, -ROUND, ALU.add, ALU.add))
                    step(V.scalar_tensor_tensor(out=red, in0=turns, scalar=-TWO_PI_PARTS[0], in1=ang,
                                                op0=ALU.mult, op1=ALU.add))
                    for part in TWO_PI_PARTS[1:]:
                        step(V.scalar_tensor_tensor(out=red, in0=turns, scalar=-float(part), in1=red,
                                                    op0=ALU.mult, op1=ALU.add))
                    if s == 0:
                        step(V.tensor_scalar(red, red, float(np.pi / 2), None, ALU.add))
                    done = V.tensor_scalar(red, red, 3.1415925, -3.1415925, ALU.min, ALU.max)
                    if s == 0:
                        step(done)
                done.then_inc(on["trig_in"], 1)

            normalize(on["x2_squares"], on["normalized2"])
            flip_lo_part(eng, ht_hi, ht_lo, KD, FLIP2, lambda k: param("norm1", k))
            rotary_tables()
            V.tensor_tensor(c1, param("lb", 0, 4), param("lb", 4, 4), ALU.subtract).then_inc(on["lb_in"], 1)
            eng.wait_ge(on["lb_tanh"], 1)
            step(V.tensor_scalar(c1, c1, 0.5, 0.5, ALU.mult, ALU.add))
            step(V.tensor_scalar(c2, c1, 0.5, 0.5, ALU.mult, ALU.add))
            step(V.tensor_scalar(c1, c1, -0.5, 0.5, ALU.mult, ALU.add))
            for b in range(4):
                eng.wait_ge(acc_out[b], SLAB_AI)
            step(V.memset(HB["AM"][:], 0.0))

            def rotary(bank, ch, n):
                turned = rope_t[:, n[1]]
                eng.wait_ge(on["rot_ready"], n[0] + 1)
                V.tensor_tensor(turned, bank[:], rope[:, 1], ALU.mult).then_inc(on["rot_used"], 1)
                step(V.tensor_tensor(PB2[:, ch], PB2[:, ch], rope[:, 0], ALU.mult))
                eng.wait_ge(on["rot_used"], n[0] + 2)
                V.tensor_tensor(PB2[:, ch], PB2[:, ch], turned, ALU.add).then_inc(on["roped"], 1)
                eng.wait_ge(on["roped"], n[0] + 1)

            def hgrn_head_on_vector(h, with_rotary):
                one = bass.ds(h, 1)
                eng.wait_ge(on["h_th"], h + 1)
                V.tensor_scalar(HB["F"][:], HB["F"][:], c1[:, one], c2[:, one], ALU.mult,
                                ALU.add).then_inc(on["h_f"], 1)
                eng.wait_ge(on["h_lf"], h + 1)
                step(V.tensor_scalar(HB["KK"][:], HB["F"][:], -1.0, 1.0, ALU.mult, ALU.add))
                V.tensor_tensor_scan(HB["B"][:], const("restart"), HB["LF"][:], 0.0, ALU.mult,
                                     ALU.add).then_inc(on["h_b"], 1)
                eng.wait_ge(on["h_b"], h + 1)
                b8 = HB["B"][:].rearrange("p (n s) -> p n s", s=CHUNKS)
                V.tensor_tensor(HB["ET"][:].rearrange("p (n s) -> p n s", s=CHUNKS),
                                b8[:, :, CHUNKS - 1:CHUNKS].to_broadcast([P, T // CHUNKS, CHUNKS]), b8,
                                ALU.subtract).then_inc(on["h_tail"], 1)
                eng.wait_ge(on["h_exps"], h * 2 + 2)
                step(V.tensor_tensor(HB["QD"][:], PB2[:, h], HB["E"][:], ALU.mult))
                step(V.tensor_tensor(HB["KD"][:], HB["KK"][:], HB["EI"][:], ALU.mult))
                eng.wait_ge(on["h_et"], h + 1)
                step(V.tensor_tensor(HB["KT"][:], HB["KK"][:], HB["ET"][:], ALU.mult))
                e4, kt4, kl4 = chunked(HB["E"]), chunked(HB["KT"]), chunked(HB["KL"])
                qd4, ql4 = chunked(HB["QD"]), chunked(HB["QL"])
                last = slice(CHUNKS - 1, CHUNKS)
                shape = [P, NT, CHUNKS]
                step(V.tensor_tensor(ql4[:, :, 1], qd4[:, :, 1], e4[:, :, 0, last].to_broadcast(shape), ALU.mult))
                step(V.tensor_copy(ql4[:, :, 0], qd4[:, :, 0]))
                step(V.tensor_tensor(dec.unsqueeze(2), e4[:, :, 0, last], e4[:, :, 1, last], ALU.mult))
                step(V.tensor_copy(kl4[:, :, 1], kt4[:, :, 1]))
                V.tensor_tensor(kl4[:, :, 0], kt4[:, :, 0], e4[:, :, 1, last].to_broadcast(shape),
                                ALU.mult).then_inc(on["h_kl"], 1)
                eng.wait_ge(on["h_attn"], h + 1)
                alone(eng)
                attn = aux[1][:].rearrange("p (t s) -> p t s", t=NT)
                am = HB["AM"][:].rearrange("p (t s) -> p t s", t=NT)
                mask = const("tri").bitcast(I32)
                step(V.copy_predicated(am[0:CHUNKS],
                                       mask[0:CHUNKS].unsqueeze(1).to_broadcast([CHUNKS, NT, P]), attn[0:CHUNKS]))
                alone(eng)
                step(V.copy_predicated(am[CHUNKS:P, :, CHUNKS:P],
                                       mask[CHUNKS:P, CHUNKS:P].unsqueeze(1).to_broadcast([CHUNKS, NT, CHUNKS]),
                                       attn[CHUNKS:P, :, CHUNKS:P]))
                eng.wait_ge(on["h_kv"], h + 1)
                step(V.tensor_copy(HB["SS"][:, 0:P], aux[2][:, 0:P]))
                step(V.scalar_tensor_tensor(out=HB["SS"][:, P:2 * P], in0=HB["SS"][:, 0:P], scalar=dec[:, 1:2],
                                            in1=aux[2][:, P:2 * P], op0=ALU.mult, op1=ALU.add))
                V.scalar_tensor_tensor(out=HB["SS"][:, 2 * P:3 * P], in0=HB["SS"][:, P:2 * P],
                                       scalar=dec[:, 2:3], in1=aux[2][:, 2 * P:3 * P], op0=ALU.mult,
                                       op1=ALU.add).then_inc(on["h_states"], 1)
                eng.wait_ge(on["h_oa"], h * 2 + 2)
                V.tensor_reduce(heads(h_ss)[:, :, one], HB["SQ"][:].rearrange("p (t d) -> p t d", t=NT),
                                AX, ALU.add).then_inc(on["h_summed"], 1)
                if with_rotary:
                    for k in range(3):
                        rotary(aux[k], h * 3 + (FIRST_ROPED - 6 + k), (h * 3 + (k - 6), k % 2))

            for h in step.loop(2, 12):
                hgrn_head_on_vector(h, False)
            eng.wait_ge(on["sine"], 1)
            for b in range(4):
                eng.wait_ge(acc_out[b], SLAB_Q2 + 2)
            for h in step.loop(2, 15, first=2):
                hgrn_head_on_vector(h, True)
            rotary(aux[0], FIRST_ROPED + N_ROPED - 1, (N_ROPED - 1, 0))
            V.memset(hid[:], 0.0).then_inc(on["hid_zero"], 1)
            step(V.memset(kcz[:], 0.0))
            eng.wait_ge(on["h_summed"], HG + 1)
            step(V.tensor_scalar(h_ss, h_ss, 1.0 / DG, EPS, ALU.mult, ALU.add))
            rsqrt(step, h_ss, h_rs, t32[:, 0:16])
            step(V.memset(kz2[:], 0.0))
            for s in range(2):
                for g in range(2):
                    rows = slice(g * DH, (g + 1) * DH)
                    step(V.tensor_copy(kz2[rows, s, g], PB2[rows, 13 + s]))
            eng.wait_ge(pe_in, 16)
            eng.wait_ge(on["cmp_moved"], 16 * 8)
            for kv in range(2):
                tokens = kc2[:, kv].rearrange("p g (c l two) -> p l (g c) two", l=8, two=2)[:, :, :, 0]
                for ab in range(2):
                    done = V.tensor_tensor(
                        xc[:, kv, ab].rearrange("p l g c -> p l (g c)"), tokens,
                        pe[:, kv, 8 * ab:8 * ab + 8].unsqueeze(2).to_broadcast([P, 8, 2 * CMP_C]), ALU.add)
                    if ab == 0:
                        step(done)
                done.then_inc(on["cmp_blocks"], 1)
            eng.wait_ge(on["g_silu"], 1)
            for t in range(NT):
                step(V.tensor_tensor(OA[:, t], OA[:, t], spread(h_rs[:, t * HG:(t + 1) * HG], DG), ALU.mult))
                step(V.tensor_tensor(AG[:, t], AG[:, t], OA[:, t].rearrange("p h d -> p (h d)"), ALU.mult))
            V.memset(vcz[:], 0.0).then_inc(on["ya_ready"], 1)
            eng.wait_ge(on["ya_ready"], 1)
            flip_lo_part(eng, ya_hi, ya_lo, 4, FLIP_A, lambda k: param("hgrn_norm"))
            eng.wait_ge(on["hid_out"], 2)
            for hh in range(2):
                done = V.tensor_copy(hid4[:, hh], hid[:, 1, hh].unsqueeze(2).to_broadcast([P, 2, 4, CMP_C]))
                if hh == 0:
                    step(done)
            done.then_inc(on["hid4_ready"], 1)
            eng.wait_ge(on["gate_th"], 1)
            step(V.tensor_scalar(sg[:], sg[:], 0.5, 0.5, ALU.mult, ALU.add))
            eng.wait_ge(on["cmp_kv"], 1)
            for g in range(2):
                rows = slice(g * DH, (g + 1) * DH)
                step(V.tensor_copy(kcz[rows, g], aux[2][rows, g * CMP_C:(g + 1) * CMP_C]))
            for h in range(4):
                rows = slice(h * CMP_C, (h + 1) * CMP_C)
                done = V.tensor_copy(vcz[rows, :, h], aux[3][rows, 0:2 * DH].rearrange("p (g d) -> p g d", g=2))
                if h < 3:
                    step(done)
            done.then_inc(on["cmp_z"], 1)
            def tables_of(name, a):
                table = const(name)[:, 2 * a * CMP_C:2 * (a + 1) * CMP_C].rearrange("p (t c) -> p t c", t=2)
                return table.unsqueeze(2).to_broadcast([P, 2, 8, CMP_C])

            def per_row(column):
                return column.rearrange("p (t h) -> p t h", t=2)

            def each_column(column):
                return per_row(column).unsqueeze(3).to_broadcast([P, 2, 8, CMP_C])

            for a in range(2):
                half = slice(2 * a, 2 * a + 2)
                eng.wait_ge(on["c_scores"], a + 1)
                for t in range(2):
                    step(V.scalar_tensor_tensor(
                        out=lc[:, 2 * a + t], in0=aux[a][:].rearrange("p (t h c) -> p t h c", t=2, h=8)[:, t],
                        scalar=-DH ** -0.5, in1=tables_of("cmp_hide", a)[:, t], op0=ALU.mult, op1=ALU.add))
                step(V.tensor_reduce(per_row(mn16), lc[:, half], AX, ALU.min))
                V.tensor_tensor(lc[:, half], each_column(mn16), lc[:, half], ALU.subtract)\
                    .then_inc(on["c_shift"], 1)
            for a in range(2):
                half = slice(2 * a, 2 * a + 2)
                eng.wait_ge(on["c_exp"], a + 1)
                step(V.tensor_tensor(pc[:, half], pc[:, half], tables_of("cmp_keep", a), ALU.mult))
                step(V.tensor_reduce(per_row(sm16), pc[:, half], AX, ALU.add))
                step(V.tensor_scalar(sm16, sm16, 1e-30, None, ALU.max))
                step(V.reciprocal(sm16, sm16))
                step(V.tensor_tensor(per_row(sm16), per_row(sm16),
                                     sg[:, half].rearrange("p t (h b) -> p t h b", b=3)[:, :, :, 0], ALU.mult))
                V.tensor_tensor(pc[:, half], pc[:, half], each_column(sm16), ALU.mult).then_inc(on["c_probs"], 1)
            eng.wait_ge(on["c_out"], NT)
            def branch_a_out(s):
                for b in range(4):
                    chunk = gate_a[:, s * 4 + b]
                    wait_bank(eng, b, SLAB_BR + s, U_BR + 2 * s + 1)
                    V.scalar_tensor_tensor(out=chunk, in0=chunk, scalar=1.0, in1=acc[b][:], op0=ALU.add,
                                           op1=ALU.mult).then_inc(acc_out[b], 1)

            for first, branch, bodies in ((SELECTED, 1, (0, 2)), (WINDOW, 2, (0, 1)), (WINDOW, 2, (1, 2))):
                if bodies[0] == 0:
                    eng.wait_ge(values_used, first + 1)
                last = (first, bodies[0]) == (WINDOW, 1)
                attention_on_vector(
                    eng, first, branch_banks, step, lambda i, pair: PB2[:, i * 2 + (8 + pair)],
                    lambda h: const("causal"),
                    lambda i, pair, h, t: sg[:, t, bass.ds(i * 6 + (3 * pair + 12 * h + branch), 1)],
                    lambda i, pair, h, t: YB[:, t, bass.ds(i * 2 * DH + (pair * DH + 4 * DH * h), DH)],
                    lambda i, pair, n: branch_a_out(pair) if last and n == 7 else None, 0, bodies)
            flip_lo_part(eng, yb_hi, yb_lo, 4, FLIP_B, lambda k: 1.0)
            def merged_lo(s, b):
                eng.wait_ge(on["mt_hi_s"], s * 4 + (b + 1))
                V.scalar_tensor_tensor(out=mt_lo[:, s * 4 + b], in0=gate_b[:, s * 4 + b], scalar=0.5,
                                       in1=mt_hi[:, s * 4 + b].bitcast(F32), op0=ALU.mult,
                                       op1=ALU.subtract).then_inc(on["mt_lo_s"], 1)

            with eng.Fori(0, 2) as s:
                for b in range(4):
                    both = gate_b[:, s * 4 + b]
                    wait_bank(eng, b, s + (SLAB_BR + 2), s * 2 + (U_BR + 5))
                    V.scalar_tensor_tensor(out=TM[:, b % 2], in0=both, scalar=1.0, in1=acc[b][:], op0=ALU.add,
                                           op1=ALU.mult).then_inc(acc_out[b], 1)
                    eng.wait_ge(acc_out[b], s + (SLAB_BR + 3))
                    V.tensor_tensor(both, gate_a[:, s * 4 + b], TM[:, b % 2], ALU.add).then_inc(on["m_merged"], 1)
                    if b:
                        merged_lo(s, b - 1)
                merged_lo(s, 3)

            def add_to_residual(slab, last_unit, n):
                for b in range(4):
                    wait_bank(eng, b, slab, last_unit)
                    cols = X[:, b, bass.ts(n, NC)]
                    V.tensor_tensor(cols, cols, acc[b][:], ALU.add).then_inc(acc_out[b], 1)

            with eng.Fori(0, O2_SLABS) as i:
                add_to_residual(i + SLAB_O2, i * UPS + (U_O2 + UPS - 1), i)
            normalize(on["x3_squares"], on["normalized3"])
            flip_lo_part(eng, ht_hi, ht_lo, KD, FLIP3, lambda k: param("norm2", k))
            with eng.Fori(0, FF_HALVES) as f:
                with eng.Fori(0, FF1_SLABS) as i:
                    for b in range(4):
                        eng.wait_ge(acc_out[b], f * SLABS_HALF + i + (SLAB_FF + 1))
                        V.tensor_tensor(ff_s[:, b], ff_r[:, b], ff_r[:, b], ALU.mult).then_inc(on["square_s"], 1)
                    for b in range(4):
                        eng.wait_ge(on["ffhi_s"], f * 16 + i * 4 + (b + 1))
                        V.tensor_tensor(ff_lo[:, i * 4 + b], ff_s[:, b], ff_hi[:, i * 4 + b].bitcast(F32),
                                        ALU.subtract).then_inc(on["fflo_s"], 1)
                with eng.Fori(0, 2) as n:
                    add_to_residual(f * SLABS_HALF + n + (SLAB_FF + FF1_SLABS),
                                    f * U_HALF + n * FF2_UNITS + (U_FF + UPS * FF1_SLABS + FF2_UNITS - 1), n)
            eng.wait_ge(on["x4_squares"], NT)
            eng.wait_ge(fin_in, 16)
            step(V.tensor_scalar(ss, ss, 1.0 / D, EPS, ALU.mult, ALU.add))
            rsqrt(step, ss, rstd, tmp4)
            for t in range(NT):
                V.scalar_tensor_tensor(out=xn[:, t], in0=X[:, t], scalar=rstd[:, t:t + 1], in1=fin_w[:],
                                       op0=ALU.mult, op1=ALU.mult).then_inc(on["final_s"], 1)

        def sp_rest(sp):
            rows = out.rearrange("(t p) d -> p t d", p=P)
            for t in range(NT):
                sp.wait_ge(on["final_s"], t + 1)
                sp.dma_start(rows[:, t], xn[:, t]).then_inc(stored, 16)
            sp.wait_ge(stored, 16 * NT)

        block = ctx.enter_context(nc.Block())

        @block.sync
        def _(sp):
            for t in range(NT):
                sp.dma_start(X[:, t], x[t * P:(t + 1) * P]).then_inc(x_in[t], 16)
            sp.dma_start(C[:], consts).then_inc(consts_in, 16)
            sp.dma_start(PAR[:], params).then_inc(consts_in, 16)
            for j in range(RING):
                sp.dma_start(raw[:, j].rearrange("p k n -> p (k n)"), units[j]).then_inc(raw_in[j], 16)
            sp.dma_start(wba[:].rearrange("p k n -> p (k n)"), w_ba).then_inc(small_in, 16)
            with sp.Fori(1, N_UNITS // RING) as i:
                for j in range(RING):
                    sp.wait_ge(w_split, i * RING + (j - RING + 1))
                    sp.dma_start(raw[:, j].rearrange("p k n -> p (k n)"),
                                 units[i * RING + j]).then_inc(raw_in[j], 16)
            sp_rest(sp)

        @block.gpsimd
        def _(pool):
            one = const("ones")[:, 0:1].unsqueeze(2).to_broadcast([P, 2, NC])

            def split(unit, i, j, reused):
                pool.wait_ge(raw_in[j], i * 16 + 16)
                if reused:
                    pool.wait_ge(unit_used, unit - (PARTS - 1))
                    alone(pool)
                slot = j % PARTS
                nc.gpsimd.tensor_tensor(w_hi[:, slot], raw[:, j], one, ALU.mult).then_inc(hi_split, 1)
                pool.wait_ge(hi_split, unit + 1)
                nc.gpsimd.tensor_tensor(w_lo[:, slot], raw[:, j], w_hi[:, slot].bitcast(F32),
                                        ALU.subtract).then_inc(w_split, 1)

            pool.wait_ge(consts_in, 32)
            for j in range(RING):
                split(j, 0, j, j >= PARTS)
            with pool.Fori(1, N_UNITS // RING) as i:
                for j in range(RING):
                    split(i * RING + j, i, j, True)

        def delta_tile_on_tensor(pe, n, fill):
            def per_head(bank, left, right, start=True, stop=True):
                for h in range(HG):
                    done = nc.tensor.matmul(bank[:, h * P:(h + 1) * P], left(h), right(h), start=start, stop=stop)
                return done

            pe.wait_ge(on["tg_ready"], n + 1)
            nc.tensor.matmul(aux[0][:], const("ones"), G["TG"][:], start=True, stop=True)
            nc.tensor.matmul(aux[1][:], const("ones"), G["IB"][:], start=True, stop=True).then_inc(on["row_sums"], 1)
            fill(1)
            pe.wait_ge(on["o_out"], n + 1)
            per_head(aux[2], lambda h: G["KT"][:, h], lambda h: G["KT"][:, h])
            per_head(aux[3], lambda h: G["KT"][:, h],
                     lambda h: PB[:, h, bass.ts(n, P)]).then_inc(on["qk_ready"], 1)
            fill(5)
            pe.wait_ge(on["u0"], n + 1)
            for h in range(HG):
                done = nc.tensor.transpose(aux[0][:, h * P:(h + 1) * P], G["U"][:, h], ident)
            done.then_inc(on["t0"], 1)
            fill(1)
            pe.wait_ge(on["t0_out"], n + 1)
            for m in range(6):
                mask = G[f"MA{(m + 1) % 2}"]
                pe.wait_ge(on["masked"], n * 6 + m + 1)
                if m:
                    pe.wait_ge(on["merged"], n * 10 + 2 * m - 1)
                per_head(aux[1], lambda h: mask[:, h], lambda h: G["TI"][:, h]).then_inc(on["x_ready"], 1)
                fill(1)
                pe.wait_ge(on["x_out"], n * 6 + m + 1)
                if m:
                    pe.wait_ge(on["merged"], n * 10 + 2 * m)
                if m < 5:
                    per_head(aux[2], lambda h: G["U"][:, h], lambda h: G["XS"][:, h]).then_inc(on["tx_ready"], 1)
                per_head(aux[3], lambda h: G["XS"][:, h], lambda h: G["U"][:, h]).then_inc(on["tx_ready"], 1)
            pe.wait_ge(on["solved"], n + 1)
            per_head(aux[0], lambda h: G["KBG"][:, h], lambda h: G["U"][:, h]).then_inc(on["wt_ready"], 1)
            fill(1)
            pe.wait_ge(on["wn_out"], n + 1)
            for h in range(HG):
                nc.tensor.matmul(aux[1][:, h * P:(h + 1) * P], G["U"][:, h], G["VB"][:, h],
                                 start=True, stop=False)
                done = nc.tensor.matmul(aux[1][:, h * P:(h + 1) * P], G["WN"][:, h], G["S"][:, h],
                                        start=False, stop=True)
            done.then_inc(on["vn_ready"], 1)
            fill(2)
            pe.wait_ge(on["vn_out"], n + 1)
            for h in range(HG):
                nc.tensor.matmul(aux[2][:, h * P:(h + 1) * P], G["QD"][:, h], G["S"][:, h],
                                 start=True, stop=False)
                nc.tensor.matmul(aux[2][:, h * P:(h + 1) * P], G["INT"][:, h], G["VN"][:, h],
                                 start=False, stop=True)
            per_head(aux[3], lambda h: G["KDEC"][:, h], lambda h: G["VN"][:, h]).then_inc(on["o_ready"], 1)

        @block.tensor
        def _(pe):
            for count in (*acc_ready, scored):
                pe.sem_inc(count, 1)
            pe.wait_ge(consts_in, 32)
            flip_on_tensor(pe, lambda t, k: xn[:, t, k * P:(k + 1) * P], KD, FLIP1, on["normalized"])
            with pe.Fori(0, D1_SLABS) as i:
                weight_slab(pe, i * UPS + U_D1, ht_hi, ht_lo, i + SLAB_D1, False, operand=(flip_lo, FLIP1))
            pe.wait_ge(on["ba_split"], 2)
            for k in range(KD):
                done = split_product(pe, aux[2][:], (wba_hi[:, k], wba_lo[:, k]),
                                     (ht_hi[:, k], ht_lo[:, k]), k == 0, k == KD - 1)
            done.then_inc(on["ba_product"], 1)
            fill = slab_in_pieces(pe, U_DZ, ht_hi, ht_lo, SLAB_DZ, True)
            fill(2)
            pe.wait_ge(on["ba_row_out"], 1)
            for t in range(NT):
                done = nc.tensor.transpose(aux[3][:, t * 8:(t + 1) * 8], ba_row[0:8, t * P:(t + 1) * P],
                                           ident[0:8, 0:8])
            done.then_inc(on["ba_flipped"], 1)
            for n in range(12):
                fill(1)
                pe.wait_ge(on["conv_silu"], n + 2)
                if n >= 2:
                    pe.wait_ge(on["g_copy"], n - 1)
                for t in range(NT):
                    done = nc.tensor.transpose(aux[n % 2][:, t * P:(t + 1) * P],
                                               PB[:, n, t * P:(t + 1) * P], ident)
                done.then_inc(on["g_flip"], 1)
            pe.wait_ge(on["gate_sums"], 1)
            nc.tensor.matmul(aux[2][:, 0:16], const("tri"), gcol, start=True, stop=True)
            nc.tensor.matmul(aux[2][:, 16:32], const("ones"), gcol, start=True,
                             stop=True).then_inc(on["gate_cols"], 1)
            fill(2)
            pe.wait_ge(on["gate_done"], 1)
            for by_token in (False, True):
                with pe.Fori(2 * by_token, 2 * by_token + 2) as n:
                    fill = slab_in_pieces(pe, n * UPS + U_Q1, ht_hi, ht_lo, n + SLAB_Q1, by_token)
                    delta_tile_on_tensor(pe, n, fill)
            pe.wait_ge(on["k_padded"], 1)
            for b in range(4):
                pe.wait_ge(acc_out[b], SLAB_O1)
            attention_on_tensor(pe, MOBA, moba_banks, lambda i, pair, h: kz[:, i * 2 + pair, h],
                                lambda i, pair, h, j: V1[:, j, bass.ds(i * 2 * P + (pair * P + h * DH), DH)],
                                lambda i: lambda n: None)
            pe.wait_ge(on["go_done"], NT)
            pe.wait_ge(values_used, MOBA + STEPS + 1)
            flip_on_tensor(pe, lambda t, k: PA[:, 1 + k // 4, t, (k % 4) * P:(k % 4 + 1) * P], KD, FLIP_MIXED, None)
            with pe.Fori(0, O1_SLABS) as i:
                weight_slab(pe, i * UPS + U_O1, ht_hi, ht_lo, i + SLAB_O1, True, operand=(flip_lo, FLIP_MIXED))
            pe_second(pe)

        def delta_tile_on_scalar(act, n):
            act.wait_ge(on["row_sums"], n + 1)
            nc.scalar.activation(G["EG"][:], aux[0][:], ACT.Exp).then_inc(on["e_ready"], 1)
            act.wait_ge(on["dec_in"], n + 1)
            nc.scalar.activation(G["DEC"][:], G["DEC"][:], ACT.Exp).then_inc(on["dec_ready"], 1)
            act.wait_ge(on["t0"], n + 1)
            nc.scalar.activation(G["TI"][:], aux[0][:], ACT.Copy).then_inc(on["t0_out"], 1)
            for m in range(6):
                act.wait_ge(on["x_ready"], n * 6 + m + 1)
                nc.scalar.activation(G["XS"][:], aux[1][:], ACT.Copy).then_inc(on["x_out"], 1)
            act.wait_ge(on["wt_ready"], n + 1)
            nc.scalar.activation(G["WN"][:], aux[0][:], ACT.Copy, scale=-1.0).then_inc(on["wn_out"], 1)
            act.wait_ge(on["vn_ready"], n + 1)
            nc.scalar.activation(G["VN"][:], aux[1][:], ACT.Copy).then_inc(on["vn_out"], 1)

        @block.scalar
        def _(act):
            for count in (*acc_out, on["conv_silu"]):
                act.sem_inc(count, 1)
            for t in range(NT):
                act.wait_ge(x_in[t], 16)
                nc.scalar.activation(xn[:, t], X[:, t], ACT.Square,
                                     accum_out=ss[:, t:t + 1]).then_inc(on["x_squares"], 1)
            act.wait_ge(consts_in, 32)
            flip_hi_part(act, ht_hi, KD, FLIP1, lambda k: param("norm_pre", k))
            with act.Fori(0, D1_SLABS) as i:
                for b in range(4):
                    wait_bank(act, b, i + SLAB_D1, i * UPS + (U_D1 + UPS - 1))
                    nc.scalar.activation(PB[:, i * 4 + b], acc[b][:], ACT.Copy).then_inc(acc_out[b], 1)
                for b in range(4):
                    act.wait_ge(on["conv_done"], i * 4 + (b + 1))
                    alone(act)
                    nc.scalar.activation(PB[:, i * 4 + b], conv4[:, b], ACT.Silu).then_inc(on["conv_silu"], 1)
            act.wait_ge(on["ba_product"], 1)
            nc.scalar.activation(ba_row[0:8], aux[2][0:8, :], ACT.Copy).then_inc(on["ba_row_out"], 1)
            act.wait_ge(on["ba_in"], 1)
            bv = ba.rearrange("p (t c) -> p t c", c=8)
            nc.scalar.activation(heads(beta), bv[:, :, 0:4], ACT.Tanh, scale=0.5).then_inc(on["ba_tanh"], 1)
            nc.scalar.activation(nega, param("a_log", 0, HG), ACT.Exp).then_inc(on["ba_tanh"], 1)
            nc.scalar.activation(t32[:, 0:16], t32[:, 0:16], ACT.Exp, scale=-1.0).then_inc(on["ba_exps"], 1)
            act.wait_ge(on["ba_exps"], 1)
            nc.scalar.activation(t32[:, 16:32], t32[:, 0:16], ACT.Ln, bias=1.0).then_inc(on["sp_log"], 1)
            for n in range(12):
                act.wait_ge(on["g_flip"], n + 1)
                if n < 8:
                    act.wait_ge(on["g_reduced"], n + 1)
                if n < 4:
                    nc.scalar.activation(sq[:], aux[n % 2][:], ACT.Square).then_inc(on["g_copy"], 1)
                elif n < 8:
                    nc.scalar.activation(sq[:], aux[n % 2][:], ACT.Square).then_inc(on["g_square"], 1)
                    nc.scalar.activation(KM[:, n - 4], aux[n % 2][:], ACT.Copy).then_inc(on["g_copy"], 1)
                else:
                    nc.scalar.activation(VM[:, n - 8], aux[n % 2][:], ACT.Copy).then_inc(on["g_copy"], 1)
            for b in range(4):
                wait_bank(act, b, SLAB_DZ, U_DZ + UPS - 1)
                nc.scalar.activation(DZ[:, b], acc[b][:], ACT.Silu).then_inc(acc_out[b], 1)
            act.wait_ge(on["gate_cols"], 1)
            nc.scalar.activation(eg, aux[2][:, 0:16], ACT.Exp).then_inc(on["gate_exps"], 1)
            nc.scalar.activation(egl, aux[2][:, 16:32], ACT.Exp).then_inc(on["gate_exps"], 1)
            act.wait_ge(on["gate_done"], 1)
            nc.scalar.activation(dl, dl, ACT.Exp).then_inc(on["gate_exps"], 1)
            for by_token in (False, True):
                with act.Fori(2 * by_token, 2 * by_token + 2) as n:
                    delta_tile_on_scalar(act, n)
                    for b in range(4):
                        wait_bank(act, b, n + SLAB_Q1, n * UPS + (U_Q1 + UPS - 1))
                        target = PA[:, n + -2, b] if by_token else PB[:, n * 4 + (12 + b)]
                        nc.scalar.activation(target, acc[b][:], ACT.Copy).then_inc(acc_out[b], 1)
                    act.wait_ge(on["o_out"], n + 2)
                    nc.scalar.activation(G["AT"][:], GO[:, n], ACT.Square).then_inc(on["o_square"], 1)
            for b in range(4):
                act.wait_ge(acc_out[b], SLAB_O1)
            nc.scalar.activation(Z1, Z1, ACT.Silu).then_inc(on["z_silu"], 1)
            act.wait_ge(on["o_out"], NT + 1)
            act.dma_start(post_w[:], norm_post).then_inc(post_in, 16)
            attention_on_scalar(act, MOBA, moba_banks, lambda i: None)
            flip_hi_part(act, ht_hi, KD, FLIP_MIXED, lambda k: param("gdn_norm") if k >= 4 else 1.0)
            for n in range(O1_SLABS):
                for b in range(4):
                    wait_bank(act, b, n + SLAB_O1, n * UPS + (U_O1 + UPS - 1))
                    nc.scalar.activation(xn[:, b, n * NC:(n + 1) * NC], acc[b][:], ACT.Square,
                                         accum_out=half_ss[:, 4 * n + b:4 * n + b + 1])\
                        .then_inc(on["mixed_squares"], 1)
            act_second(act)

        @block.vector
        def _(eng):
            step = Steps(eng, dve)
            for count in (values_used, on["g_reduced"], on["o_out"], on["rot_used"], on["h_summed"],
                          on["mt_lo_s"], on["fflo_s"]):
                eng.sem_inc(count, 1)
            V = nc.vector

            def row_norm(squares, n, width):
                step(V.tensor_scalar(ss, ss, 1.0 / width, EPS, ALU.mult, ALU.add))
                rsqrt(step, ss, rstd, tmp4)

            eng.wait_ge(on["x_squares"], NT)
            row_norm(ss, NT, D)
            for t in range(NT):
                V.tensor_scalar(xn[:, t], X[:, t], rstd[:, t:t + 1], None, ALU.mult).then_inc(on["normalized"], 1)
            eng.wait_ge(consts_in, 32)
            flip_lo_part(eng, ht_hi, ht_lo, KD, FLIP1, lambda k: param("norm_pre", k))
            eng.wait_ge(small_in, 16)
            step(V.memset(wba_hi[:].bitcast(F32), 0.0))
            step(V.memset(wba_lo[:].bitcast(F32), 0.0))
            V.tensor_copy(wba_hi[:, :, 0:8], wba[:]).then_inc(on["ba_split"], 1)
            eng.wait_ge(on["ba_split"], 1)
            V.tensor_tensor(wba_lo[:, :, 0:8], wba[:], wba_hi[:, :, 0:8].bitcast(F32),
                            ALU.subtract).then_inc(on["ba_split"], 1)
            for i in step.loop(3, 12):
                eng.wait_ge(on["conv_silu"], i * 4 + 1)
                for b in range(4):
                    eng.wait_ge(acc_out[b], i + (SLAB_D1 + 1))
                    src = PB[:, i * 4 + b]
                    taps = PAR[:, bass.ds(i * 16 + (PARAM_COLS["conv"][0] + 4 * b), 4)]
                    step(V.tensor_scalar(conv4[:, b], src, taps[:, 3:4], None, ALU.mult))
                    for back in (1, 2):
                        step(V.scalar_tensor_tensor(out=conv4[:, b, back:], in0=src[:, :T - back],
                                                    scalar=taps[:, 3 - back:4 - back], in1=conv4[:, b, back:],
                                                    op0=ALU.mult, op1=ALU.add))
                    V.scalar_tensor_tensor(out=conv4[:, b, 3:], in0=src[:, :T - 3], scalar=taps[:, 0:1],
                                           in1=conv4[:, b, 3:], op0=ALU.mult,
                                           op1=ALU.add).then_inc(on["conv_done"], 1)
            eng.wait_ge(on["ba_flipped"], 1)
            bv = ba.rearrange("p (t c) -> p t c", c=8)
            step(V.tensor_copy(ba, aux[3][:, 0:32]))
            step(V.tensor_tensor(bv[:, :, 4:8], bv[:, :, 4:8],
                                 param("dt_bias", 0, HG).unsqueeze(1).to_broadcast([P, NT, HG]), ALU.add))
            V.scalar_tensor_tensor(out=heads(t32[:, 0:16]), in0=bv[:, :, 4:8], scalar=-1.0, in1=bv[:, :, 4:8],
                                   op0=ALU.mult, op1=ALU.max).then_inc(on["ba_in"], 1)
            eng.wait_ge(on["sp_log"], 1)
            eng.wait_ge(on["ba_tanh"], 2)
            step(V.tensor_scalar(beta, beta, 0.5, 0.5, ALU.mult, ALU.add))
            step(V.scalar_tensor_tensor(out=heads(gcol), in0=bv[:, :, 4:8], scalar=0.0,
                                        in1=heads(t32[:, 16:32]), op0=ALU.max, op1=ALU.add))
            V.scalar_tensor_tensor(out=heads(gcol), in0=heads(gcol), scalar=-1.0,
                                   in1=nega.unsqueeze(1).to_broadcast([P, NT, HG]), op0=ALU.mult,
                                   op1=ALU.mult).then_inc(on["gate_sums"], 1)
            def prepare_tile(n):
                four = bass.ts(n, HG)
                step(V.tensor_tensor(G["TG"][:], each_head(const("tri")), spread(gcol[:, four], P), ALU.mult))
                step(V.tensor_copy(G["KT"][:], tile_of(PB, 4, n)))
                V.tensor_tensor(G["IB"][:], each_head(ident), spread(c_bk[:, four], P),
                                ALU.mult).then_inc(on["tg_ready"], 1)

            sums = ssq.rearrange("p (s t h) -> p s t h", s=2, h=HG)
            for n in range(8):
                eng.wait_ge(on["g_copy"] if n < 4 else on["g_square"], n + 1 if n < 4 else n - 3)
                V.tensor_reduce(sums[:, n // 4, :, n % 4], sq[:], AX, ALU.add).then_inc(on["g_reduced"], 1)
            eng.wait_ge(on["g_reduced"], 9)
            step(V.tensor_scalar(ssq, ssq, EPS, None, ALU.add))
            rsqrt(step, ssq, rkq, t32)
            rq, rk = rkq[:, 0:16], rkq[:, 16:32]
            step(V.tensor_tensor(c_bk, beta, rk, ALU.mult))
            gc_col = t32[:, 0:16]
            eng.wait_ge(on["g_copy"], 12)
            prepare_tile(0)
            step(V.tensor_scalar(c_rq, rq, DG ** -0.5, None, ALU.mult))
            eng.wait_ge(on["gate_exps"], 2)
            step(V.tensor_tensor(c_kbg, c_bk, eg, ALU.mult))
            step(V.tensor_copy(t32, aux[2][:, 0:32]))
            V.tensor_tensor(dl, t32[:, 16:32], t32[:, 0:16], ALU.subtract).then_inc(on["gate_done"], 1)
            eng.wait_ge(on["gate_exps"], 3)
            step(V.tensor_tensor(c_kdec, rk, dl, ALU.mult))
            step(V.memset(G["S"][:], 0.0))

            def delta_tile_on_vector(n, beside, after_solved, last):
                four = bass.ts(n, HG)
                eng.wait_ge(on["qk_ready"], n + 1)
                eng.wait_ge(on["e_ready"], n + 1)
                row_decay = aux[0][:].rearrange("p (h t) -> p h t", h=HG)
                step(V.tensor_tensor(G["DEC"][:], row_decay, spread(gc_col[:, four], P), ALU.subtract))
                V.tensor_tensor(G["DEC"][:], G["DEC"][:], each_head(const("future")),
                                ALU.add).then_inc(on["dec_in"], 1)
                step(V.tensor_tensor(G["QD"][:], tile_of(PB, 0, n), G["EG"][:], ALU.mult))
                eng.wait_ge(on["dec_ready"], n + 1)
                step(V.tensor_tensor(G["DEC"][:], G["DEC"][:], spread(rk[:, four], P), ALU.mult))
                step(V.tensor_tensor(G["AT"][:], as_heads(aux[2]), G["DEC"][:], ALU.mult))
                step(V.tensor_tensor(G["AT"][:], as_heads(aux[1]), G["AT"][:], ALU.mult))
                step(V.tensor_tensor(G["MA0"][:], G["AT"][:], each_head(const("level1")), ALU.mult))
                V.tensor_tensor(G["U"][:], each_head(ident), G["MA0"][:], ALU.subtract).then_inc(on["u0"], 1)

                def mask_level(m):
                    V.tensor_tensor(G[f"MA{(m + 1) % 2}"][:], G["AT"][:], each_head(const(f"level{LEVELS[m + 1]}")),
                                    ALU.mult).then_inc(on["masked"], 1)

                step(V.tensor_tensor(G["INT"][:], as_heads(aux[3]), G["DEC"][:], ALU.mult))
                mask_level(0)
                eng.wait_ge(on["u0"], n + 1)
                mask_level(1)
                eng.wait_ge(on["t0_out"], n + 1)
                for m in range(5):
                    eng.wait_ge(on["tx_ready"], n * 11 + 2 * m + 1)
                    V.tensor_tensor(G["TI"][:], G["TI"][:], as_heads(aux[2]), ALU.subtract).then_inc(on["merged"], 1)
                    eng.wait_ge(on["tx_ready"], n * 11 + 2 * m + 2)
                    V.tensor_tensor(G["U"][:], G["U"][:], as_heads(aux[3]), ALU.subtract).then_inc(on["merged"], 1)
                    if m < 4:
                        mask_level(m + 2)
                    if m == 0:
                        step(V.tensor_tensor(G["KBG"][:], KM[:, :, n], spread(c_kbg[:, four], DG), ALU.mult))
                    if m == 1:
                        step(V.tensor_tensor(G["KDEC"][:], KM[:, :, n], spread(c_kdec[:, four], DG), ALU.mult))
                    if m == 2:
                        step(V.tensor_tensor(G["VB"][:], VM[:, :, n], spread(beta[:, four], DG), ALU.mult))
                    beside(m)
                eng.wait_ge(on["tx_ready"], n * 11 + 11)
                V.tensor_tensor(G["U"][:], G["U"][:], as_heads(aux[3]), ALU.subtract).then_inc(on["solved"], 1)
                after_solved(n)
                eng.wait_ge(on["o_ready"], n + 1)
                if not last:
                    step(V.tensor_tensor(G["S"][:], G["S"][:], spread(egl[:, four], DG), ALU.mult))
                    step(V.tensor_tensor(G["S"][:], G["S"][:], as_heads(aux[3]), ALU.add))
                V.tensor_tensor(GO[:, n], as_heads(aux[2]), spread(c_rq[:, four], DG),
                                ALU.mult).then_inc(on["o_out"], 1)
                eng.wait_ge(on["o_square"], n + 1)
                step(V.tensor_reduce(go_ss[:, four], G["AT"][:], AX, ALU.add))

            def pad_keys(m):
                if m < 4:
                    step(V.memset(kz[:, m], 0.0))
                    for h in range(2):
                        step(V.tensor_copy(kz[h * DH:(h + 1) * DH, m, h], PB[h * DH:(h + 1) * DH, 16 + m]))

            for n in step.loop(NT - 1, 15):
                delta_tile_on_vector(n, lambda m: None, lambda n: prepare_tile(n + 1), False)
            for b in range(4):
                eng.wait_ge(acc_out[b], SLAB_Q1 + 2)

            def make_alibi(n):
                step(V.tensor_copy(alibi[0][:], const("alibi")))
                V.tensor_scalar(alibi[1][:], const("alibi"), 0.5, None, ALU.mult).then_inc(on["k_padded"], 1)

            delta_tile_on_vector(NT - 1, pad_keys, make_alibi, True)
            step(V.tensor_scalar(go_ss, go_ss, 1.0 / DG, EPS, ALU.mult, ALU.add))
            rsqrt(step, go_ss, go_rs, t32[:, 0:16])
            eng.wait_ge(on["k_padded"], 1)
            eng.wait_ge(on["z_silu"], 1)

            def beside(i, pair, n):
                t = i * 2 + pair
                if n == 1:
                    step(V.tensor_tensor(GO[:, t], GO[:, t], spread(go_rs[:, bass.ts(t, HG)], DG), ALU.mult))
                if n == 5:
                    V.tensor_tensor(DZ[:, t], DZ[:, t], GO[:, t].rearrange("p h d -> p (h d)"),
                                    ALU.mult).then_inc(on["go_done"], 1)
                if n % NT == NT - 1:
                    bias = alibi[n // NT]
                    eng.wait_ge(biased, i * BODY + (MOBA + 8 * pair + n + 1))
                    step(V.tensor_scalar(bias[:], bias[:], 0.25, None, ALU.mult))

            attention_on_vector(eng, MOBA, moba_banks, step, lambda i, pair: PB[:, i * 2 + (12 + pair)],
                                lambda h: alibi[h], None,
                                lambda i, pair, h, t: Z1[:, t, bass.ds(i * 2 * P + (pair * P + h * DH), DH)],
                                beside, 3)
            flip_lo_part(eng, ht_hi, ht_lo, KD, FLIP_MIXED, lambda k: param("gdn_norm") if k >= 4 else 1.0)
            eng.wait_ge(post_in, 16)
            for n in range(O1_SLABS):
                cols = slice(n * NC, (n + 1) * NC)
                for b in range(4):
                    eng.wait_ge(on["mixed_squares"], 4 * n + b + 1)
                    V.tensor_tensor(mixed[:, b, cols], acc[b][:], post_w[:, cols], ALU.mult)\
                        .then_inc(acc_out[b], 1)
            step(V.tensor_tensor(ss, half_ss[:, 0:4], half_ss[:, 4:8], ALU.add))
            row_norm(ss, NT, D)
            for t in range(NT):
                eng.wait_ge(acc_out[t], SLAB_B2)
                V.scalar_tensor_tensor(out=X[:, t], in0=mixed[:, t], scalar=rstd[:, t:t + 1], in1=X[:, t],
                                       op0=ALU.mult, op1=ALU.add).then_inc(on["post_done"], 1)
            dve_second(eng, step)


def kernel(**inputs):
    import concourse.bacc as bacc
    from concourse.bass_utils import run_bass_kernel_spmd

    a = {k: np.asarray(v) for k, v in inputs.items()}
    w, w2 = a["w_in"][0], a["w_in_2"][0]
    q2 = w2[:, 2048:2560].reshape(D, 2, 4, DH).transpose(0, 2, 1, 3).reshape(D, NC)
    kv = w2[:, 2560:3328]
    gate = w2[:, 3352:5400]
    at = lambda m, *starts: [m[:, c:c + NC] for c in starts]
    slabs = at(w, 2048, 2560, 3072, 3584, 0, 512, 1024, 1536)
    slabs += at(a["w_out"][0], 0, NC)
    slabs += at(w2, 0, 512, 1024)
    slabs += [q2, np.concatenate([kv[:, 0:128], kv[:, 256:384], kv[:, 512:640], kv[:, 128:256]], axis=1),
              w2[:, 1536:2048],
              np.concatenate([kv[:, 384:512], kv[:, 640:768], w2[:, 3328:3352]], axis=1)]
    slabs += at(gate, 0, NC, D, D + NC)
    slabs += at(a["w_br_a_2"][0], 0, NC) + at(a["w_br_b_2"][0], 0, NC)
    slabs += [a["w_out_2"][0][:, n:n + NC] for n in (0, NC)]
    for f in range(FF_HALVES):
        half = slice(f * FF // 2, (f + 1) * FF // 2)
        slabs += [a["w_ff1_2"][0][:, half][:, i * NC:(i + 1) * NC] for i in range(FF1_SLABS)]
        slabs += [a["w_ff2_2"][0][half, n:n + NC] for n in (0, NC)]
    params = np.zeros((P, N_PARAM), np.float32)

    def put(name, value):
        p, q = PARAM_COLS[name]
        params[:, p:q] = value

    put("norm_pre", by_partition(a["norm_pre_w"][0]))
    put("norm1", by_partition(a["norm1_g_2"][0]))
    put("norm2", by_partition(a["norm2_g_2"][0]))
    put("conv", a["conv_w"][0].reshape(4, 12, P).transpose(2, 1, 0).reshape(P, 48))
    put("gdn_norm", a["gdn_norm_w"][0][:, None])
    put("hgrn_norm", a["hgrn_norm_g_2"][0][:, None])
    put("lb", np.concatenate([by_partition(a["lb_param_2"][0]), by_partition(a["lb_param_2"][1])], axis=1))
    put("a_log", a["a_log"][0][None, :])
    put("dt_bias", a["dt_bias"][0][None, :])
    pe = np.stack([a["cmp_pe_k_2"][0], a["cmp_pe_v_2"][0]]).reshape(2, 16, P).transpose(2, 0, 1)
    w1 = np.stack([a["cmp_w1_k_2"][0], a["cmp_w1_v_2"][0]]).reshape(2, 2, 8, P, 256).transpose(0, 1, 3, 2, 4)
    w2c = np.stack([a["cmp_w2_k_2"][0], a["cmp_w2_v_2"][0]]).reshape(2, 2, P, DH).transpose(2, 0, 1, 3)
    arrays = {
        "units": np.concatenate([slab_units(s) for s in slabs]),
        "consts": constant_table(),
        "params": params,
        "x": a["x"][0],
        "w_ba": w[:, 4096:4104].reshape(KD, P, 8).transpose(1, 0, 2).reshape(P, 8 * KD),
        "norm_post": np.broadcast_to(a["norm_post_w"][0], (P, D)),
        "final_g": np.broadcast_to(a["final_g_2"], (P, D)),
        "positions": np.broadcast_to(a["positions_2"][0], (P, T)),
        "pe_kv": pe.reshape(P, 32),
        "w1_kv": w1.reshape(2, 2, P, 8 * 256),
        "w2_kv": np.concatenate([w2c, w2c], axis=3).reshape(P, 4 * P),
    }
    arrays = {k: np.ascontiguousarray(v) for k, v in arrays.items()}
    nc = bacc.Bacc("TRN2", target_bir_lowering=False, num_devices=1)
    aps = {k: nc.dram_tensor(k, v.shape, mybir.dt.from_np(v.dtype), kind="ExternalInput").ap()
           for k, v in arrays.items()}
    result = nc.dram_tensor("result", (T, D), F32, kind="ExternalOutput").ap()
    two_blocks(nc, out=result, **aps)
    r = run_bass_kernel_spmd(nc, [arrays], core_ids=[0])
    return r.results[0]["result"].reshape(1, T, D)
```
